# Optimizing a Trainium2 kernel written in Bass

```python
import jax, jax.numpy as jnp
from jax import lax
import numpy as np

D_MODEL = 1024
BATCH = 1
SEQ = 512
DEPTH = 2
DEC_BATCH = 8
DEC_SEQ = 1
PAST_LEN = 256
PAGE_SIZE = 128

D_PLE = 256
N_AB_LAYERS = (DEPTH + 1) // 2
N_C_LAYERS = DEPTH // 2
H_A = 8
HD_A = 64
D_A = H_A * HD_A
D_B = D_MODEL - D_A
CONV_B = 3
D_RNN = D_MODEL
N_BLK_C = 8
BS_C = D_RNN // N_BLK_C
CONV_C = 4
LRU_C = 8.0
D_FF = 2816
Q_BLOCK = 128
N_NORMS = 7
EPS = 1e-6
NEG = -1e30
D_IN_AB = 3 * D_A + H_A + 3 * D_B
AB_SPLITS = (D_A, 2 * D_A, 3 * D_A, 3 * D_A + H_A, 3 * D_A + H_A + D_B, 3 * D_A + H_A + 2 * D_B)

kernel_name = 'fox_conv_rglru_hybrid_step'

def rmsnorm(x, g):
    xf = x.astype(jnp.float32)
    y = xf * lax.rsqrt(jnp.mean(xf * xf, axis=-1, keepdims=True) + EPS)
    return (y * g.astype(jnp.float32)).astype(x.dtype)

def swiglu(x, wi, wo):
    g, u = jnp.split(x @ wi, 2, axis=-1)
    return (jax.nn.silu(g) * u) @ wo

def ffn_half(x, g_pre, g_post, wi, wo):
    return x + 0.5 * rmsnorm(swiglu(rmsnorm(x, g_pre), wi, wo), g_post)

def ple_add(x, p, g, w_pe, w_pg):
    gate = jax.nn.sigmoid(rmsnorm(x, g) @ w_pg)
    return x + (p @ w_pe) * gate

def causal_dwconv(u, buf, w):
    width = w.shape[0]
    t = u.shape[1]
    full = jnp.concatenate([buf.astype(u.dtype), u], axis=1)
    y = full[:, 0:t] * w[0]
    for j in range(1, width):
        y = y + full[:, j:j + t] * w[j]
    return y, full[:, -(width - 1):]

def fox_prompt(q, k, v, logf):
    bsz, s_len, nh, hd = q.shape
    nb = s_len // Q_BLOCK
    ch = jnp.cumsum(logf, axis=1).transpose(0, 2, 1)
    qb = q.reshape(bsz, nb, Q_BLOCK, nh, hd).transpose(1, 0, 2, 3, 4)
    cqb = ch.reshape(bsz, nh, nb, Q_BLOCK).transpose(2, 0, 1, 3)
    kpos = jnp.arange(s_len)
    scale = hd ** -0.5

    def block(args):
        i, qi, ci = args
        s = jnp.einsum('bqhd,bkhd->bhqk', qi, k).astype(jnp.float32) * scale
        s = s + ci[..., :, None] - ch[:, :, None, :]
        qpos = i * Q_BLOCK + jnp.arange(Q_BLOCK)
        s = jnp.where(kpos[None, :] <= qpos[:, None], s, NEG)
        p = jax.nn.softmax(s, axis=-1).astype(v.dtype)
        return jnp.einsum('bhqk,bkhd->bqhd', p, v)

    o = lax.map(block, (jnp.arange(nb), qb, cqb))
    return o.transpose(1, 0, 2, 3, 4).reshape(bsz, s_len, nh * hd)

def fox_decode(q, k_new, v_new, logf_new, k_past, v_past, logf_past):
    bsz, t, nh, hd = q.shape
    p_len = k_past.shape[1]
    k = jnp.concatenate([k_past.astype(k_new.dtype), k_new], axis=1)
    v = jnp.concatenate([v_past.astype(v_new.dtype), v_new], axis=1)
    logf = jnp.concatenate([logf_past.astype(jnp.float32), logf_new.astype(jnp.float32)], axis=1)
    ch = jnp.cumsum(logf, axis=1).transpose(0, 2, 1)
    s = jnp.einsum('bqhd,bkhd->bhqk', q, k).astype(jnp.float32) * (hd ** -0.5)
    s = s + ch[:, :, p_len:, None] - ch[:, :, None, :]
    kpos = jnp.arange(p_len + t)
    qpos = p_len + jnp.arange(t)
    s = jnp.where(kpos[None, :] <= qpos[:, None], s, NEG)
    p = jax.nn.softmax(s, axis=-1).astype(v.dtype)
    return jnp.einsum('bhqk,bkhd->bqhd', p, v).reshape(bsz, t, nh * hd)

def ab_mixer(h, conv_buf, past, w_in, b_f, conv_w, w_out):
    bsz, t, _ = h.shape
    q, k, v, f_lin, b_gate, c_gate, x_in = jnp.split(h @ w_in, AB_SPLITS, axis=-1)
    q = q.reshape(bsz, t, H_A, HD_A)
    k = k.reshape(bsz, t, H_A, HD_A)
    v = v.reshape(bsz, t, H_A, HD_A)
    logf = jax.nn.log_sigmoid(f_lin.astype(jnp.float32) + b_f.astype(jnp.float32))
    if past is None:
        y_a = fox_prompt(q, k, v, logf)
    else:
        y_a = fox_decode(q, k, v, logf, past[0], past[1], past[2])
    conv, new_buf = causal_dwconv(c_gate * x_in, conv_buf, conv_w)
    y_b = b_gate * conv
    y = jnp.concatenate([y_a, y_b.astype(y_a.dtype)], axis=-1) @ w_out
    return y, k, v, logf.astype(h.dtype), new_buf

def rglru(xc, h0, w_rg, b_rg, w_ig, b_ig, lam):
    bsz, t, _ = xc.shape
    xb = xc.reshape(bsz, t, N_BLK_C, BS_C)
    r = jax.nn.sigmoid(jnp.einsum('btnc,ncd->btnd', xb, w_rg).reshape(bsz, t, D_RNN) + b_rg)
    i = jax.nn.sigmoid(jnp.einsum('btnc,ncd->btnd', xb, w_ig).reshape(bsz, t, D_RNN) + b_ig)
    log_a = -LRU_C * r.astype(jnp.float32) * jax.nn.softplus(-lam.astype(jnp.float32))
    a = jnp.exp(log_a)
    u = jnp.sqrt(-jnp.expm1(2.0 * log_a)) * (i * xc).astype(jnp.float32)

    def step(hc, au):
        hc = au[0] * hc + au[1]
        return hc, hc

    h_last, hs = lax.scan(step, h0.astype(jnp.float32), (a.transpose(1, 0, 2), u.transpose(1, 0, 2)))
    return hs.transpose(1, 0, 2).astype(xc.dtype), h_last.astype(xc.dtype)

def c_mixer(h, conv_buf, h0, w_in, conv_w, conv_b, w_rg, b_rg, w_ig, b_ig, lam, w_out):
    gate, xr = jnp.split(h @ w_in, 2, axis=-1)
    xc, new_buf = causal_dwconv(xr, conv_buf, conv_w)
    xc = xc + conv_b
    hs, h_last = rglru(xc, h0, w_rg, b_rg, w_ig, b_ig, lam)
    y = (jax.nn.gelu(gate) * hs) @ w_out
    return y, new_buf, h_last

def setup_inputs(seed: int = 0) -> dict:
    key = jax.random.key(seed)
    ks = jax.random.split(key, 40)
    f32 = jnp.float32
    n_pages = PAST_LEN // PAGE_SIZE
    n_used = DEC_BATCH * n_pages
    n_phys = n_used + max(1, n_used // 4)
    nrm = lambda k, shape, s: jax.random.normal(k, shape, f32) * s
    page_table = jax.random.permutation(ks[0], n_phys)[:n_used].reshape(DEC_BATCH, n_pages).astype(jnp.int32)
    a0 = jax.random.uniform(ks[1], (N_C_LAYERS, D_RNN), f32, 0.9, 0.999)
    s0 = a0 ** (1.0 / LRU_C)
    lam = jnp.log(s0) - jnp.log1p(-s0)
    return {
        'x_prompt': nrm(ks[2], (BATCH, SEQ, D_MODEL), 1.0),
        'x_sample': nrm(ks[3], (DEC_BATCH, DEC_SEQ, D_MODEL), 1.0),
        'p_prompt': nrm(ks[4], (DEPTH, BATCH, SEQ, D_PLE), 1.0),
        'p_sample': nrm(ks[5], (DEPTH, DEC_BATCH, DEC_SEQ, D_PLE), 1.0),
        'cache_k': nrm(ks[6], (n_phys, N_AB_LAYERS, PAGE_SIZE, H_A, HD_A), 1.0),
        'cache_v': nrm(ks[7], (n_phys, N_AB_LAYERS, PAGE_SIZE, H_A, HD_A), 1.0),
        'cache_logf': jax.nn.log_sigmoid(1.0 + nrm(ks[8], (n_phys, N_AB_LAYERS, PAGE_SIZE, H_A), 1.0)),
        'state_conv_b': nrm(ks[9], (DEC_BATCH, N_AB_LAYERS, CONV_B - 1, D_B), 1.0),
        'state_conv_c': nrm(ks[10], (DEC_BATCH, N_C_LAYERS, CONV_C - 1, D_RNN), 1.0),
        'state_h_c': nrm(ks[11], (DEC_BATCH, N_C_LAYERS, D_RNN), 0.5),
        'page_table': page_table,
        'norms': 1.0 + nrm(ks[12], (DEPTH, N_NORMS, D_MODEL), 0.05),
        'ffn1_wi': nrm(ks[13], (DEPTH, D_MODEL, 2 * D_FF), D_MODEL ** -0.5),
        'ffn1_wo': nrm(ks[14], (DEPTH, D_FF, D_MODEL), D_FF ** -0.5),
        'ffn2_wi': nrm(ks[15], (DEPTH, D_MODEL, 2 * D_FF), D_MODEL ** -0.5),
        'ffn2_wo': nrm(ks[16], (DEPTH, D_FF, D_MODEL), D_FF ** -0.5),
        'ple_w_pe': nrm(ks[17], (DEPTH, D_PLE, D_MODEL), D_PLE ** -0.5),
        'ple_w_pg': nrm(ks[18], (DEPTH, D_MODEL, D_MODEL), D_MODEL ** -0.5),
        'ab_w_in': nrm(ks[19], (N_AB_LAYERS, D_MODEL, D_IN_AB), D_MODEL ** -0.5),
        'ab_b_f': 1.0 + nrm(ks[20], (N_AB_LAYERS, H_A), 0.1),
        'ab_conv_w': nrm(ks[21], (N_AB_LAYERS, CONV_B, D_B), CONV_B ** -0.5),
        'ab_w_out': nrm(ks[22], (N_AB_LAYERS, D_A + D_B, D_MODEL), (D_A + D_B) ** -0.5),
        'c_w_in': nrm(ks[23], (N_C_LAYERS, D_MODEL, 2 * D_RNN), D_MODEL ** -0.5),
        'c_conv_w': nrm(ks[24], (N_C_LAYERS, CONV_C, D_RNN), CONV_C ** -0.5),
        'c_conv_b': nrm(ks[25], (N_C_LAYERS, D_RNN), 0.01),
        'c_w_rg': nrm(ks[26], (N_C_LAYERS, N_BLK_C, BS_C, BS_C), BS_C ** -0.5),
        'c_b_rg': nrm(ks[27], (N_C_LAYERS, D_RNN), 0.01),
        'c_w_ig': nrm(ks[28], (N_C_LAYERS, N_BLK_C, BS_C, BS_C), BS_C ** -0.5),
        'c_b_ig': nrm(ks[29], (N_C_LAYERS, D_RNN), 0.01),
        'c_lam': lam,
        'c_w_out': nrm(ks[30], (N_C_LAYERS, D_RNN, D_MODEL), D_RNN ** -0.5),
    }

def reference(x_prompt, x_sample, p_prompt, p_sample, cache_k, cache_v, cache_logf, state_conv_b,
              state_conv_c, state_h_c, page_table, norms, ffn1_wi, ffn1_wo, ffn2_wi, ffn2_wo,
              ple_w_pe, ple_w_pg, ab_w_in, ab_b_f, ab_conv_w, ab_w_out, c_w_in, c_conv_w, c_conv_b,
              c_w_rg, c_b_rg, c_w_ig, c_b_ig, c_lam, c_w_out):
    xp, xs = x_prompt, x_sample
    bp = xp.shape[0]
    bs = xs.shape[0]
    kp_l, vp_l, fp_l, ks_l, vs_l, fs_l = [], [], [], [], [], []
    cbp_l, cbs_l, ccp_l, ccs_l, hp_l, hs_l = [], [], [], [], [], []
    for i in range(DEPTH):
        g = norms[i]
        xp = ffn_half(xp, g[0], g[1], ffn1_wi[i], ffn1_wo[i])
        xs = ffn_half(xs, g[0], g[1], ffn1_wi[i], ffn1_wo[i])
        hp = rmsnorm(xp, g[2])
        hs = rmsnorm(xs, g[2])
        l = i // 2
        if i % 2 == 0:
            buf0 = jnp.zeros((bp, CONV_B - 1, D_B), hp.dtype)
            yp, kp, vp, fp, cbp = ab_mixer(hp, buf0, None, ab_w_in[l], ab_b_f[l], ab_conv_w[l], ab_w_out[l])
            k_past = cache_k[page_table, l].reshape(bs, -1, H_A, HD_A)
            v_past = cache_v[page_table, l].reshape(bs, -1, H_A, HD_A)
            f_past = cache_logf[page_table, l].reshape(bs, -1, H_A)
            ys, ks_, vs_, fs_, cbs = ab_mixer(hs, state_conv_b[:, l], (k_past, v_past, f_past),
                                              ab_w_in[l], ab_b_f[l], ab_conv_w[l], ab_w_out[l])
            kp_l.append(kp); vp_l.append(vp); fp_l.append(fp)
            ks_l.append(ks_); vs_l.append(vs_); fs_l.append(fs_)
            cbp_l.append(cbp); cbs_l.append(cbs)
        else:
            buf0 = jnp.zeros((bp, CONV_C - 1, D_RNN), hp.dtype)
            h0 = jnp.zeros((bp, D_RNN), hp.dtype)
            yp, ccp, hlp = c_mixer(hp, buf0, h0, c_w_in[l], c_conv_w[l], c_conv_b[l], c_w_rg[l], c_b_rg[l],
                                   c_w_ig[l], c_b_ig[l], c_lam[l], c_w_out[l])
            ys, ccs, hls = c_mixer(hs, state_conv_c[:, l], state_h_c[:, l], c_w_in[l], c_conv_w[l], c_conv_b[l],
                                   c_w_rg[l], c_b_rg[l], c_w_ig[l], c_b_ig[l], c_lam[l], c_w_out[l])
            ccp_l.append(ccp); ccs_l.append(ccs); hp_l.append(hlp); hs_l.append(hls)
        xp = xp + rmsnorm(yp, g[3])
        xs = xs + rmsnorm(ys, g[3])
        xp = ffn_half(xp, g[4], g[5], ffn2_wi[i], ffn2_wo[i])
        xs = ffn_half(xs, g[4], g[5], ffn2_wi[i], ffn2_wo[i])
        xp = ple_add(xp, p_prompt[i], g[6], ple_w_pe[i], ple_w_pg[i])
        xs = ple_add(xs, p_sample[i], g[6], ple_w_pe[i], ple_w_pg[i])
    st = lambda lst: jnp.stack(lst, axis=1)
    return (xp, xs, st(kp_l), st(vp_l), st(fp_l), st(ks_l), st(vs_l), st(fs_l),
            st(cbp_l), st(cbs_l), st(ccp_l), st(ccs_l), st(hp_l), st(hs_l))


_drawn_inputs = setup_inputs


def setup_inputs(seed=0):
    import zlib

    import numpy as np

    out = dict(_drawn_inputs(seed))
    spreads = {}
    factors = {'c_b_rg': 25.981, 'c_b_ig': 8.0}
    for name, (base, spread) in spreads.items():
        noise = np.random.default_rng([zlib.crc32(name.encode()), seed]).standard_normal(out[name].shape)
        drawn = base * np.exp(spread * noise) if base else spread * noise
        out[name] = __import__('jax').numpy.asarray(drawn.astype(out[name].dtype))
    for name, factor in factors.items():
        out[name] = (out[name] * factor).astype(out[name].dtype)
    return out
```

```python
import math
from contextlib import ExitStack

import numpy as np
import concourse.bass as bass
from concourse import mybir

F32 = mybir.dt.float32
F32R = mybir.dt.float32r
I32 = mybir.dt.int32
ALU = mybir.AluOpType
ACT = mybir.ActivationFunctionType
AXX = mybir.AxisListType.X

P = 128
D = 1024
KC = D // P
SEQ, DEC = 512, 8
TOK = SEQ + DEC
HALF = TOK // 2
DEPTH = 2
D_FF = 2816
FT = D_FF // P
HID = (12, FT - 12)
HEADS, HD = 8, 64
AC = HEADS * HD // P
D_A = HEADS * HD
CB, CC = 3, 4
LRU_C = 8.0
PLE_K = 256 // P
PAGES, PAGE = 2, 128
PAST = PAGES * PAGE
BH = DEC * HEADS
NN = 7
EPS = 1e-6
NEG = -1e30
QB = SEQ // P
ACCS = 4
UNIT = 2048
RING = 4

PARAMS = {}
_at = 0
for _name, _n in (("norm", DEPTH * NN * KC), ("bf", 1), ("convb_w", CB * AC), ("convc_w", CC * KC),
                  ("convc_b", KC), ("b_rg", KC), ("b_ig", KC), ("lam", KC),
                  ("state_b", AC * (CB - 1) * DEC), ("state_c", KC * (CC - 1) * DEC), ("h0", KC * DEC)):
    PARAMS[_name] = (_at, _n)
    _at += _n
N_PARAMS = _at
IDENT, MASK, SAME_B, TO_BH, TO_ROWS = 0, P, 2 * P, 2 * P + DEC, 2 * P + DEC + BH
N_CONST = TO_ROWS + AC * P


class Plan:

    def __init__(self):
        self.job, self.units, self.unit, self.last_of, self.size = {}, [], {}, {}, 0

    def add_job(self, name, unit=None):
        self.job[name] = len(self.job)
        if unit is not None:
            self.last_of[unit] = name

    def add_unit(self, name, what):
        size = what[3] * sum(b - a for a, b in what[4])
        self.unit[name] = len(self.units)
        self.units.append((name, self.size, size, what))
        self.size += P * size

    def refills(self):
        return {job: self.unit[u] + 2 for u, job in self.last_of.items() if self.unit[u] + 2 < len(self.units)}


def col(i, n=1):
    return (i * P, (i + n) * P)


def make_plan():
    pl = Plan()

    def first_group(s, tiles, units):
        for n in range(3):
            pl.add_job(f"{s}.{tiles[n]}", units[n // 2])
        pl.add_job(f"{s}.pre")
        pl.add_job(f"{s}.{tiles[3]}", units[1])

    def out_tiles(s, what, k, ks, tag=""):
        for m in range(KC):
            pl.add_unit(f"{s}.out{tag}{m}", (*what, k, ks, [col(m)]))
            pl.add_job(f"{s}.out{tag}{m}", f"{s}.out{tag}{m}")

    def out_pairs(s, what):
        for m in range(0, KC, 2):
            pl.add_unit(f"{s}.out{m}", (*what, 0, KC, [col(m, 2)]))
            pl.add_job(f"{s}.out{m}", f"{s}.out{m}")
            pl.add_job(f"{s}.out{m + 1}", f"{s}.out{m}")

    def ffn(s, name, layer):
        if s % 4:
            pl.add_job(f"{s}.post")
        for half, k0 in enumerate((0, HID[0])):
            for j in range(k0, k0 + HID[half]):
                pl.add_unit(f"{s}.in{j}", (name + "_wi", layer, 0, KC, [col(j), col(FT + j)]))
            if half == 0:
                first_group(s, ["g0", "u0", "g1", "u1"], [f"{s}.in0", f"{s}.in1"])
            for j in range(k0 + 2 * (half == 0), k0 + HID[half]):
                pl.add_job(f"{s}.g{j}", f"{s}.in{j}")
                pl.add_job(f"{s}.u{j}", f"{s}.in{j}")
            out_tiles(s, (name + "_wo", layer), k0, HID[half], "ab"[half])

    def ple(s, layer):
        pl.add_job(f"{s}.post")
        gate = lambda m: (f"{s}.gate{m}", ("ple_w_pg", layer, 0, KC, [col(m, 2)]))
        embed = lambda m: (f"{s}.pe{m}", ("ple_w_pe", layer, 0, PLE_K, [col(m, 4)]))
        for m in (0, 4):
            pl.add_unit(*gate(m))
            pl.add_unit(*gate(m + 2))
            pl.add_unit(*embed(m))
            if m == 0:
                first_group(s, ["gate0", "gate1", "gate2", "gate3"], [f"{s}.gate0", f"{s}.gate2"])
            else:
                for n in range(m, m + 4):
                    pl.add_job(f"{s}.gate{n}", f"{s}.gate{n // 2 * 2}")
            for n in range(m, m + 4):
                pl.add_job(f"{s}.pe{n}", f"{s}.pe{m}")

    def ab(s):
        w = ("ab_w_in", 0, 0, KC)
        f0 = 3 * D_A
        gate0, c0, x0 = (f0 + HEADS + n * D_A for n in range(3))
        tile = lambda at, m, n=1: (at + m * P, at + (m + n) * P)
        pl.add_job(f"{s}.post")
        for m in (0, 2):
            pl.add_unit(f"{s}.q{m}", (*w, [tile(0, m, 2)]))
        first_group(s, ["q0", "q1", "q2", "q3"], [f"{s}.q0", f"{s}.q2"])
        for m in (0, 2):
            pl.add_unit(f"{s}.k{m}", (*w, [tile(D_A, m, 2)]))
            pl.add_job(f"{s}.k{m}", f"{s}.k{m}")
            pl.add_job(f"{s}.k{m + 1}", f"{s}.k{m}")
        pl.add_unit(f"{s}.f", (*w, [(f0, f0 + HEADS)]))
        pl.add_job(f"{s}.f", f"{s}.f")
        for m in (0, 2):
            pl.add_unit(f"{s}.v{m}", (*w, [tile(2 * D_A, m, 2)]))
            pl.add_job(f"{s}.v{m}", f"{s}.v{m}")
            pl.add_job(f"{s}.v{m + 1}", f"{s}.v{m}")
        for j in ("vt0", "vt2", "cq", "ck0", "s0.0", "s0.2"):
            pl.add_job(f"{s}.{j}")
        for h in range(HEADS):
            if h < AC:
                pl.add_unit(f"{s}.cx{h}", (*w, [tile(c0, h), tile(x0, h)]))
                pl.add_job(f"{s}.c{h}", f"{s}.cx{h}")
                pl.add_job(f"{s}.x{h}", f"{s}.cx{h}")
            elif h < AC + AC // 2:
                m = 2 * (h - AC)
                pl.add_unit(f"{s}.b{m}", (*w, [tile(gate0, m, 2)]))
                pl.add_job(f"{s}.b{m}", f"{s}.b{m}")
                pl.add_job(f"{s}.b{m + 1}", f"{s}.b{m}")
            for j in {1: ["dec_s"], 2: ["dec_t"], 3: ["dec_p"], 4: ["dec_o"]}.get(h, []):
                pl.add_job(f"{s}.{j}")
            pl.add_job(f"{s}.pt{h}.0")
            pl.add_job(f"{s}.pt{h}.2")
            if h + 1 < HEADS:
                for j in (f"ck{h + 1}", f"s{h + 1}.0", f"s{h + 1}.2"):
                    pl.add_job(f"{s}.{j}")
            pl.add_job(f"{s}.pv{h}")
        out_pairs(s, ("ab_w_out", 0))

    def cm(s):
        pl.add_job(f"{s}.post")
        xr = lambda m: pl.add_unit(f"{s}.xr{m}", ("c_w_in", 0, 0, KC, [(D + m * P, D + (m + 2) * P)]))

        def pair(kind, m):
            pl.add_job(f"{s}.{kind}{m}", f"{s}.{kind}{m}")
            pl.add_job(f"{s}.{kind}{m + 1}", f"{s}.{kind}{m}")

        def gates(m):
            pl.add_unit(f"{s}.ri{m}", ("c_w_ri", 0, 0, 1, [col(2 * m, 4)]))
            for n in (m, m + 1):
                pl.add_job(f"{s}.r{n}", f"{s}.ri{m}")
                pl.add_job(f"{s}.i{n}", f"{s}.ri{m}")

        def gate(m):
            pl.add_unit(f"{s}.gt{m}", ("c_w_in", 0, 0, KC, [col(m, 2)]))
            pair("gt", m)

        xr(0)
        xr(2)
        first_group(s, ["xr0", "xr1", "xr2", "xr3"], [f"{s}.xr0", f"{s}.xr2"])
        gates(0)
        for m in (4, 6):
            xr(m)
            pair("xr", m)
            gates(m - 2)
        gate(0)
        gates(6)
        for m in (2, 4, 6):
            gate(m)
        out_pairs(s, ("c_w_out", 0))

    for layer in range(DEPTH):
        ffn(4 * layer, "ffn1", layer)
        (ab if layer % 2 == 0 else cm)(4 * layer + 1)
        ffn(4 * layer + 2, "ffn2", layer)
        ple(4 * layer + 3, layer)
    return pl


PLAN = make_plan()
SUBS = 4 * DEPTH
POSTS = [s for s in range(SUBS) if s % 4]
IS_FFN = lambda s: s % 2 == 0
S_AB, S_C = 1, 5


def trunk(nc, weights, params_d, const_d, x_d, p_d, kpages_d, vpages_d, lfpages_d, table_d,
          y_o, k_o, v_o, logf_o, cx_o, cbstate_o, xr_o, ccstate_o, h_o):
    J, U = PLAN.job, PLAN.unit
    REFILL = PLAN.refills()
    n_units = len(PLAN.units)
    last_job = [J[PLAN.last_of[name]] for name, *_ in PLAN.units]

    ctx = ExitStack()
    with ctx:
        def sb(name, shape, dt=F32):
            return ctx.enter_context(nc.sbuf_tensor(name, shape, dt))

        def sem(name):
            return ctx.enter_context(nc.semaphore(name))

        def overlay(*groups):
            made, most = [], 0
            for group in groups:
                with ExitStack() as own:
                    made += [own.enter_context(nc.sbuf_tensor(n, s, dt)) for n, s, dt in group]
                    most = max(most, sum(4 * math.prod(s[1:]) for _, s, _ in group))
            sb("under_" + groups[0][0][0], [P, (most + 63) // 4])
            return made

        x = sb("x", [P, KC, TOK])
        act_hi = sb("act_hi", [P, KC, TOK], F32R)
        act_lo = sb("act_lo", [P, KC, TOK], F32R)
        raw = [sb(f"raw{i}", [P, UNIT]) for i in range(2)]
        w_hi = [sb(f"w_hi{i}", [P, UNIT], F32R) for i in range(2)]
        w_lo = [sb(f"w_lo{i}", [P, UNIT], F32R) for i in range(2)]
        params = sb("params", [P, N_PARAMS])
        half_norm = sb("half_norm", [P, DEPTH * NN * KC])
        const = sb("const", [P, N_CONST])
        mean_of = sb("mean_of", [P, P])
        one = sb("one", [P, 1])
        eps = sb("eps", [P, 1])
        rs_pre = sb("rs_pre", [P, TOK])
        rs_post = sb("rs_post", [P, TOK])
        xsum = sb("xsum", [P, TOK])
        ysum = sb("ysum", [P, TOK])
        xsq = [sb(f"xsq{i}", [P, TOK]) for i in range(2)]
        ysq = [sb(f"ysq{i}", [P, TOK]) for i in range(2)]
        t = [sb(f"t{i}", [P, TOK]) for i in range(2)]
        lru = sb("lru", [P, 4 * KC])
        xr_tail = sb("xr_tail", [P, KC, CC - 1 + DEC])
        y, ring, v_tok, xi = overlay(
            [("y", [P, KC, TOK], F32)],
            [("ring", [P, RING, D_A], F32), ("v_tok", [P, QB, D_A], F32)],
            [("xi", [P, KC, TOK], F32)])
        (hid_hi, hid_lo, gs0, gs1, us0, us1,
         p_raw, p_hi, p_lo, sig,
         q, k, v, conv, sc, pt, ckb, logf, ch, cq, nmx, den, rden, cx_tail,
         qbd, kqbd, sT, dlf, dch, ds, dsn, pT, onew, dnmx, dden, dtmp,
         lru_a, lru_v, gt, xc_hi, xc_lo) = overlay(
            [("hid_hi", [P, HID[0], TOK], F32R), ("hid_lo", [P, HID[0], TOK], F32R),
             ("gs0", [P, TOK], F32), ("gs1", [P, TOK], F32), ("us0", [P, TOK], F32), ("us1", [P, TOK], F32)],
            [("p_raw", [P, PLE_K, TOK], F32), ("p_hi", [P, PLE_K, TOK], F32R), ("p_lo", [P, PLE_K, TOK], F32R),
             ("sig", [P, KC, TOK], F32)],
            [("q", [P, AC, TOK], F32), ("k", [P, AC, TOK], F32), ("v", [P, AC, TOK], F32),
             ("conv", [P, AC, TOK], F32), ("sc", [P, QB, SEQ], F32), ("pt", [P, QB, SEQ], F32),
             ("ckb", [P, SEQ], F32), ("logf", [HEADS, TOK], F32), ("ch", [HEADS, SEQ], F32),
             ("cq", [P, QB, HEADS], F32), ("nmx", [P, QB], F32), ("den", [P, QB], F32), ("rden", [P, QB], F32),
             ("cx_tail", [P, AC, CB - 1 + DEC], F32),
             ("qbd", [P, DEC, AC, 2], F32), ("kqbd", [P, DEC, AC, 2], F32), ("sT", [P, PAGES * BH], F32),
             ("dlf", [BH, PAST + 1], F32), ("dch", [BH, PAST + 1], F32), ("ds", [BH, PAST + 1], F32),
             ("dsn", [BH, DEC], F32), ("pT", [P, PAGES * BH], F32), ("onew", [P, AC, DEC], F32),
             ("dnmx", [BH, 1], F32), ("dden", [BH, 1], F32), ("dtmp", [BH, DEC], F32)],
            [("lru_a", [P, KC, TOK], F32), ("lru_v", [P, KC, TOK], F32), ("gt", [P, KC, TOK], F32),
             ("xc_hi", [P, 4, TOK], F32R), ("xc_lo", [P, 4, TOK], F32R)])
        gs, us = [gs0, gs1], [us0, us1]
        table = sb("table", [1, DEC * PAGES], I32)
        ident = const[:, IDENT:IDENT + P]
        mask = const[:, MASK:MASK + P]
        same_b = const[0:BH, SAME_B:SAME_B + DEC]
        to_bh = const[0:HEADS, TO_BH:TO_BH + BH]
        to_rows = const[0:BH, TO_ROWS:TO_ROWS + AC * P]
        acc = [ctx.enter_context(nc.psum_tensor(f"acc{i}", [P, 2, 512], F32)) for i in range(ACCS)]

        def par(name, i=0, n=1, parts=P):
            at = PARAMS[name][0] + i
            return params[0:parts, at:at + n]

        def gain(s, which, c, scaled=False):
            src = half_norm if scaled else params
            at = ((s // 4) * NN + which) * KC + c
            return src[:, at:at + 1]

        def pre_gain(s, c):
            return gain(s, (0, 2, 4, 6)[s % 4], c)

        def post_gain(s, c):
            return gain(s, (None, 1, 3, 5)[s % 4], c, scaled=IS_FFN(s - 1))

        def two(ap):
            return ap.rearrange("p (a n) -> p a n", a=2)

        def acc_of(name):
            return acc[J[name] % ACCS]

        def tile_of(j):
            return acc[j % ACCS][:, :, 0:HALF]

        in_x, in_params, in_const, in_table = sem("in_x"), sem("in_params"), sem("in_const"), sem("in_table")
        raw_loaded = [sem(f"raw_loaded{i}") for i in range(2)]
        p_loaded = sem("p_loaded")
        ring_loaded = [sem(f"ring_loaded{i}") for i in range(RING)]
        lf_loaded = sem("lf_loaded")
        hi_ready, lo_ready = sem("hi_ready"), sem("lo_ready")
        acc_ready = sem("acc_ready")
        drained = [sem(f"drained{i}") for i in range(ACCS)]
        consts_made = sem("consts_made")
        half_made, nl_act, nl_made = sem("half_made"), sem("nl_act"), sem("nl_made")
        rs_ready = sem("rs_ready")
        ysum_zeroed, ysq_ready, ysum_added = sem("ysum_zeroed"), sem("ysq_ready"), sem("ysum_added")
        xsq_ready, xsum_added = sem("xsq_ready"), sem("xsum_added")
        t_ready, x_ready, ple_x = sem("t_ready"), sem("x_ready"), sem("ple_x")
        acth_ready, actl_ready = sem("acth_ready"), sem("actl_ready")
        silu_ready, h_ready = sem("silu_ready"), sem("h_ready")
        hidh_ready, hidl_ready = sem("hidh_ready"), sem("hidl_ready")
        ph_ready, pl_ready, sig_ready, pe_t = sem("ph_ready"), sem("pl_ready"), sem("sig_ready"), sem("pe_t")
        y_stored = sem("y_stored")
        stored = sem("stored")
        f_z, f_exp, f_log, f_ch = sem("f_z"), sem("f_exp"), sem("f_log"), sem("f_ch")
        scores_ready, exp_ready, probs_ready = sem("scores_ready"), sem("exp_ready"), sem("probs_ready")
        cx_ready = sem("cx_ready")
        mixh_ready, mixl_ready = sem("mixh_ready"), sem("mixl_ready")
        qbd_zero, qbd_ready, kqbd_ready = sem("qbd_zero"), sem("qbd_ready"), sem("kqbd_ready")
        page_used = sem("page_used")
        dscores_ready, dexp_ready, dprobs_ready = sem("dscores_ready"), sem("dexp_ready"), sem("dprobs_ready")
        xc_ready, xch_ready, xcl_ready = sem("xc_ready"), sem("xch_ready"), sem("xcl_ready")
        tail_ready = sem("tail_ready")
        tr_done, a_done, a2_ready, ti_ready = sem("tr_done"), sem("a_done"), sem("a2_ready"), sem("ti_ready")
        v_ready, xi_ready, root_ready, gelu_ready = sem("v_ready"), sem("xi_ready"), sem("root_ready"), sem("gelu_ready")
        hs_ready, hg_ready = sem("hs_ready"), sem("hg_ready")
        dve_order, act_order = sem("dve_order"), sem("act_order")

        block = ctx.enter_context(nc.Block())

        def wait_job(eng, name_or_j):
            j = J[name_or_j] if isinstance(name_or_j, str) else name_or_j
            eng.wait_ge(acc_ready, j + 1)

        def wait_drained(eng, name):
            eng.wait_ge(drained[J[name] % ACCS], J[name] // ACCS + 1)

        def drains(ins, name):
            ins.then_inc(drained[J[name] % ACCS], 1)

        stat_order = [f"{s}.{w}" for s in range(SUBS) for w in ("post", "pre") if f"{s}.{w}" in J]

        def rs_count(name):
            return stat_order.index(name) + 1

        def x_count(s, c):
            return KC * POSTS.index(s) + c + 1

        def wait_x(eng, s, c):
            if s == 0:
                eng.wait_ge(in_x, 16)
            elif s % 4 == 0:
                eng.wait_ge(ple_x, KC * (s // 4 - 1) + c + 1)
            else:
                eng.wait_ge(x_ready, x_count(s, c))

        @block.sync
        def _(sp):
            sp.dma_start(params[:, :], params_d).then_inc(in_params, 16)
            sp.dma_start(x[:, :, :], x_d).then_inc(in_x, 16)

            def load(n, slot, size, src):
                if not isinstance(n, int) or n >= 2:
                    sp.wait_ge(lo_ready, n - 1)
                sp.dma_start(raw[slot][:, 0:size], src.rearrange("(p n) -> p n", p=P)).then_inc(raw_loaded[slot], 16)

            n = 0
            while n < n_units:
                _, at, size, _ = PLAN.units[n]
                alike = 1
                while n + alike < n_units and PLAN.units[n + alike][2] == size:
                    alike += 1
                pairs = alike // 2 if n >= 2 else 0
                if pairs >= 2:
                    with sp.Fori(0, pairs) as i:
                        for e in range(2):
                            load(n + e + 2 * i, (n + e) % 2, size,
                                 weights[bass.ds(at + e * P * size + i * (2 * P * size), P * size)])
                    n += 2 * pairs
                else:
                    load(n, n % 2, size, weights[at:at + P * size])
                    n += 1
            for m in range(KC):
                sp.wait_ge(ple_x, KC * (DEPTH - 1) + m + 1)
                sp.dma_start(y_o[:, m, :], x[:, m, :]).then_inc(y_stored, 16)
            sp.wait_ge(y_stored, 16 * KC)

        @block.gpsimd
        def _(pool):
            pool.memset(mean_of[:, :], 1.0 / D).then_inc(consts_made, 1)
            pool.memset(one[:, :], 1.0).then_inc(consts_made, 1)
            pool.memset(eps[:, :], EPS).then_inc(consts_made, 1)
            pool.dma_start(const[:, :], const_d).then_inc(in_const, 16)
            pool.dma_start(table[:, :], table_d).then_inc(in_table, 16)

            def add_squares(s):
                for c in range(1, KC):
                    pool.wait_ge(xsq_ready, KC * s + c + 1)
                    if c > 1:
                        pool.wait_ge(xsum_added, (KC - 1) * s + c - 1)
                    nc.gpsimd.tensor_tensor(xsum[:, :], xsum[:, :], xsq[c % 2][:, :], ALU.add)\
                        .then_inc(xsum_added, 1)

            def store(out, src):
                pool.dma_start(out, src).then_inc(stored, 16)
                count[0] += 16

            count = [0]
            for s in range(SUBS):
                add_squares(s)
                if s % 4 == 3:
                    pool.wait_ge(x_ready, x_count(s, 0))
                    pool.dma_start(p_raw[:, :, :], p_d[s // 4]).then_inc(p_loaded, 16)
                if s == S_AB:
                    pool.wait_ge(x_ready, x_count(s, KC - 1))
                    nc.gpsimd.memset(qbd[:, :, :, :], 0.0).then_inc(qbd_zero, 1)
                    pool.wait_ge(in_table, 16)
                    pages = []
                    for n in range(DEC * PAGES):
                        page = pool.value_load(table[0:1, n:n + 1], min_val=0, max_val=kpages_d.shape[0] - 1)
                        pages.append(page)
                        b, g = divmod(n, PAGES)
                        pool.dma_start(dlf[b * HEADS:(b + 1) * HEADS, g * PAGE:(g + 1) * PAGE],
                                       lfpages_d[bass.ds(page, 1), :, :].rearrange("a h n -> (a h) n"))\
                            .then_inc(lf_loaded, 16)
                        if n < RING:
                            pool.dma_start(ring[:, n, :], kpages_d[bass.ds(page, 1), :, :]
                                           .rearrange("a p n -> (a p) n")).then_inc(ring_loaded[n], 16)
                    for g in range(RING, 2 * DEC * PAGES):
                        src = kpages_d if g < DEC * PAGES else vpages_d
                        page = pages[g % (DEC * PAGES)]
                        page = pool.value_load(table[0:1, g % (DEC * PAGES):g % (DEC * PAGES) + 1],
                                               min_val=0, max_val=kpages_d.shape[0] - 1)
                        pool.wait_ge(page_used, g - RING + 1)
                        pool.dma_start(ring[:, g % RING, :], src[bass.ds(page, 1), :, :]
                                       .rearrange("a p n -> (a p) n")).then_inc(ring_loaded[g % RING], 16)
                    wait_drained(pool, f"{s}.k3")
                    store(k_o, k[:, :, :])
                    wait_drained(pool, f"{s}.v3")
                    store(v_o, v[:, :, :])
                    pool.wait_ge(f_log, 1)
                    store(logf_o, logf[:, :])
                    pool.wait_ge(cx_ready, AC)
                    store(cx_o, cx_tail[:, :, :])
                    state = par("state_b", 0, AC * (CB - 1) * DEC).rearrange("p (c j b) -> p c j b", c=AC, j=CB - 1)
                    store(cbstate_o, state[:, :, CB - 2, :])
                    pool.wait_ge(stored, count[0])
                if s == S_C:
                    pool.wait_ge(tail_ready, KC)
                    store(xr_o, xr_tail[:, :, :])
                    state = par("state_c", 0, KC * (CC - 1) * DEC)\
                        .rearrange("p (c j) -> p c j", c=KC)
                    store(ccstate_o, state[:, :, DEC:(CC - 1) * DEC])
                    pool.wait_ge(hs_ready, KC + 1)
                    store(h_o, xi[:, :, SEQ - 1:TOK])
                    pool.wait_ge(stored, count[0])

        @block.scalar
        def _(act):
            order = [0]

            def chained(ins):
                order[0] += 1
                ins.then_inc(act_order, 1)
                act.wait_ge(act_order, order[0])

            def split_hi(n, slot, size, before=None):
                act.wait_ge(raw_loaded[slot], 16 * (n // 2) + 16 if isinstance(n, int) else n)
                if before is not None:
                    act.wait_ge(acc_ready, before + 1)
                nc.scalar.activation(w_hi[slot][:, 0:size], raw[slot][:, 0:size], ACT.Copy).then_inc(hi_ready, 1)

            def refill(n):
                split_hi(n, n % 2, PLAN.units[n][2], last_job[n - 2] if n >= 2 else None)

            def done(name):
                if name in REFILL:
                    refill(REFILL[name])

            act.wait_ge(consts_made, 3)
            refill(0)
            refill(1)
            act.wait_ge(in_params, 16)
            chained(nc.scalar.activation(lru[:, 0:KC], par("lam", 0, KC), ACT.Abs))
            nc.scalar.activation(lru[:, KC:2 * KC], lru[:, 0:KC], ACT.Exp, scale=-1.0).then_inc(nl_act, 1)

            def statistics(name, rs):
                wait_job(act, name)
                drains(nc.scalar.activation(two(rs[:, :]), tile_of(J[name]), ACT.Sqrt, bias=eps[:, 0:1]), name)

            def begin(s):
                if s % 4:
                    statistics(f"{s}.post", rs_post)
                elif s:
                    wait_job(act, f"{s - 1}.pe{KC - 1}")
                for c in range(KC):
                    wait_x(act, s, c)
                    if c == 0:
                        act.wait_ge(in_params, 16)
                    nc.scalar.activation(act_hi[:, c, :], x[:, c, :], ACT.Copy, scale=pre_gain(s, c))\
                        .then_inc(acth_ready, 1)
                    if c >= 3:
                        act.wait_ge(xsum_added, (KC - 1) * s + c - 2)
                    nc.scalar.activation(xsum[:, :] if c == 0 else xsq[c % 2][:, :], x[:, c, :], ACT.Square)\
                        .then_inc(xsq_ready, 1)
                statistics(f"{s}.pre", rs_pre)

            def hidden(s, j, jobs, e, unit_hi):
                g, u, tile = jobs
                act.wait_ge(drained[g % ACCS if isinstance(g, int) else g[0]],
                            g // ACCS + 1 if isinstance(g, int) else g[1])
                nc.scalar.activation(gs[e][:, :], gs[e][:, :], ACT.Silu).then_inc(silu_ready, 1)
                unit_hi()
                act.wait_ge(h_ready, tile + 1)
                nc.scalar.activation(hid_hi[:, j, :] if isinstance(j, int) else
                                     hid_hi[:, j, :].rearrange("p a n -> p (a n)"),
                                     us[e][:, :], ACT.Copy).then_inc(hidh_ready, 1)

            def squares(s, m, e, name):
                wait_drained(act, name)
                n = KC * POSTS.index(s + 1) + m
                if n >= 2:
                    act.wait_ge(ysum_added, n - 1)
                nc.scalar.activation(ysq[e][:, :], y[:, m, :], ACT.Square).then_inc(ysq_ready, 1)

            def ffn(s):
                tile0 = FT * (s // 2)
                k0 = 0
                for half in range(2):
                    n_t = HID[half]
                    pairs = n_t // 2

                    def straight(i):
                        for e in range(2):
                            j = k0 + 2 * i + e
                            hidden(s, j - k0, (J[f"{s}.g{j}"], J[f"{s}.u{j}"], tile0 + j), e,
                                   lambda: done(f"{s}.u{j}"))
                    first = 0
                    if half == 0:
                        straight(0)
                        first = 1
                    j0 = k0 + 2 * first
                    base = J[f"{s}.g{j0}"]
                    unit = U[f"{s}.in{j0}"]
                    with act.Fori(0, pairs - 1 - first) as i:
                        for e in range(2):
                            g = base + 2 * e
                            hidden(s, bass.ds(2 * i + (2 * first + e), 1),
                                   ((g % ACCS, i + (g // ACCS + 1)), None, 2 * i + (tile0 + j0 + e)), e,
                                   lambda: hidden_refill(unit + e, base + 2 * e + 1, i))
                    straight(pairs - 1)
                    for m in range(KC):
                        name = f"{s}.out{'ab'[half]}{m}"
                        if half == 1:
                            squares(s, m, m % 2, name)
                        done(name)
                    k0 += n_t

            def hidden_refill(n, last, i):
                slot = n % 2
                act.wait_ge(raw_loaded[slot], 16 * i + 16 * ((n + 2) // 2 + 1))
                act.wait_ge(acc_ready, ACCS * i + (last + 1))
                nc.scalar.activation(w_hi[slot][:, :], raw[slot][:, :], ACT.Copy).then_inc(hi_ready, 1)

            def attention(s):
                for m in range(4):
                    done(f"{s}.q{m}")
                for m in range(AC):
                    done(f"{s}.k{m}")
                act.wait_ge(f_z, 1)
                chained(nc.scalar.activation(xsq[0][0:HEADS, :], t[0][0:HEADS, :], ACT.Abs))
                nc.scalar.activation(xsq[1][0:HEADS, :], xsq[0][0:HEADS, :], ACT.Exp, scale=-1.0).then_inc(f_exp, 1)
                done(f"{s}.f")
                for m in range(AC):
                    done(f"{s}.v{m}")
                for kb in (0, 2):
                    name = f"{s}.vt{kb}"
                    wait_job(act, name)
                    drains(nc.scalar.activation(v_tok[:, kb:kb + 2, :], acc_of(name)[:, :, :], ACT.Copy), name)

                def decay_row(h):
                    name = f"{s}.ck{h}"
                    wait_job(act, name)
                    if h:
                        wait_drained(act, f"{s}.s{h - 1}.2")
                    drains(nc.scalar.activation(ckb[:, :], acc_of(name)[:, 0, :], ACT.Copy), name)

                def exponentials(h):
                    for qb in range(QB):
                        w = (qb + 1) * P
                        act.wait_ge(scores_ready, QB * h + qb + 1)
                        nc.scalar.activation(sc[:, qb, 0:w], sc[:, qb, 0:w], ACT.Exp, bias=nmx[:, qb:qb + 1],
                                             accum_out=den[:, qb:qb + 1]).then_inc(exp_ready, 1)

                decay_row(0)
                exponentials(0)
                for h in range(HEADS):
                    for n in tiles_at(s, h):
                        done(n)
                    if h == 2:
                        act.wait_ge(dscores_ready, 1)
                        nc.scalar.activation(ds[:, :], ds[:, :], ACT.Exp, bias=dnmx[:, 0:1],
                                             accum_out=dden[:, 0:1]).then_inc(dexp_ready, 1)
                    name = f"{s}.pt{h}.2"
                    wait_job(act, name)
                    if h:
                        wait_job(act, f"{s}.pv{h - 1}")
                    a = acc_of(name)
                    chained(nc.scalar.activation(pt[:, 2, 2 * P:SEQ], a[:, 0, 2 * P:SEQ], ACT.Copy))
                    drains(nc.scalar.activation(pt[:, 3, 3 * P:SEQ], a[:, 1, 3 * P:SEQ], ACT.Copy), name)
                    if h + 1 < HEADS:
                        decay_row(h + 1)
                        exponentials(h + 1)
                    name = f"{s}.pv{h}"
                    wait_job(act, name)
                    r = HD * (h % 2)
                    drains(nc.scalar.activation(q[r:r + HD, h // 2, 0:SEQ], acc_of(name)[r:r + HD, 0, :], ACT.Copy), name)
                wait_drained(act, f"{s}.dec_o")
                for c in range(KC):
                    if c >= AC:
                        act.wait_ge(cx_ready, AC + c - AC + 1)
                    else:
                        wait_drained(act, f"{s}.pv{2 * c}")
                        wait_drained(act, f"{s}.pv{2 * c + 1}")
                    src = q[:, c, :] if c < AC else conv[:, c - AC, :]
                    nc.scalar.activation(act_hi[:, c, :], src, ACT.Copy).then_inc(mixh_ready, 1)
                for m in range(KC):
                    squares(s, m, m % 2, f"{s}.out{m}")
                    done(f"{s}.out{m}")

            def recurrent(s):
                def conv_hi(c):
                    if c >= 4:
                        wait_job(act, f"{s}.i{c - 4}")
                    act.wait_ge(xc_ready, c + 1)
                    nc.scalar.activation(xc_hi[:, c % 4, :], xi[:, c, :], ACT.Copy).then_inc(xch_ready, 1)
                    nc.scalar.activation(xr_tail[:, c, :], lru_v[:, c, SEQ - CC + 1:TOK], ACT.Copy)\
                        .then_inc(tail_ready, 1)

                def gates(c):
                    tr, th, a2, ti = ysq[0], ysq[1], xsq[0], xsq[1]
                    name = f"{s}.r{c}"
                    wait_job(act, name)
                    if c:
                        act.wait_ge(tr_done, c)
                    drains(nc.scalar.activation(two(tr[:, :]), tile_of(J[name]), ACT.Tanh, scale=0.5,
                                                bias=lru[:, 2 * KC + c:2 * KC + c + 1]), name)
                    wait_drained(act, name)
                    nc.scalar.activation(lru_a[:, c, :], tr[:, :], ACT.Exp, scale=lru[:, c:c + 1],
                                         bias=lru[:, c:c + 1]).then_inc(a_done, 1)
                    if c:
                        act.wait_ge(v_ready, c)
                    nc.scalar.activation(th[:, :], tr[:, :], ACT.Tanh, scale=lru[:, KC + c:KC + c + 1],
                                         bias=lru[:, KC + c:KC + c + 1]).then_inc(tr_done, 1)
                    act.wait_ge(a_done, c + 1)
                    nc.scalar.activation(a2[:, :], lru_a[:, c, :], ACT.Square).then_inc(a2_ready, 1)
                    name = f"{s}.i{c}"
                    wait_job(act, name)
                    if c:
                        act.wait_ge(xi_ready, c)
                    drains(nc.scalar.activation(two(ti[:, :]), tile_of(J[name]), ACT.Tanh, scale=0.5,
                                                bias=lru[:, 3 * KC + c:3 * KC + c + 1]), name)

                act.wait_ge(nl_made, 1)
                for kind, c in c_steps():
                    if kind == "xr":
                        conv_hi(c)
                        done(f"{s}.xr{c}")
                    elif kind == "ri":
                        gates(c)
                        done(f"{s}.i{c}")
                    else:
                        done(f"{s}.gt{c}")
                for c in range(KC):
                    act.wait_ge(v_ready, c + 1)
                    nc.scalar.activation(lru_v[:, c, :], lru_v[:, c, :], ACT.Sqrt, scale=0.25).then_inc(root_ready, 1)
                for c in range(KC):
                    wait_drained(act, f"{s}.gt{c}")
                    nc.scalar.activation(gt[:, c, :], gt[:, c, :], ACT.Gelu_apprx_tanh).then_inc(gelu_ready, 1)
                for c in range(KC):
                    act.wait_ge(hg_ready, c + 1)
                    nc.scalar.activation(act_hi[:, c, :], t[c % 2][:, :], ACT.Copy).then_inc(mixh_ready, 1)
                for m in range(KC):
                    squares(s, m, m % 2, f"{s}.out{m}")
                    done(f"{s}.out{m}")

            def ple(s):
                for m in range(KC):
                    if m == 0:
                        act.wait_ge(p_loaded, 16 * (s // 4 + 1))
                        nc.scalar.activation(p_hi[:, :, :], p_raw[:, :, :], ACT.Copy).then_inc(ph_ready, 1)
                    wait_drained(act, f"{s}.gate{m}")
                    nc.scalar.activation(sig[:, m, :], sig[:, m, :], ACT.Sigmoid).then_inc(sig_ready, 1)
                    done(f"{s}.gate{m}")
                    if m % 4 == 3:
                        done(f"{s}.pe{m}")

            for s in range(SUBS):
                begin(s)
                {S_AB: attention, S_C: recurrent}.get(s, ffn if IS_FFN(s) else ple)(s)

        @block.vector
        def _(dve):
            order = [0]

            def chained(ins):
                order[0] += 1
                ins.then_inc(dve_order, 1)
                dve.wait_ge(dve_order, order[0])

            def split_lo(slot, size, n):
                dve.wait_ge(hi_ready, n + 1)
                nc.vector.tensor_tensor(w_lo[slot][:, 0:size], raw[slot][:, 0:size],
                                        w_hi[slot][:, 0:size].bitcast(F32), ALU.subtract).then_inc(lo_ready, 1)

            def refill(n):
                split_lo(n % 2, PLAN.units[n][2], n)

            def done(name):
                if name in REFILL:
                    refill(REFILL[name])

            def log1p(e, parts, tmp):
                a, b = tmp
                chained(nc.vector.tensor_scalar(a, e, 2.0, None, ALU.add))
                chained(nc.vector.reciprocal(a, a))
                chained(nc.vector.tensor_tensor(e, e, a, ALU.mult))
                chained(nc.vector.tensor_tensor(a, e, e, ALU.mult))
                chained(nc.vector.tensor_scalar(b, a, 1.0 / 15, None, ALU.mult))
                for odd in (13, 11, 9, 7, 5, 3):
                    chained(nc.vector.scalar_tensor_tensor(out=b, in0=b, scalar=1.0 / odd, in1=a,
                                                           op0=ALU.add, op1=ALU.mult))
                chained(nc.vector.scalar_tensor_tensor(out=e, in0=b, scalar=1.0, in1=e, op0=ALU.add, op1=ALU.mult))

            refill(0)
            refill(1)
            nc.vector.memset(ysum[:, :], 0.0).then_inc(ysum_zeroed, 1)
            dve.wait_ge(in_params, 16)
            nc.vector.tensor_scalar(half_norm[:, :], par("norm", 0, DEPTH * NN * KC), 0.5, None, ALU.mult)\
                .then_inc(half_made, 1)
            dve.wait_ge(nl_act, 1)
            e = lru[:, KC:2 * KC]
            log1p(e, P, (lru[:, 2 * KC:3 * KC], lru[:, 3 * KC:4 * KC]))
            chained(nc.vector.tensor_scalar(lru[:, 0:KC], par("lam", 0, KC), -1.0, 0.0, ALU.mult, ALU.max))
            chained(nc.vector.scalar_tensor_tensor(out=lru[:, 0:KC], in0=e, scalar=2.0, in1=lru[:, 0:KC],
                                                   op0=ALU.mult, op1=ALU.add))
            chained(nc.vector.tensor_scalar(lru[:, KC:2 * KC], lru[:, 0:KC], LRU_C / 2, None, ALU.mult))
            chained(nc.vector.tensor_scalar(lru[:, 0:KC], lru[:, 0:KC], -LRU_C / 2, None, ALU.mult))
            chained(nc.vector.tensor_scalar(lru[:, 2 * KC:3 * KC], par("b_rg", 0, KC), 0.5, None, ALU.mult))
            nc.vector.tensor_scalar(lru[:, 3 * KC:4 * KC], par("b_ig", 0, KC), 0.5, None, ALU.mult)\
                .then_inc(nl_made, 1)

            def begin(s):
                if s % 4:
                    name = f"{s}.post"
                    wait_drained(dve, name)
                    nc.vector.reciprocal(rs_post[:, :], rs_post[:, :]).then_inc(rs_ready, 1)
                    if s != POSTS[-1]:
                        nc.vector.memset(ysum[:, :], 0.0).then_inc(ysum_zeroed, 1)
                    dve.wait_ge(half_made, 1)

                def low(c):
                    dve.wait_ge(acth_ready, KC * s + c + 1)
                    nc.vector.scalar_tensor_tensor(out=act_lo[:, c, :], in0=x[:, c, :], scalar=pre_gain(s, c),
                                                   in1=act_hi[:, c, :].bitcast(F32), op0=ALU.mult,
                                                   op1=ALU.subtract).then_inc(actl_ready, 1)
                for c in range(KC):
                    if s % 4:
                        dve.wait_ge(rs_ready, rs_count(f"{s}.post"))
                        nc.vector.scalar_tensor_tensor(out=t[c % 2][:, :], in0=y[:, c, :], scalar=post_gain(s, c),
                                                       in1=rs_post[:, :], op0=ALU.mult, op1=ALU.mult)\
                            .then_inc(t_ready, 1)
                        dve.wait_ge(t_ready, x_count(s, c))
                        nc.vector.tensor_tensor(x[:, c, :], x[:, c, :], t[c % 2][:, :], ALU.add).then_inc(x_ready, 1)
                        if c:
                            low(c - 1)
                    else:
                        low(c)
                if s % 4:
                    low(KC - 1)
                wait_drained(dve, f"{s}.pre")
                nc.vector.reciprocal(rs_pre[:, :], rs_pre[:, :]).then_inc(rs_ready, 1)
                dve.wait_ge(rs_ready, rs_count(f"{s}.pre"))

            def scaled(out, name):
                wait_job(dve, name)
                drains(nc.vector.tensor_tensor(two(out), tile_of(J[name]), two(rs_pre[:, :]), ALU.mult), name)

            def hidden(j, e, gate, up, tile, unit_lo):
                for out, (a, wait, _) in ((gs[e], gate), (us[e], up)):
                    dve.wait_ge(acc_ready, wait)
                    nc.vector.tensor_tensor(two(out[:, :]), acc[a][:, :, 0:HALF], two(rs_pre[:, :]), ALU.mult)\
                        .then_inc(drained[a], 1)
                unit_lo()
                dve.wait_ge(silu_ready, tile + 1)
                dve.wait_ge(drained[up[0]], up[2])
                nc.vector.tensor_tensor(us[e][:, :], us[e][:, :], gs[e][:, :], ALU.mult).then_inc(h_ready, 1)
                dve.wait_ge(h_ready, tile + 1)
                dve.wait_ge(hidh_ready, tile + 1)
                pick = (lambda z: z[:, j, :]) if isinstance(j, int) else \
                    (lambda z: z[:, j, :].rearrange("p a n -> p (a n)"))
                nc.vector.tensor_tensor(pick(hid_lo), us[e][:, :], pick(hid_hi).bitcast(F32), ALU.subtract)\
                    .then_inc(hidl_ready, 1)

            def add_square(s, m):
                n = KC * POSTS.index(s + 1) + m
                dve.wait_ge(ysq_ready, n + 1)
                if m == 0:
                    dve.wait_ge(ysum_zeroed, POSTS.index(s + 1) + 1)
                else:
                    dve.wait_ge(ysum_added, n)
                nc.vector.tensor_tensor(ysum[:, :], ysum[:, :], ysq[m % 2][:, :], ALU.add).then_inc(ysum_added, 1)

            def ffn(s):
                tile0 = FT * (s // 2)
                k0 = 0
                for half in range(2):
                    pairs = HID[half] // 2

                    def straight(i):
                        for e in range(2):
                            j = k0 + 2 * i + e
                            g, u = J[f"{s}.g{j}"], J[f"{s}.u{j}"]
                            hidden(j - k0, e, (g % ACCS, g + 1, g // ACCS + 1), (u % ACCS, u + 1, u // ACCS + 1),
                                   tile0 + j, lambda: done(f"{s}.u{j}"))
                    first = 0
                    if half == 0:
                        straight(0)
                        first = 1
                    j0 = k0 + 2 * first
                    base = J[f"{s}.g{j0}"]
                    unit = U[f"{s}.in{j0}"]
                    with dve.Fori(0, pairs - 1 - first) as i:
                        for e in range(2):
                            g, u = base + 2 * e, base + 2 * e + 1
                            hidden(bass.ds(2 * i + (2 * first + e), 1), e,
                                   (g % ACCS, ACCS * i + (g + 1), None),
                                   (u % ACCS, ACCS * i + (u + 1), i + (u // ACCS + 1)),
                                   2 * i + (tile0 + j0 + e),
                                   lambda: split_lo((unit + e) % 2, UNIT, 2 * i + (unit + e + 2)))
                    straight(pairs - 1)
                    for m in range(KC):
                        name = f"{s}.out{'ab'[half]}{m}"
                        wait_job(dve, name)
                        if half == 0:
                            ins = nc.vector.tensor_copy(two(y[:, m, :]), tile_of(J[name]))
                        else:
                            ins = nc.vector.tensor_tensor(two(y[:, m, :]), tile_of(J[name]), two(y[:, m, :]), ALU.add)
                        drains(ins, name)
                        if half == 1:
                            add_square(s, m)
                        done(name)
                    k0 += HID[half]

            def mixer_out(s):
                for m in range(KC):
                    name = f"{s}.out{m}"
                    wait_job(dve, name)
                    drains(nc.vector.tensor_copy(two(y[:, m, :]), tile_of(J[name])), name)
                    add_square(s, m)
                    done(name)

            def attention(s):
                for m in range(AC):
                    name = f"{s}.q{m}"
                    wait_job(dve, name)
                    drains(nc.vector.scalar_tensor_tensor(out=two(q[:, m, :]), in0=tile_of(J[name]), scalar=HD ** -0.5,
                                                          in1=two(rs_pre[:, :]), op0=ALU.mult, op1=ALU.mult), name)
                    done(name)
                for m in range(AC):
                    scaled(k[:, m, :], f"{s}.k{m}")
                    done(f"{s}.k{m}")
                dve.wait_ge(qbd_zero, 1)
                for m in range(AC):
                    wait_drained(dve, f"{s}.q{m}")
                    wait_drained(dve, f"{s}.k{m}")
                for r in range(2):
                    rows = slice(HD * r, HD * (r + 1))
                    nc.vector.tensor_copy(qbd[rows, :, :, r], q[rows, :, SEQ:TOK].rearrange("p c b -> p b c"))\
                        .then_inc(qbd_ready, 1)
                dve.wait_ge(qbd_ready, 2)
                knew = k[:, :, SEQ:TOK].rearrange("p c b -> p b c")
                for r in range(2):
                    nc.vector.tensor_tensor(kqbd[:, :, :, r], qbd[:, :, :, r], knew, ALU.mult).then_inc(kqbd_ready, 1)
                name = f"{s}.f"
                z, mag, e = t[0][0:HEADS, :], xsq[0][0:HEADS, :], xsq[1][0:HEADS, :]
                wait_job(dve, name)
                drains(nc.vector.tensor_tensor(two(z), acc_of(name)[0:HEADS, :, 0:HALF], two(rs_pre[0:HEADS, :]),
                                               ALU.mult), name)
                wait_drained(dve, name)
                nc.vector.tensor_scalar(z, z, par("bf", 0, 1, HEADS), None, ALU.add).then_inc(f_z, 1)
                done(name)
                for m in range(AC):
                    scaled(v[:, m, :], f"{s}.v{m}")
                    done(f"{s}.v{m}")
                dve.wait_ge(f_exp, 1)
                dve.wait_ge(f_z, 1)
                log1p(e, HEADS, (mag, t[1][0:HEADS, :]))
                chained(nc.vector.tensor_scalar(mag, z, 0.0, None, ALU.min))
                nc.vector.scalar_tensor_tensor(out=logf[:, :], in0=e, scalar=-2.0, in1=mag, op0=ALU.mult,
                                               op1=ALU.add).then_inc(f_log, 1)
                dve.wait_ge(f_log, 1)
                chained(nc.vector.memset(t[1][0:HEADS, :], 1.0))
                nc.vector.tensor_tensor_scan(ch[:, :], t[1][0:HEADS, 0:SEQ], logf[:, 0:SEQ], 0.0,
                                             ALU.mult, ALU.add).then_inc(f_ch, 1)
                name = f"{s}.cq"
                wait_job(dve, name)
                drains(nc.vector.tensor_copy(cq[:, :, :], acc_of(name)[:, 0, 0:QB * HEADS]
                                             .rearrange("p (a h) -> p a h", a=QB)), name)
                wait_drained(dve, name)

                def softmax(h):
                    for qb in range(QB):
                        w = (qb + 1) * P
                        name = f"{s}.s{h}.{qb // 2 * 2}"
                        if qb % 2 == 0:
                            wait_job(dve, name)
                        if qb == 0:
                            wait_drained(dve, f"{s}.ck{h}")
                            if h:
                                wait_job(dve, f"{s}.pt{h - 1}.2")
                        ins = nc.vector.scalar_tensor_tensor(
                            out=sc[:, qb, 0:w], in0=acc_of(name)[:, qb % 2, 0:w], scalar=cq[:, qb, h:h + 1],
                            in1=ckb[:, 0:w], op0=ALU.add, op1=ALU.subtract)
                        if qb % 2:
                            drains(ins, name)
                            wait_drained(dve, name)
                        else:
                            chained(ins)
                        chained(nc.vector.tensor_tensor(sc[:, qb, w - P:w], sc[:, qb, w - P:w], mask, ALU.add))
                        nc.vector.tensor_reduce(nmx[:, qb:qb + 1], sc[:, qb, 0:w], AXX, ALU.max, negate=True)\
                            .then_inc(scores_ready, 1)
                    dve.wait_ge(exp_ready, QB * (h + 1))
                    chained(nc.vector.reciprocal(rden[:, :], den[:, :]))
                    for qb in range(QB):
                        w = (qb + 1) * P
                        nc.vector.tensor_scalar(sc[:, qb, 0:w], sc[:, qb, 0:w], rden[:, qb:qb + 1], None, ALU.mult)\
                            .then_inc(probs_ready, 1)

                def short_conv(m):
                    w = lambda j: par("convb_w", j * AC + m)
                    st = lambda j: par("state_b", (m * (CB - 1) + j) * DEC, DEC)
                    out = conv[:, m, :]
                    scaled(t[0][:, :], f"{s}.c{m}")
                    scaled(t[1][:, :], f"{s}.x{m}")
                    wait_drained(dve, f"{s}.c{m}")
                    wait_drained(dve, f"{s}.x{m}")
                    u = t[0]
                    chained(nc.vector.tensor_tensor(u[:, :], t[0][:, :], t[1][:, :], ALU.mult))
                    chained(nc.vector.tensor_scalar(out, u[:, :], w(CB - 1), None, ALU.mult))
                    for j in range(CB - 1):
                        back = CB - 1 - j
                        chained(nc.vector.scalar_tensor_tensor(out=out[:, back:SEQ], in0=u[:, 0:SEQ - back],
                                                               scalar=w(j), in1=out[:, back:SEQ],
                                                               op0=ALU.mult, op1=ALU.add))
                        chained(nc.vector.scalar_tensor_tensor(out=out[:, SEQ:TOK], in0=st(j), scalar=w(j),
                                                               in1=out[:, SEQ:TOK], op0=ALU.mult, op1=ALU.add))
                    nc.vector.tensor_copy(cx_tail[:, m, :], u[:, SEQ - CB + 1:TOK]).then_inc(cx_ready, 1)

                def decode(h):
                    if h == 1:
                        name = f"{s}.dec_s"
                        wait_job(dve, name)
                        a = acc_of(name)
                        chained(nc.vector.tensor_copy(sT[:, :], a[:, 0, 0:PAGES * BH]))
                        drains(nc.vector.tensor_tensor(dtmp[:, :], a[0:BH, 1, 0:DEC], same_b, ALU.mult), name)
                        wait_drained(dve, name)
                        chained(nc.vector.reduce_sum(dlf[:, PAST:PAST + 1], dtmp[:, :], AXX))
                        dve.wait_ge(lf_loaded, 16 * DEC * PAGES)
                        chained(nc.vector.memset(ds[:, :], 1.0))
                        chained(nc.vector.tensor_tensor_scan(dch[:, :], ds[:, :], dlf[:, :], 0.0, ALU.mult, ALU.add))
                    if h == 2:
                        name = f"{s}.dec_t"
                        wait_job(dve, name)
                        a = acc_of(name)
                        last = dch[:, PAST:PAST + 1]
                        chained(nc.vector.scalar_tensor_tensor(out=ds[:, 0:PAST], in0=a[0:BH, 0, 0:PAST], scalar=last,
                                                               in1=dch[:, 0:PAST], op0=ALU.add, op1=ALU.subtract))
                        drains(nc.vector.scalar_tensor_tensor(out=ds[:, PAST:PAST + 1], in0=a[0:BH, 1, 0:1],
                                                              scalar=last, in1=last, op0=ALU.add, op1=ALU.subtract),
                               name)
                        wait_drained(dve, name)
                        nc.vector.tensor_reduce(dnmx[:, :], ds[:, :], AXX, ALU.max, negate=True)\
                            .then_inc(dscores_ready, 1)
                        dve.wait_ge(dexp_ready, 1)
                        chained(nc.vector.reciprocal(dden[:, :], dden[:, :]))
                        chained(nc.vector.tensor_scalar(ds[:, :], ds[:, :], dden[:, 0:1], None, ALU.mult))
                        nc.vector.tensor_scalar(dsn[:, :], same_b, ds[:, PAST:PAST + 1], None, ALU.mult)\
                            .then_inc(dprobs_ready, 1)
                    if h == 3:
                        name = f"{s}.dec_p"
                        wait_job(dve, name)
                        a = acc_of(name)
                        chained(nc.vector.tensor_copy(pT[:, :], a[:, 0, 0:PAGES * BH]))
                        drains(nc.vector.tensor_tensor(onew[:, :, :], a[:, 1, 0:AC * DEC]
                                                       .rearrange("p (c b) -> p c b", c=AC),
                                                       v[:, :, SEQ:TOK], ALU.mult), name)
                        wait_drained(dve, name)
                    if h == 4:
                        name = f"{s}.dec_o"
                        wait_job(dve, name)
                        a = acc_of(name)[:, 0, 0:DEC * AC * 2].rearrange("p (b c r) -> p c b r", b=DEC, c=AC)
                        for r in range(2):
                            rows = slice(HD * r, HD * (r + 1))
                            ins = nc.vector.tensor_tensor(q[rows, :, SEQ:TOK], a[rows, :, :, r], onew[rows, :, :], ALU.add)
                            if r == 0:
                                chained(ins)
                        drains(ins, name)

                softmax(0)
                for h in range(HEADS):
                    if h < AC:
                        short_conv(h)
                    elif h < AC + AC // 2:
                        for m in (2 * (h - AC), 2 * (h - AC) + 1):
                            scaled(t[m % 2][:, :], f"{s}.b{m}")
                            wait_drained(dve, f"{s}.b{m}")
                            nc.vector.tensor_tensor(conv[:, m, :], conv[:, m, :], t[m % 2][:, :], ALU.mult)\
                                .then_inc(cx_ready, 1)
                    for n in tiles_at(s, h):
                        done(n)
                    decode(h)
                    name = f"{s}.pt{h}.0"
                    wait_job(dve, name)
                    if h:
                        wait_job(dve, f"{s}.pv{h - 1}")
                    a = acc_of(name)
                    chained(nc.vector.tensor_copy(pt[:, 0, :], a[:, 0, :]))
                    drains(nc.vector.tensor_copy(pt[:, 1, P:SEQ], a[:, 1, P:SEQ]), name)
                    if h + 1 < HEADS:
                        softmax(h + 1)
                for c in range(KC):
                    dve.wait_ge(mixh_ready, c + 1)
                    src = q[:, c, :] if c < AC else conv[:, c - AC, :]
                    nc.vector.tensor_tensor(act_lo[:, c, :], src, act_hi[:, c, :].bitcast(F32), ALU.subtract)\
                        .then_inc(mixl_ready, 1)
                mixer_out(s)

            def recurrent(s):
                def conv_gates(c):
                    w = lambda j: par("convc_w", j * KC + c)
                    st = lambda j: par("state_c", (c * (CC - 1) + j) * DEC, DEC)
                    u, out = lru_v[:, c, :], xi[:, c, :]
                    scaled(u, f"{s}.xr{c}")
                    wait_drained(dve, f"{s}.xr{c}")
                    chained(nc.vector.tensor_scalar(out, u, w(CC - 1), par("convc_b", c), ALU.mult, ALU.add))
                    for j in range(CC - 1):
                        back = CC - 1 - j
                        chained(nc.vector.scalar_tensor_tensor(out=out[:, SEQ:TOK], in0=st(j), scalar=w(j),
                                                               in1=out[:, SEQ:TOK], op0=ALU.mult, op1=ALU.add))
                        ins = nc.vector.scalar_tensor_tensor(out=out[:, back:SEQ], in0=u[:, 0:SEQ - back],
                                                             scalar=w(j), in1=out[:, back:SEQ],
                                                             op0=ALU.mult, op1=ALU.add)
                        if j < CC - 2:
                            chained(ins)
                    ins.then_inc(xc_ready, 1)
                    dve.wait_ge(xc_ready, c + 1)
                    dve.wait_ge(xch_ready, c + 1)
                    nc.vector.tensor_tensor(xc_lo[:, c % 4, :], out, xc_hi[:, c % 4, :].bitcast(F32), ALU.subtract)\
                        .then_inc(xcl_ready, 1)

                def gates(c):
                    th, a2, ti = ysq[1], xsq[0], xsq[1]
                    dve.wait_ge(a2_ready, c + 1)
                    dve.wait_ge(tr_done, c + 1)
                    nc.vector.scalar_tensor_tensor(out=lru_v[:, c, :], in0=a2[:, :], scalar=1.0, in1=th[:, :],
                                                   op0=ALU.add, op1=ALU.mult).then_inc(v_ready, 1)
                    wait_drained(dve, f"{s}.i{c}")
                    nc.vector.scalar_tensor_tensor(out=xi[:, c, :], in0=ti[:, :], scalar=1.0, in1=xi[:, c, :],
                                                   op0=ALU.add, op1=ALU.mult).then_inc(xi_ready, 1)

                for kind, c in c_steps():
                    if kind == "xr":
                        conv_gates(c)
                        done(f"{s}.xr{c}")
                    elif kind == "ri":
                        gates(c)
                        done(f"{s}.i{c}")
                    else:
                        scaled(gt[:, c, :], f"{s}.gt{c}")
                        done(f"{s}.gt{c}")
                dve.wait_ge(xi_ready, KC)
                for c in range(KC):
                    dve.wait_ge(root_ready, c + 1)
                    chained(nc.vector.tensor_tensor(lru_v[:, c, :], lru_v[:, c, :], xi[:, c, :], ALU.mult))
                h0 = par("h0", 0, KC * DEC).rearrange("p (c b) -> p c b", c=KC)
                last = xi[:, :, SEQ:TOK]
                dve.wait_ge(a_done, KC)
                chained(nc.vector.tensor_tensor(last, lru_a[:, :, SEQ:TOK], h0, ALU.mult))
                nc.vector.tensor_tensor(last, last, lru_v[:, :, SEQ:TOK], ALU.add).then_inc(hs_ready, 1)
                for c in range(KC):
                    nc.vector.tensor_tensor_scan(xi[:, c, 0:SEQ], lru_a[:, c, 0:SEQ], lru_v[:, c, 0:SEQ], 0.0,
                                                 ALU.mult, ALU.add).then_inc(hs_ready, 1)
                    dve.wait_ge(hs_ready, c + 2)
                    dve.wait_ge(gelu_ready, c + 1)
                    if c >= 2:
                        dve.wait_ge(mixl_ready, KC + c - 1)
                        dve.wait_ge(mixh_ready, KC + c - 1)
                    nc.vector.tensor_tensor(t[c % 2][:, :], gt[:, c, :], xi[:, c, :], ALU.mult).then_inc(hg_ready, 1)
                    dve.wait_ge(hg_ready, c + 1)
                    dve.wait_ge(mixh_ready, KC + c + 1)
                    nc.vector.tensor_tensor(act_lo[:, c, :], t[c % 2][:, :], act_hi[:, c, :].bitcast(F32),
                                            ALU.subtract).then_inc(mixl_ready, 1)
                dve.wait_ge(stored, 16 * 8)
                mixer_out(s)

            def ple(s):
                n = KC * (s // 4)

                def embedding(m):
                    name = f"{s}.pe{m}"
                    wait_job(dve, name)
                    dve.wait_ge(sig_ready, n + m + 1)
                    ins = nc.vector.tensor_tensor(two(t[m % 2][:, :]), tile_of(J[name]), two(sig[:, m, :]), ALU.mult)
                    drains(ins, name)
                    wait_drained(dve, name)
                    nc.vector.tensor_tensor(x[:, m, :], x[:, m, :], t[m % 2][:, :], ALU.add).then_inc(ple_x, 1)
                for m in range(KC):
                    if m == 0:
                        dve.wait_ge(ph_ready, s // 4 + 1)
                        nc.vector.tensor_tensor(p_lo[:, :, :], p_raw[:, :, :], p_hi[:, :, :].bitcast(F32),
                                                ALU.subtract).then_inc(pl_ready, 1)
                    scaled(sig[:, m, :], f"{s}.gate{m}")
                    done(f"{s}.gate{m}")
                    if m % 4 == 3:
                        for c in range(m - 3, m + 1):
                            embedding(c)
                        done(f"{s}.pe{m}")

            for s in range(SUBS):
                begin(s)
                {S_AB: attention, S_C: recurrent}.get(s, ffn if IS_FFN(s) else ple)(s)

        @block.tensor
        def _(pe):
            def claim(j, turn=None):
                if turn is not None:
                    pe.wait_ge(drained[j % ACCS], turn)
                elif j >= ACCS:
                    pe.wait_ge(drained[j % ACCS], j // ACCS)
                return acc[j % ACCS]

            def chunk(a, slot, at, hi, lo, first, last, width=P):
                for n, (w, m) in enumerate(((w_hi, hi), (w_hi, lo), (w_lo, hi))):
                    for half in range(2):
                        ins = nc.tensor.matmul(a[0:width, half, 0:HALF], w[slot][:, at:at + width],
                                               m[:, half * HALF:(half + 1) * HALF],
                                               start=first and n == 0, stop=last and n == 2)
                return ins

            def tile(j, slot, ks, at, hi, lo, turn=None, wait=None, width=P):
                a = claim(j, turn)
                for c in range(ks):
                    if wait is not None:
                        wait(c)
                    ins = chunk(a, slot, at(c), hi[:, c, :], lo[:, c, :], c == 0, c == ks - 1, width)
                ins.then_inc(acc_ready, 1)

            def wait_unit(n):
                pe.wait_ge(lo_ready, n + 1)

            def pair(s, names, unit, ks=KC, tiles=2, hi=None, lo=None):
                n = U[f"{s}.{unit}"]
                wait_unit(n)
                for i, name in enumerate(names):
                    tile(J[f"{s}.{name}"], n % 2, ks, lambda c: (c * tiles + i) * P, hi or act_hi, lo or act_lo)

            def k_outer(jobs, units, ready, wait):
                accs = [claim(j) for j in jobs]
                for c in range(KC):
                    wait(c)
                    for n, a in enumerate(accs):
                        unit = units[n // 2]
                        if c == 0 and n % 2 == 0:
                            wait_unit(unit)
                        ins = chunk(a, unit % 2, (2 * c + n % 2) * P, act_hi[:, c, :], act_lo[:, c, :],
                                    c == 0, c == KC - 1)
                        if c == KC - 1:
                            ins.then_inc(acc_ready, 1)

            def mean(name, squares_of):
                a = claim(J[name])
                for half in range(2):
                    ins = nc.tensor.matmul(a[:, half, 0:HALF], mean_of[:, :],
                                           squares_of[:, half * HALF:(half + 1) * HALF], start=True, stop=True)
                ins.then_inc(acc_ready, 1)

            def begin(s, tiles, units):
                if s % 4:
                    pe.wait_ge(ysum_added, KC * (POSTS.index(s) + 1))
                    mean(f"{s}.post", ysum)
                un = [U[f"{s}.{u}"] for u in units]
                k_outer([J[f"{s}.{n}"] for n in tiles[0:3]], un, None,
                        lambda c: pe.wait_ge(actl_ready, KC * s + c + 1))
                pe.wait_ge(xsum_added, (KC - 1) * (s + 1))
                mean(f"{s}.pre", xsum)
                tile(J[f"{s}.{tiles[3]}"], un[1] % 2, KC, lambda c: (2 * c + 1) * P, act_hi, act_lo)

            def ffn(s):
                begin(s, ["g0", "u0", "g1", "u1"], ["in0", "in1"])
                tile0 = FT * (s // 2)
                k0 = 0
                for half in range(2):
                    first = 2 if half == 0 else 0
                    j0 = k0 + first
                    base, unit = J[f"{s}.g{j0}"], U[f"{s}.in{j0}"]
                    with pe.Fori(0, (HID[half] - first) // 2) as i:
                        for e in range(2):
                            pe.wait_ge(lo_ready, 2 * i + (unit + e + 1))
                            for n in range(2):
                                j = base + 2 * e + n
                                tile(j, (unit + e) % 2, KC, lambda c: (2 * c + n) * P, act_hi, act_lo,
                                     turn=i + j // ACCS)
                    tag = "ab"[half]
                    base, unit = J[f"{s}.out{tag}0"], U[f"{s}.out{tag}0"]
                    with pe.Fori(0, KC // 4) as i:
                        for e in range(4):
                            pe.wait_ge(lo_ready, 4 * i + (unit + e + 1))
                            wait = (lambda c: pe.wait_ge(hidl_ready, tile0 + k0 + c + 1)) if e == 0 else None
                            tile(base + e, (unit + e) % 2, HID[half], lambda c: c * P, hid_hi, hid_lo,
                                 turn=i + (base + e) // ACCS, wait=wait)
                    k0 += HID[half]

            def mixer_out(s, n0):
                un = [U[f"{s}.out0"], U[f"{s}.out2"]]
                k_outer([J[f"{s}.out{m}"] for m in range(3)], un, None, lambda c: pe.wait_ge(mixl_ready, n0 + c + 1))
                tile(J[f"{s}.out3"], un[1] % 2, KC, lambda c: (2 * c + 1) * P, act_hi, act_lo)
                for m in (4, 6):
                    pair(s, [f"out{m}", f"out{m + 1}"], f"out{m}")

            def attention(s):
                begin(s, ["q0", "q1", "q2", "q3"], ["q0", "q2"])
                for m in (0, 2):
                    pair(s, [f"k{m}", f"k{m + 1}"], f"k{m}")
                n = U[f"{s}.f"]
                wait_unit(n)
                tile(J[f"{s}.f"], n % 2, KC, lambda c: c * HEADS, act_hi, act_lo, width=HEADS)
                for m in (0, 2):
                    pair(s, [f"v{m}", f"v{m + 1}"], f"v{m}")
                pe.wait_ge(in_const, 16)
                for m in range(AC):
                    wait_drained(pe, f"{s}.v{m}")
                    wait_drained(pe, f"{s}.q{m}")
                    wait_drained(pe, f"{s}.k{m}")
                for kb in (0, 2):
                    a = claim(J[f"{s}.vt{kb}"])
                    for n in range(2):
                        for m in range(AC):
                            ins = nc.tensor.transpose(a[:, n, m * P:(m + 1) * P],
                                                      v[:, m, (kb + n) * P:(kb + n + 1) * P], ident)
                    ins.then_inc(acc_ready, 1)
                pe.wait_ge(f_ch, 1)
                a = claim(J[f"{s}.cq"])
                for qb in range(QB):
                    ins = nc.tensor.transpose(a[:, 0, qb * HEADS:(qb + 1) * HEADS], ch[:, qb * P:(qb + 1) * P],
                                              const[0:HEADS, IDENT:IDENT + HEADS])
                ins.then_inc(acc_ready, 1)

                def scores(h):
                    a = claim(J[f"{s}.ck{h}"])
                    nc.tensor.matmul(a[:, 0, :], const[0:HEADS, IDENT + h:IDENT + h + 1].broadcast_to([HEADS, P]),
                                     ch[:, :], start=True, stop=True).then_inc(acc_ready, 1)
                    rows = slice(HD * (h % 2), HD * (h % 2) + HD)
                    for qb in range(QB):
                        if qb % 2 == 0:
                            a = claim(J[f"{s}.s{h}.{qb}"])
                        ins = nc.tensor.matmul(a[:, qb % 2, 0:(qb + 1) * P], q[rows, h // 2, qb * P:(qb + 1) * P],
                                               k[rows, h // 2, 0:(qb + 1) * P], start=True, stop=True)
                        if qb % 2:
                            ins.then_inc(acc_ready, 1)

                def decode(h):
                    if h == 1:
                        a = claim(J[f"{s}.dec_s"])
                        pe.wait_ge(qbd_ready, 2)
                        for n in range(DEC * PAGES):
                            b, g = divmod(n, PAGES)
                            pe.wait_ge(ring_loaded[n % RING], 16 * (n // RING + 1))
                            for c in range(AC):
                                at = g * BH + b * HEADS + 2 * c
                                ins = nc.tensor.matmul(a[:, 0, at:at + 2], ring[:, n % RING, c * P:(c + 1) * P],
                                                       qbd[:, b, c, :], start=True, stop=True)
                            ins.then_inc(page_used, 1)
                        nc.tensor.matmul(a[0:BH, 1, 0:DEC], to_bh, logf[:, SEQ:TOK], start=True, stop=True).then_inc(acc_ready, 1)
                    if h == 2:
                        a = claim(J[f"{s}.dec_t"])
                        wait_drained(pe, f"{s}.dec_s")
                        for g in range(PAGES):
                            nc.tensor.transpose(a[0:BH, 0, g * PAGE:(g + 1) * PAGE], sT[:, g * BH:(g + 1) * BH], ident)
                        pe.wait_ge(kqbd_ready, 2)
                        nc.tensor.matmul(a[0:BH, 1, 0:1], kqbd[:, :, :, :].rearrange("p b c r -> p (b c r)"), one[:, :],
                                         start=True, stop=True).then_inc(acc_ready, 1)
                    if h == 3:
                        a = claim(J[f"{s}.dec_p"])
                        pe.wait_ge(dprobs_ready, 1)
                        for g in range(PAGES):
                            nc.tensor.transpose(a[:, 0, g * BH:(g + 1) * BH], ds[:, g * PAGE:(g + 1) * PAGE],
                                                const[0:BH, IDENT:IDENT + BH])
                        for c in range(AC):
                            ins = nc.tensor.matmul(a[:, 1, c * DEC:(c + 1) * DEC], to_rows[:, c * P:(c + 1) * P],
                                                   dsn[:, :], start=True, stop=True)
                        ins.then_inc(acc_ready, 1)
                    if h == 4:
                        a = claim(J[f"{s}.dec_o"])
                        wait_drained(pe, f"{s}.dec_p")
                        for b in range(DEC):
                            n = DEC * PAGES + b * PAGES
                            for g in range(PAGES):
                                pe.wait_ge(ring_loaded[(n + g) % RING], 16 * ((n + g) // RING + 1))
                            for c in range(AC):
                                at = (b * AC + c) * 2
                                for g in range(PAGES):
                                    src = g * BH + b * HEADS + 2 * c
                                    ins = nc.tensor.matmul(a[:, 0, at:at + 2], ring[:, (n + g) % RING, c * P:(c + 1) * P],
                                                           pT[:, src:src + 2], start=g == 0, stop=g == PAGES - 1)
                                    if c == AC - 1 and b < DEC - 1:
                                        ins.then_inc(page_used, 1)
                        ins.then_inc(acc_ready, 1)

                scores(0)
                for h in range(HEADS):
                    if h < AC:
                        pair(s, [f"c{h}", f"x{h}"], f"cx{h}")
                    elif h < AC + AC // 2:
                        m = 2 * (h - AC)
                        pair(s, [f"b{m}", f"b{m + 1}"], f"b{m}")
                    decode(h)
                    pe.wait_ge(probs_ready, QB * (h + 1))
                    for kb in range(QB):
                        if kb % 2 == 0:
                            a = claim(J[f"{s}.pt{h}.{kb}"])
                        for qb in range(kb, QB):
                            ins = nc.tensor.transpose(a[:, kb % 2, qb * P:(qb + 1) * P],
                                                      sc[:, qb, kb * P:(kb + 1) * P], ident)
                        if kb % 2:
                            ins.then_inc(acc_ready, 1)
                    if h + 1 < HEADS:
                        scores(h + 1)
                    a = claim(J[f"{s}.pv{h}"])
                    wait_drained(pe, f"{s}.pt{h}.0")
                    wait_drained(pe, f"{s}.pt{h}.2")
                    if h == 0:
                        wait_drained(pe, f"{s}.vt0")
                        wait_drained(pe, f"{s}.vt2")
                    r = HD * (h % 2)
                    for kb in range(QB):
                        ins = nc.tensor.matmul(a[r:r + HD, 0, kb * P:SEQ], v_tok[:, kb, h * HD:(h + 1) * HD],
                                               pt[:, kb, kb * P:SEQ], start=kb == 0, stop=kb == QB - 1)
                    ins.then_inc(acc_ready, 1)
                mixer_out(s, 0)

            def recurrent(s):
                begin(s, ["xr0", "xr1", "xr2", "xr3"], ["xr0", "xr2"])

                def gates(m):
                    n = U[f"{s}.ri{m}"]
                    wait_unit(n)
                    for c in (m, m + 1):
                        pe.wait_ge(xcl_ready, c + 1)
                        for i, kind in enumerate("ri"):
                            j = J[f"{s}.{kind}{c}"]
                            a = claim(j)
                            chunk(a, n % 2, (2 * (c - m) + i) * P, xc_hi[:, c % 4, :], xc_lo[:, c % 4, :], True, True)\
                                .then_inc(acc_ready, 1)

                gates(0)
                for m in (4, 6):
                    pair(s, [f"xr{m}", f"xr{m + 1}"], f"xr{m}")
                    gates(m - 2)
                pair(s, ["gt0", "gt1"], "gt0")
                gates(6)
                for m in (2, 4, 6):
                    pair(s, [f"gt{m}", f"gt{m + 1}"], f"gt{m}")
                mixer_out(s, KC)

            def ple(s):
                begin(s, ["gate0", "gate1", "gate2", "gate3"], ["gate0", "gate2"])
                for m in (0, 4):
                    if m:
                        pair(s, ["gate4", "gate5"], "gate4")
                        pair(s, ["gate6", "gate7"], "gate6")
                    pe.wait_ge(pl_ready, s // 4 + 1)
                    pair(s, [f"pe{n}" for n in range(m, m + 4)], f"pe{m}", ks=PLE_K, tiles=4, hi=p_hi, lo=p_lo)

            pe.wait_ge(consts_made, 3)
            for s in range(SUBS):
                {S_AB: attention, S_C: recurrent}.get(s, ffn if IS_FFN(s) else ple)(s)


def tiles_at(s, h):
    if h < AC:
        return [f"{s}.c{h}", f"{s}.x{h}"]
    if h < AC + AC // 2:
        return [f"{s}.b{2 * (h - AC)}", f"{s}.b{2 * (h - AC) + 1}"]
    return []


def c_steps():
    steps = [("xr", c) for c in range(4)]
    steps += [("ri", 0), ("ri", 1)]
    for m in (4, 6):
        steps += [("xr", m), ("xr", m + 1), ("ri", m - 2), ("ri", m - 1)]
    steps += [("gt", 0), ("gt", 1), ("ri", 6), ("ri", 7)]
    return steps + [("gt", c) for c in range(2, KC)]


def kernel(**inputs):
    import concourse.bacc as bacc
    from concourse.bass_utils import run_bass_kernel_spmd

    a = {name: np.asarray(value) for name, value in inputs.items()}
    f32 = np.float32

    def feature_major(m):
        return m.T.reshape(m.shape[1] // P, P, m.shape[0]).transpose(1, 0, 2)

    def by_chunk(m):
        lead = m.shape[:-1]
        return np.moveaxis(m.reshape(*lead, m.shape[-1] // P, P), -1, 0)

    ri = np.stack([a["c_w_rg"][0], a["c_w_ig"][0]], axis=1)
    a["c_w_ri"] = ri.transpose(2, 0, 1, 3).reshape(1, P, 2 * D)
    stream = np.empty(PLAN.size, f32)
    for _, at, size, (array, layer, k0, ks, ranges) in PLAN.units:
        w = a[array][layer][k0 * P:(k0 + ks) * P]
        w = np.concatenate([w[:, lo:hi] for lo, hi in ranges], axis=1)
        stream[at:at + P * size] = w.reshape(ks, P, -1).transpose(1, 0, 2).reshape(-1)

    blocks = {
        "norm": by_chunk(a["norms"]),
        "bf": np.concatenate([a["ab_b_f"][0], np.zeros(P - HEADS, f32)]),
        "convb_w": by_chunk(a["ab_conv_w"][0]), "convc_w": by_chunk(a["c_conv_w"][0]),
        "convc_b": by_chunk(a["c_conv_b"][0]), "b_rg": by_chunk(a["c_b_rg"][0]),
        "b_ig": by_chunk(a["c_b_ig"][0]), "lam": by_chunk(a["c_lam"][0]),
        "state_b": by_chunk(a["state_conv_b"][:, 0]).transpose(0, 3, 2, 1),
        "state_c": by_chunk(a["state_conv_c"][:, 0]).transpose(0, 3, 2, 1),
        "h0": by_chunk(a["state_h_c"][:, 0]).transpose(0, 2, 1),
    }
    params = np.concatenate([blocks[n].reshape(P, -1) for n in PARAMS], axis=1)

    const = np.zeros((P, N_CONST), f32)
    const[:, IDENT:IDENT + P] = np.eye(P)
    const[:, MASK:MASK + P] = np.triu(np.full((P, P), NEG), 1)
    const[0:BH, SAME_B:SAME_B + DEC] = np.repeat(np.eye(DEC), HEADS, axis=0)
    const[0:HEADS, TO_BH:TO_BH + BH] = np.tile(np.eye(HEADS), (1, DEC))
    const[0:BH, TO_ROWS:TO_ROWS + AC * P] = np.tile(np.repeat(np.eye(HEADS), HD, axis=1), (DEC, 1))

    tokens = np.concatenate([a["x_prompt"][0], a["x_sample"][:, 0]])
    p = np.stack([feature_major(np.concatenate([a["p_prompt"][i, 0], a["p_sample"][i, :, 0]])) for i in range(DEPTH)])
    pages = a["cache_k"].shape[0]
    k_pages = a["cache_k"][:, 0].reshape(pages, PAGE, AC, P).transpose(0, 3, 2, 1).reshape(pages, P, D_A)
    v_pages = a["cache_v"][:, 0].reshape(pages, PAGE, D_A)
    lf_pages = a["cache_logf"][:, 0].transpose(0, 2, 1)
    host = {"weights": stream, "params": params, "const": const, "x": feature_major(tokens), "p": p,
            "k_pages": k_pages, "v_pages": v_pages, "lf_pages": lf_pages,
            "table": a["page_table"].reshape(1, DEC * PAGES)}
    outs = {"y": (P, KC, TOK), "k": (P, AC, TOK), "v": (P, AC, TOK), "logf": (HEADS, TOK),
            "cx": (P, AC, CB - 1 + DEC), "cb_state": (P, AC, DEC),
            "xr": (P, KC, CC - 1 + DEC), "cc_state": (P, KC, (CC - 2) * DEC), "h": (P, KC, 1 + DEC)}

    nc = bacc.Bacc("TRN2", target_bir_lowering=False, num_devices=1)
    arrays, args = {}, []
    for name, value in host.items():
        value = np.ascontiguousarray(value)
        arrays[f"in_{name}"] = value
        args.append(nc.dram_tensor(f"in_{name}", value.shape, mybir.dt.from_np(value.dtype), kind="ExternalInput").ap())
    for name, shape in outs.items():
        args.append(nc.dram_tensor(f"out_{name}", shape, F32, kind="ExternalOutput").ap())
    trunk(nc, *args)
    r = run_bass_kernel_spmd(nc, [arrays], core_ids=[0]).results[0]
    o = {name: np.asarray(r[f"out_{name}"]) for name in outs}

    def tokens_of(m):
        return m.transpose(2, 1, 0).reshape(m.shape[2], -1)

    y, k, v = (tokens_of(o[n]) for n in "ykv")
    logf, cx, xr, h = o["logf"].T, tokens_of(o["cx"]), tokens_of(o["xr"]), tokens_of(o["h"])
    heads = lambda m: m.reshape(m.shape[0], HEADS, HD)
    cb0 = tokens_of(o["cb_state"])
    cc0 = o["cc_state"].reshape(P, KC, CC - 2, DEC).transpose(3, 2, 1, 0).reshape(DEC, CC - 2, D)
    return (
        y[None, :SEQ], y[SEQ:, None],
        heads(k[:SEQ])[None, None], heads(v[:SEQ])[None, None], logf[None, None, :SEQ],
        heads(k[SEQ:])[:, None, None], heads(v[SEQ:])[:, None, None], logf[SEQ:][:, None, None],
        cx[None, None, :CB - 1], np.stack([cb0, cx[CB - 1:]], axis=1)[:, None],
        xr[None, None, :CC - 1], np.concatenate([cc0, xr[CC - 1:][:, None]], axis=1)[:, None],
        h[None, None, 0], h[1:][:, None],
    )
```

```python
import math
from contextlib import ExitStack

import numpy as np
import concourse.bass as bass
from concourse import mybir

F32 = mybir.dt.float32
F32R = mybir.dt.float32r
I32 = mybir.dt.int32
ALU = mybir.AluOpType
ACT = mybir.ActivationFunctionType
AXX = mybir.AxisListType.X

P = 128
D = 1024
KC = D // P
SEQ, DEC = 512, 8
TOK = SEQ + DEC
HALF = TOK // 2
DEPTH = 2
D_FF = 2816
FT = D_FF // P
HID = (12, FT - 12)
HEADS, HD = 8, 64
AC = HEADS * HD // P
D_A = HEADS * HD
CB, CC = 3, 4
LRU_C = 8.0
PLE_K = 256 // P
PAGES, PAGE = 2, 128
PAST = PAGES * PAGE
BH = DEC * HEADS
NN = 7
EPS = 1e-6
NEG = -1e30
QB = SEQ // P
ACCS = 4
UNIT = 2048
RING = 4
STEPS = DEC * PAGES // RING

PARAMS = {}
_at = 0
for _name, _n in (("norm", DEPTH * NN * KC), ("bf", 1), ("convb_w", CB * AC), ("convc_w", CC * KC),
                  ("convc_b", KC), ("b_rg", KC), ("b_ig", KC), ("lam", KC),
                  ("state_b", AC * (CB - 1) * DEC), ("state_c", KC * (CC - 1) * DEC), ("h0", KC * DEC)):
    PARAMS[_name] = (_at, _n)
    _at += _n
N_PARAMS = _at
IDENT, MASK, SAME_B, TO_BH, TO_ROWS = 0, P, 2 * P, 2 * P + DEC, 2 * P + DEC + BH
N_CONST = TO_ROWS + AC * P


def decode_step(h):
    return ["dec_s2", "dec_s3", "dec_t", "dec_p", "dec_o0", "dec_o1", "dec_o2", "dec_o3"][h]


class Plan:

    def __init__(self):
        self.job, self.units, self.unit, self.last_of, self.size = {}, [], {}, {}, 0

    def add_job(self, name, unit=None):
        self.job[name] = len(self.job)
        if unit is not None:
            self.last_of[unit] = name

    def add_unit(self, name, what):
        size = what[3] * sum(b - a for a, b in what[4])
        self.unit[name] = len(self.units)
        self.units.append((name, self.size, size, what))
        self.size += P * size

    def refills(self):
        return {job: self.unit[u] + 2 for u, job in self.last_of.items() if self.unit[u] + 2 < len(self.units)}


def col(i, n=1):
    return (i * P, (i + n) * P)


def make_plan():
    pl = Plan()

    def first_group(s, tiles, units):
        pl.add_job(f"{s}.pre")
        for n in range(3):
            pl.add_job(f"{s}.{tiles[n]}", units[n // 2])
        pl.add_job(f"{s}.{tiles[3]}", units[1])

    def out_tiles(s, what, k, ks, tag=""):
        for m in range(KC):
            pl.add_unit(f"{s}.out{tag}{m}", (*what, k, ks, [col(m)]))
            pl.add_job(f"{s}.out{tag}{m}", f"{s}.out{tag}{m}")

    def out_pairs(s, what):
        for m in range(0, KC, 2):
            pl.add_unit(f"{s}.out{m}", (*what, 0, KC, [col(m, 2)]))
            pl.add_job(f"{s}.out{m}", f"{s}.out{m}")
            pl.add_job(f"{s}.out{m + 1}", f"{s}.out{m}")

    def ffn(s, name, layer):
        if s % 4:
            pl.add_job(f"{s}.post")
        for half, k0 in enumerate((0, HID[0])):
            for j in range(k0, k0 + HID[half]):
                pl.add_unit(f"{s}.in{j}", (name + "_wi", layer, 0, KC, [col(j), col(FT + j)]))
            if half == 0:
                first_group(s, ["g0", "u0", "g1", "u1"], [f"{s}.in0", f"{s}.in1"])
            for j in range(k0 + 2 * (half == 0), k0 + HID[half]):
                pl.add_job(f"{s}.g{j}", f"{s}.in{j}")
                pl.add_job(f"{s}.u{j}", f"{s}.in{j}")
            out_tiles(s, (name + "_wo", layer), k0, HID[half], "ab"[half])

    def ple(s, layer):
        pl.add_job(f"{s}.post")
        gate = lambda m: (f"{s}.gate{m}", ("ple_w_pg", layer, 0, KC, [col(m, 2)]))
        embed = lambda m: (f"{s}.pe{m}", ("ple_w_pe", layer, 0, PLE_K, [col(m, 4)]))
        for m in (0, 4):
            pl.add_unit(*gate(m))
            pl.add_unit(*gate(m + 2))
            pl.add_unit(*embed(m))
            if m == 0:
                first_group(s, ["gate0", "gate1", "gate2", "gate3"], [f"{s}.gate0", f"{s}.gate2"])
            else:
                for n in range(m, m + 4):
                    pl.add_job(f"{s}.gate{n}", f"{s}.gate{n // 2 * 2}")
            for n in range(m, m + 4):
                pl.add_job(f"{s}.pe{n}", f"{s}.pe{m}")

    def ab(s):
        w = ("ab_w_in", 0, 0, KC)
        f0 = 3 * D_A
        gate0, c0, x0 = (f0 + HEADS + n * D_A for n in range(3))
        tile = lambda at, m, n=1: (at + m * P, at + (m + n) * P)
        pl.add_job(f"{s}.post")
        for m in (0, 2):
            pl.add_unit(f"{s}.q{m}", (*w, [tile(0, m, 2)]))
        first_group(s, ["q0", "q1", "q2", "q3"], [f"{s}.q0", f"{s}.q2"])
        pl.add_unit(f"{s}.f", (*w, [(f0, f0 + HEADS)]))
        pl.add_job(f"{s}.f", f"{s}.f")
        for m in (0, 2):
            pl.add_unit(f"{s}.k{m}", (*w, [tile(D_A, m, 2)]))
            pl.add_job(f"{s}.k{m}", f"{s}.k{m}")
            pl.add_job(f"{s}.k{m + 1}", f"{s}.k{m}")
        for m in (0, 2):
            pl.add_unit(f"{s}.v{m}", (*w, [tile(2 * D_A, m, 2)]))
            pl.add_job(f"{s}.v{m}", f"{s}.v{m}")
            pl.add_job(f"{s}.v{m + 1}", f"{s}.v{m}")
            pl.add_job(f"{s}.dec_s{m // 2}")
        for j in ("vt0", "vt2", "cq", "ck0", "s0.0", "s0.2"):
            pl.add_job(f"{s}.{j}")
        for h in range(HEADS):
            if h < AC:
                pl.add_unit(f"{s}.cx{h}", (*w, [tile(c0, h), tile(x0, h)]))
                pl.add_job(f"{s}.c{h}", f"{s}.cx{h}")
                pl.add_job(f"{s}.x{h}", f"{s}.cx{h}")
            elif h < AC + AC // 2:
                m = 2 * (h - AC)
                pl.add_unit(f"{s}.b{m}", (*w, [tile(gate0, m, 2)]))
                pl.add_job(f"{s}.b{m}", f"{s}.b{m}")
                pl.add_job(f"{s}.b{m + 1}", f"{s}.b{m}")
            pl.add_job(f"{s}.{decode_step(h)}")
            pl.add_job(f"{s}.pt{h}.0")
            pl.add_job(f"{s}.pt{h}.2")
            if h + 1 < HEADS:
                for j in (f"ck{h + 1}", f"s{h + 1}.0", f"s{h + 1}.2"):
                    pl.add_job(f"{s}.{j}")
            pl.add_job(f"{s}.pv{h}")
        out_pairs(s, ("ab_w_out", 0))

    def cm(s):
        pl.add_job(f"{s}.post")
        xr = lambda m: pl.add_unit(f"{s}.xr{m}", ("c_w_in", 0, 0, KC, [(D + m * P, D + (m + 2) * P)]))

        def pair(kind, m):
            pl.add_job(f"{s}.{kind}{m}", f"{s}.{kind}{m}")
            pl.add_job(f"{s}.{kind}{m + 1}", f"{s}.{kind}{m}")

        def gates(m):
            pl.add_unit(f"{s}.ri{m}", ("c_w_ri", 0, 0, 1, [col(2 * m, 4)]))
            for n in (m, m + 1):
                pl.add_job(f"{s}.r{n}", f"{s}.ri{m}")
                pl.add_job(f"{s}.i{n}", f"{s}.ri{m}")

        def gate(m):
            pl.add_unit(f"{s}.gt{m}", ("c_w_in", 0, 0, KC, [col(m, 2)]))
            pair("gt", m)

        xr(0)
        xr(2)
        first_group(s, ["xr0", "xr1", "xr2", "xr3"], [f"{s}.xr0", f"{s}.xr2"])
        gate(0)
        gates(0)
        for m in (4, 6):
            xr(m)
            pair("xr", m)
            gates(m - 2)
        gate(2)
        gates(6)
        for m in (4, 6):
            gate(m)
        out_pairs(s, ("c_w_out", 0))

    for layer in range(DEPTH):
        ffn(4 * layer, "ffn1", layer)
        (ab if layer % 2 == 0 else cm)(4 * layer + 1)
        ffn(4 * layer + 2, "ffn2", layer)
        ple(4 * layer + 3, layer)
    return pl


PLAN = make_plan()
SUBS = 4 * DEPTH
POSTS = [s for s in range(SUBS) if s % 4]
IS_FFN = lambda s: s % 2 == 0
S_AB, S_C = 1, 5


def trunk(nc, weights, params_d, const_d, x_d, p_d, kpages_d, vpages_d, lfpages_d, table_d,
          y_o, k_o, v_o, logf_o, cx_o, cbstate_o, xr_o, ccstate_o, h_o):
    J, U = PLAN.job, PLAN.unit
    REFILL = PLAN.refills()
    n_units = len(PLAN.units)
    last_job = [J[PLAN.last_of[name]] for name, *_ in PLAN.units]

    ctx = ExitStack()
    with ctx:
        def sb(name, shape, dt=F32):
            return ctx.enter_context(nc.sbuf_tensor(name, shape, dt))

        def sem(name):
            return ctx.enter_context(nc.semaphore(name))

        def overlay(*groups):
            made, most = [], 0
            for group in groups:
                with ExitStack() as own:
                    made += [own.enter_context(nc.sbuf_tensor(n, s, dt)) for n, s, dt in group]
                    most = max(most, sum(4 * math.prod(s[1:]) for _, s, _ in group))
            sb("under_" + groups[0][0][0], [P, (most + 63) // 4])
            return made

        x = sb("x", [P, KC, TOK])
        act_hi = sb("act_hi", [P, KC, TOK], F32R)
        act_lo = sb("act_lo", [P, KC, TOK], F32R)
        raw = [sb(f"raw{i}", [P, UNIT]) for i in range(2)]
        w_hi = [sb(f"w_hi{i}", [P, UNIT], F32R) for i in range(2)]
        w_lo = [sb(f"w_lo{i}", [P, UNIT], F32R) for i in range(2)]
        params = sb("params", [P, N_PARAMS])
        half_norm = sb("half_norm", [P, DEPTH * NN * KC])
        const = sb("const", [P, N_CONST])
        mean_of = sb("mean_of", [P, P])
        one = sb("one", [P, 1])
        eps = sb("eps", [P, 1])
        table_use = sb("table_use", [P, 1])
        rs_pre = sb("rs_pre", [P, TOK])
        rs_post = sb("rs_post", [P, TOK])
        xsum = sb("xsum", [P, TOK])
        ysum = sb("ysum", [P, TOK])
        xsq = [sb(f"xsq{i}", [P, TOK]) for i in range(2)]
        ysq = [sb(f"ysq{i}", [P, TOK]) for i in range(2)]
        t = [sb(f"t{i}", [P, TOK]) for i in range(2)]
        lru = sb("lru", [P, 4 * KC])
        xr_tail = sb("xr_tail", [P, KC, CC - 1 + DEC])
        y, ring, v_tok, xi = overlay(
            [("y", [P, KC, TOK], F32)],
            [("ring", [P, RING, D_A], F32), ("v_tok", [P, QB, D_A], F32)],
            [("xi", [P, KC, TOK], F32)])
        (hid_hi, hid_lo, gs0, gs1, us0, us1,
         p_raw, p_hi, p_lo, sig,
         q, k, v, conv, sc, pt, ckb, logf, ch, cq, nmx, den, rden, cx_tail,
         qbd, kqbd, sT, dlf, dch, ds, dsn, pT, onew, dnmx, dden, dtmp,
         lru_a, lru_v, gt, xc_hi, xc_lo) = overlay(
            [("hid_hi", [P, HID[0], TOK], F32R), ("hid_lo", [P, HID[0], TOK], F32R),
             ("gs0", [P, TOK], F32), ("gs1", [P, TOK], F32), ("us0", [P, TOK], F32), ("us1", [P, TOK], F32)],
            [("p_raw", [P, PLE_K, TOK], F32), ("p_hi", [P, PLE_K, TOK], F32R), ("p_lo", [P, PLE_K, TOK], F32R),
             ("sig", [P, KC, TOK], F32)],
            [("q", [P, AC, TOK], F32), ("k", [P, AC, TOK], F32), ("v", [P, AC, TOK], F32),
             ("conv", [P, AC, TOK], F32), ("sc", [P, QB, SEQ], F32), ("pt", [P, QB, SEQ], F32),
             ("ckb", [P, SEQ], F32), ("logf", [HEADS, TOK], F32), ("ch", [HEADS, SEQ], F32),
             ("cq", [P, QB, HEADS], F32), ("nmx", [P, QB], F32), ("den", [P, QB], F32), ("rden", [P, QB], F32),
             ("cx_tail", [P, AC, CB - 1 + DEC], F32),
             ("qbd", [P, DEC, AC, 2], F32), ("kqbd", [P, DEC, AC, 2], F32), ("sT", [P, PAGES * BH], F32),
             ("dlf", [BH, PAST + 1], F32), ("dch", [BH, PAST + 1], F32), ("ds", [BH, PAST + 1], F32),
             ("dsn", [BH, DEC], F32), ("pT", [P, PAGES * BH], F32), ("onew", [P, AC, DEC], F32),
             ("dnmx", [BH, 1], F32), ("dden", [BH, 1], F32), ("dtmp", [BH, DEC], F32)],
            [("lru_a", [P, KC, TOK], F32), ("lru_v", [P, KC, TOK], F32), ("gt", [P, KC, TOK], F32),
             ("xc_hi", [P, 4, TOK], F32R), ("xc_lo", [P, 4, TOK], F32R)])
        gs, us = [gs0, gs1], [us0, us1]
        table = sb("table", [1, DEC * PAGES], I32)
        ident = const[:, IDENT:IDENT + P]
        mask = const[:, MASK:MASK + P]
        same_b = const[0:BH, SAME_B:SAME_B + DEC]
        to_bh = const[0:HEADS, TO_BH:TO_BH + BH]
        to_rows = const[0:BH, TO_ROWS:TO_ROWS + AC * P]
        acc = [ctx.enter_context(nc.psum_tensor(f"acc{i}", [P, 2, 512], F32)) for i in range(ACCS)]

        def par(name, i=0, n=1, parts=P):
            at = PARAMS[name][0] + i
            return params[0:parts, at:at + n]

        def gain(s, which, c, scaled=False):
            src = half_norm if scaled else params
            at = ((s // 4) * NN + which) * KC + c
            return src[:, at:at + 1]

        def pre_gain(s, c):
            return gain(s, (0, 2, 4, 6)[s % 4], c)

        def post_gain(s, c):
            return gain(s, (None, 1, 3, 5)[s % 4], c, scaled=IS_FFN(s - 1))

        def mixed_of(c, early, late):
            return early[:, c, :] if c < 4 else late[:, c, :]

        def two(ap):
            return ap.rearrange("p (a n) -> p a n", a=2)

        def acc_of(name):
            return acc[J[name] % ACCS]

        def tile_of(j):
            return acc[j % ACCS][:, :, 0:HALF]

        in_x, in_params, in_const, in_table = sem("in_x"), sem("in_params"), sem("in_const"), sem("in_table")
        raw_loaded = [sem(f"raw_loaded{i}") for i in range(2)]
        p_loaded = sem("p_loaded")
        ring_loaded = sem("ring_loaded")
        lf_loaded = sem("lf_loaded")
        hi_ready, lo_ready = sem("hi_ready"), sem("lo_ready")
        acc_ready = sem("acc_ready")
        drained = [sem(f"drained{i}") for i in range(ACCS)]
        consts_made = sem("consts_made")
        half_made, nl_act, nl_made = sem("half_made"), sem("nl_act"), sem("nl_made")
        table_set = sem("table_set")
        rs_ready = sem("rs_ready")
        ysum_zeroed, ysq_ready, ysum_added = sem("ysum_zeroed"), sem("ysq_ready"), sem("ysum_added")
        xsq_ready, xsum_added = sem("xsq_ready"), sem("xsum_added")
        t_ready, x_ready, ple_x = sem("t_ready"), sem("x_ready"), sem("ple_x")
        acth_ready, actl_ready = sem("acth_ready"), sem("actl_ready")
        silu_ready, h_ready = sem("silu_ready"), sem("h_ready")
        hidh_ready, hidl_ready = sem("hidh_ready"), sem("hidl_ready")
        ph_ready, pl_ready, sig_ready, pe_t = sem("ph_ready"), sem("pl_ready"), sem("sig_ready"), sem("pe_t")
        y_stored = sem("y_stored")
        stored = sem("stored")
        f_z, f_exp, f_log, f_ch = sem("f_z"), sem("f_exp"), sem("f_log"), sem("f_ch")
        scores_ready, exp_ready, probs_ready = sem("scores_ready"), sem("exp_ready"), sem("probs_ready")
        cx_made, cx_ready, bcx_ready = sem("cx_made"), sem("cx_ready"), sem("bcx_ready")
        mixh_ready, mixl_ready = sem("mixh_ready"), sem("mixl_ready")
        qbd_zero, qbd_ready, kqbd_ready = sem("qbd_zero"), sem("qbd_ready"), sem("kqbd_ready")
        dscores_ready, dexp_ready, dprobs_ready = sem("dscores_ready"), sem("dexp_ready"), sem("dprobs_ready")
        xc_ready, xch_ready, xcl_ready = sem("xc_ready"), sem("xch_ready"), sem("xcl_ready")
        tail_ready = sem("tail_ready")
        tr_done, a_done, a2_ready, ti_ready = sem("tr_done"), sem("a_done"), sem("a2_ready"), sem("ti_ready")
        v_ready, xi_ready, root_ready, gelu_ready = sem("v_ready"), sem("xi_ready"), sem("root_ready"), sem("gelu_ready")
        hs_ready, hg_ready = sem("hs_ready"), sem("hg_ready")
        dve_order, act_order = sem("dve_order"), sem("act_order")

        block = ctx.enter_context(nc.Block())

        def wait_job(eng, name_or_j):
            j = J[name_or_j] if isinstance(name_or_j, str) else name_or_j
            eng.wait_ge(acc_ready, j + 1)

        def wait_drained(eng, name):
            eng.wait_ge(drained[J[name] % ACCS], J[name] // ACCS + 1)

        def drains(ins, name):
            ins.then_inc(drained[J[name] % ACCS], 1)

        stat_order = [f"{s}.{w}" for s in range(SUBS) for w in ("post", "pre") if f"{s}.{w}" in J]

        def rs_count(name):
            return stat_order.index(name) + 1

        def x_count(s, c):
            return KC * POSTS.index(s) + c + 1

        def wait_x(eng, s, c):
            if s == 0:
                eng.wait_ge(in_x, 16)
            elif s % 4 == 0:
                eng.wait_ge(ple_x, KC * (s // 4 - 1) + c + 1)
            else:
                eng.wait_ge(x_ready, x_count(s, c))

        @block.sync
        def _(sp):
            sp.dma_start(params[:, :], params_d).then_inc(in_params, 16)
            sp.dma_start(x[:, :, :], x_d).then_inc(in_x, 16)

            def load(n, slot, size, src):
                if not isinstance(n, int) or n >= 2:
                    sp.wait_ge(lo_ready, n - 1)
                sp.dma_start(raw[slot][:, 0:size], src.rearrange("(p n) -> p n", p=P)).then_inc(raw_loaded[slot], 16)

            n = 0
            while n < n_units:
                _, at, size, _ = PLAN.units[n]
                alike = 1
                while n + alike < n_units and PLAN.units[n + alike][2] == size:
                    alike += 1
                pairs = alike // 2 if n >= 2 else 0
                if pairs >= 2:
                    with sp.Fori(0, pairs) as i:
                        for e in range(2):
                            load(n + e + 2 * i, (n + e) % 2, size,
                                 weights[bass.ds(at + e * P * size + i * (2 * P * size), P * size)])
                    n += 2 * pairs
                else:
                    load(n, n % 2, size, weights[at:at + P * size])
                    n += 1
            for m in range(KC):
                sp.wait_ge(ple_x, KC * (DEPTH - 1) + m + 1)
                sp.dma_start(y_o[:, m, :], x[:, m, :]).then_inc(y_stored, 16)
            sp.wait_ge(y_stored, 16 * KC)

        @block.gpsimd
        def _(pool):
            pool.memset(mean_of[:, :], 1.0 / D).then_inc(consts_made, 1)
            pool.memset(one[:, :], 1.0).then_inc(consts_made, 1)
            pool.memset(eps[:, :], EPS).then_inc(consts_made, 1)
            pool.dma_start(const[:, :], const_d).then_inc(in_const, 16)
            pool.dma_start(table[:, :], table_d).then_inc(in_table, 16)

            def add_squares(s):
                for c in range(1, KC):
                    pool.wait_ge(xsq_ready, KC * s + c + 1)
                    if c > 1:
                        pool.wait_ge(xsum_added, (KC - 1) * s + c - 1)
                    nc.gpsimd.tensor_tensor(xsum[:, :], xsum[:, :], xsq[c % 2][:, :], ALU.add)\
                        .then_inc(xsum_added, 1)

            def store(out, src):
                pool.dma_start(out, src).then_inc(stored, 16)
                count[0] += 16

            count = [0]
            for s in range(SUBS):
                add_squares(s)
                if s % 4 == 3:
                    pool.wait_ge(x_ready, x_count(s, 0))
                    pool.dma_start(p_raw[:, :, :], p_d[s // 4]).then_inc(p_loaded, 16)
                if s == S_AB:
                    pool.wait_ge(x_ready, x_count(s, KC - 1))
                    nc.gpsimd.memset(qbd[:, :, :, :], 0.0).then_inc(qbd_zero, 1)
                    pool.wait_ge(in_table, 16)

                    def gather(step):
                        src = kpages_d if step < STEPS else vpages_d
                        if step:
                            wait_job(pool, f"{s}.dec_{'so'[(step - 1) // STEPS]}{(step - 1) % STEPS}")
                        for i in range(RING):
                            n = step % STEPS * RING + i
                            page = pool.value_load(table[0:1, n:n + 1], min_val=0, max_val=kpages_d.shape[0] - 1)
                            pool.dma_start(ring[:, i, :], src[bass.ds(page, 1), :, :]
                                           .rearrange("a p n -> (a p) n")).then_inc(ring_loaded, 16)

                    gather(0)
                    for n in range(DEC * PAGES):
                        page = pool.value_load(table[0:1, n:n + 1], min_val=0, max_val=kpages_d.shape[0] - 1)
                        b, g = divmod(n, PAGES)
                        pool.dma_start(dlf[b * HEADS:(b + 1) * HEADS, g * PAGE:(g + 1) * PAGE],
                                       lfpages_d[bass.ds(page, 1), :, :].rearrange("a h n -> (a h) n"))\
                            .then_inc(lf_loaded, 16)
                    gather(1)
                    gather(2)
                    for h in range(HEADS):
                        if h < AC:
                            wait_drained(pool, f"{s}.c{h}")
                            wait_drained(pool, f"{s}.x{h}")
                            nc.gpsimd.tensor_tensor(t[0][:, :], t[0][:, :], t[1][:, :], ALU.mult).then_inc(cx_made, 1)
                        elif h < AC + AC // 2:
                            for m in (2 * (h - AC), 2 * (h - AC) + 1):
                                wait_drained(pool, f"{s}.b{m}")
                                nc.gpsimd.tensor_tensor(conv[:, m, :], conv[:, m, :], t[m % 2][:, :], ALU.mult)\
                                    .then_inc(bcx_ready, 1)
                        if h in (0, 1, 4, 5, 6):
                            gather(3 + h if h < 2 else 1 + h)
                    wait_drained(pool, f"{s}.k3")
                    store(k_o, k[:, :, :])
                    wait_drained(pool, f"{s}.v3")
                    store(v_o, v[:, :, :])
                    pool.wait_ge(f_log, 1)
                    store(logf_o, logf[:, :])
                    pool.wait_ge(cx_ready, AC)
                    store(cx_o, cx_tail[:, :, :])
                    state = par("state_b", 0, AC * (CB - 1) * DEC).rearrange("p (c j b) -> p c j b", c=AC, j=CB - 1)
                    store(cbstate_o, state[:, :, CB - 2, :])
                    pool.wait_ge(stored, count[0])
                if s == S_C:
                    for c in range(KC):
                        pool.wait_ge(xch_ready, c + 1)
                        nc.gpsimd.tensor_tensor(xc_lo[:, c % 4, :], xi[:, c, :], xc_hi[:, c % 4, :].bitcast(F32),
                                                ALU.subtract).then_inc(xcl_ready, 1)
                    pool.wait_ge(tail_ready, KC)
                    store(xr_o, xr_tail[:, :, :])
                    state = par("state_c", 0, KC * (CC - 1) * DEC)\
                        .rearrange("p (c j) -> p c j", c=KC)
                    store(ccstate_o, state[:, :, DEC:(CC - 1) * DEC])
                    pool.wait_ge(hs_ready, KC + 1)
                    store(h_o, xi[:, :, SEQ - 1:TOK])
                    pool.wait_ge(stored, count[0])

        @block.scalar
        def _(act):
            order = [0]

            def chained(ins):
                order[0] += 1
                ins.then_inc(act_order, 1)
                act.wait_ge(act_order, order[0])

            def split_hi(n, slot, size, before=None):
                act.wait_ge(raw_loaded[slot], 16 * (n // 2) + 16 if isinstance(n, int) else n)
                if before is not None:
                    act.wait_ge(acc_ready, before + 1)
                nc.scalar.activation(w_hi[slot][:, 0:size], raw[slot][:, 0:size], ACT.Copy).then_inc(hi_ready, 1)

            def refill(n):
                split_hi(n, n % 2, PLAN.units[n][2], last_job[n - 2] if n >= 2 else None)

            def done(name):
                if name in REFILL:
                    refill(REFILL[name])

            act.wait_ge(consts_made, 3)
            refill(0)
            refill(1)
            act.wait_ge(in_params, 16)
            chained(nc.scalar.activation(lru[:, 0:KC], par("lam", 0, KC), ACT.Abs))
            nc.scalar.activation(lru[:, KC:2 * KC], lru[:, 0:KC], ACT.Exp, scale=-1.0).then_inc(nl_act, 1)

            def statistics(name, rs):
                wait_job(act, name)
                drains(nc.scalar.activation(two(rs[:, :]), tile_of(J[name]), ACT.Sqrt, bias=eps[:, 0:1]), name)

            def begin(s):
                if s % 4:
                    statistics(f"{s}.post", rs_post)
                elif s:
                    wait_job(act, f"{s - 1}.gate{KC - 1}")
                for c in range(KC):
                    wait_x(act, s, c)
                    if c == 0:
                        act.wait_ge(in_params, 16)
                    nc.scalar.activation(act_hi[:, c, :], x[:, c, :], ACT.Copy, scale=pre_gain(s, c))\
                        .then_inc(acth_ready, 1)
                    if c >= 3:
                        act.wait_ge(xsum_added, (KC - 1) * s + c - 2)
                    nc.scalar.activation(xsum[:, :] if c == 0 else xsq[c % 2][:, :], x[:, c, :], ACT.Square)\
                        .then_inc(xsq_ready, 1)
                statistics(f"{s}.pre", rs_pre)

            def hidden(s, j, jobs, e, unit_hi):
                g, u, tile = jobs
                act.wait_ge(drained[g % ACCS if isinstance(g, int) else g[0]],
                            g // ACCS + 1 if isinstance(g, int) else g[1])
                nc.scalar.activation(gs[e][:, :], gs[e][:, :], ACT.Silu).then_inc(silu_ready, 1)
                unit_hi()
                act.wait_ge(h_ready, tile + 1)
                nc.scalar.activation(hid_hi[:, j, :] if isinstance(j, int) else
                                     hid_hi[:, j, :].rearrange("p a n -> p (a n)"),
                                     us[e][:, :], ACT.Copy).then_inc(hidh_ready, 1)

            def squares(s, m, e, name):
                if m == KC - 1:
                    if POSTS.index(s + 1):
                        act.wait_ge(table_set, POSTS.index(s + 1))
                    nc.scalar.activation(table_use[:, :], eps[:, :], ACT.Sqrt).then_inc(table_set, 1)
                wait_drained(act, name)
                n = POSTS.index(s + 1)
                if m >= 2:
                    act.wait_ge(ysum_added, (KC - 1) * n + m - 1)
                elif n:
                    wait_job(act, f"{POSTS[n - 1]}.post")
                nc.scalar.activation(ysq[e][:, :], y[:, m, :], ACT.Square).then_inc(ysq_ready, 1)

            def ffn(s):
                tile0 = FT * (s // 2)
                k0 = 0
                for half in range(2):
                    n_t = HID[half]
                    pairs = n_t // 2

                    def straight(i):
                        for e in range(2):
                            j = k0 + 2 * i + e
                            hidden(s, j - k0, (J[f"{s}.g{j}"], J[f"{s}.u{j}"], tile0 + j), e,
                                   lambda: done(f"{s}.u{j}"))
                    first = 0
                    if half == 0:
                        straight(0)
                        first = 1
                    j0 = k0 + 2 * first
                    base = J[f"{s}.g{j0}"]
                    unit = U[f"{s}.in{j0}"]
                    with act.Fori(0, pairs - 1 - first) as i:
                        for e in range(2):
                            g = base + 2 * e
                            hidden(s, bass.ds(2 * i + (2 * first + e), 1),
                                   ((g % ACCS, i + (g // ACCS + 1)), None, 2 * i + (tile0 + j0 + e)), e,
                                   lambda: hidden_refill(unit + e, base + 2 * e + 1, i))
                    straight(pairs - 1)
                    for m in range(KC):
                        name = f"{s}.out{'ab'[half]}{m}"
                        if half == 1:
                            squares(s, m, m % 2, name)
                        done(name)
                    k0 += n_t

            def hidden_refill(n, last, i):
                slot = n % 2
                act.wait_ge(raw_loaded[slot], 16 * i + 16 * ((n + 2) // 2 + 1))
                act.wait_ge(acc_ready, ACCS * i + (last + 1))
                nc.scalar.activation(w_hi[slot][:, :], raw[slot][:, :], ACT.Copy).then_inc(hi_ready, 1)

            def attention(s):
                for m in range(4):
                    done(f"{s}.q{m}")
                act.wait_ge(f_z, 1)
                chained(nc.scalar.activation(xsq[0][0:HEADS, :], t[0][0:HEADS, :], ACT.Abs))
                nc.scalar.activation(xsq[1][0:HEADS, :], xsq[0][0:HEADS, :], ACT.Exp, scale=-1.0).then_inc(f_exp, 1)
                done(f"{s}.f")
                for m in range(AC):
                    done(f"{s}.k{m}")
                for m in range(AC):
                    done(f"{s}.v{m}")
                for kb in (0, 2):
                    name = f"{s}.vt{kb}"
                    wait_job(act, name)
                    drains(nc.scalar.activation(v_tok[:, kb:kb + 2, :], acc_of(name)[:, :, :], ACT.Copy), name)

                def decay_row(h):
                    name = f"{s}.ck{h}"
                    wait_job(act, name)
                    if h:
                        wait_drained(act, f"{s}.s{h - 1}.2")
                    drains(nc.scalar.activation(ckb[:, :], acc_of(name)[:, 0, :], ACT.Copy), name)

                def exponentials(h):
                    for qb in range(QB):
                        w = (qb + 1) * P
                        act.wait_ge(scores_ready, QB * h + qb + 1)
                        nc.scalar.activation(sc[:, qb, 0:w], sc[:, qb, 0:w], ACT.Exp, bias=nmx[:, qb:qb + 1],
                                             accum_out=den[:, qb:qb + 1]).then_inc(exp_ready, 1)

                decay_row(0)
                exponentials(0)
                for h in range(HEADS):
                    for n in tiles_at(s, h):
                        done(n)
                    if h == 2:
                        act.wait_ge(dscores_ready, 1)
                        nc.scalar.activation(ds[:, :], ds[:, :], ACT.Exp, bias=dnmx[:, 0:1],
                                             accum_out=dden[:, 0:1]).then_inc(dexp_ready, 1)
                    if h == AC + AC // 2:
                        wait_job(act, f"{s}.b{AC - 1}")
                        for c in range(AC):
                            act.wait_ge(bcx_ready, c + 1)
                            nc.scalar.activation(act_hi[:, AC + c, :], conv[:, c, :], ACT.Copy).then_inc(mixh_ready, 1)
                    for kb in (0, 2):
                        name = f"{s}.pt{h}.{kb}"
                        wait_job(act, name)
                        if h:
                            wait_job(act, f"{s}.pv{h - 1}")
                        a = acc_of(name)
                        chained(nc.scalar.activation(pt[:, kb, kb * P:SEQ], a[:, 0, kb * P:SEQ], ACT.Copy))
                        drains(nc.scalar.activation(pt[:, kb + 1, (kb + 1) * P:SEQ], a[:, 1, (kb + 1) * P:SEQ], ACT.Copy),
                               name)
                    if h + 1 < HEADS:
                        decay_row(h + 1)
                        exponentials(h + 1)
                    name = f"{s}.pv{h}"
                    wait_job(act, name)
                    r = HD * (h % 2)
                    drains(nc.scalar.activation(q[r:r + HD, h // 2, 0:SEQ], acc_of(name)[r:r + HD, 0, :], ACT.Copy), name)
                for i in range(STEPS):
                    wait_drained(act, f"{s}.dec_o{i}")
                for c in range(AC):
                    wait_drained(act, f"{s}.pv{2 * c}")
                    wait_drained(act, f"{s}.pv{2 * c + 1}")
                    nc.scalar.activation(act_hi[:, c, :], q[:, c, :], ACT.Copy).then_inc(mixh_ready, 1)
                for m in range(KC):
                    squares(s, m, m % 2, f"{s}.out{m}")
                    done(f"{s}.out{m}")

            def recurrent(s):
                def conv_hi(c):
                    if c >= 4:
                        wait_job(act, f"{s}.i{c - 4}")
                    act.wait_ge(xc_ready, c + 1)
                    nc.scalar.activation(xc_hi[:, c % 4, :], xi[:, c, :], ACT.Copy).then_inc(xch_ready, 1)
                    nc.scalar.activation(xr_tail[:, c, :], lru_v[:, c, SEQ - CC + 1:TOK], ACT.Copy)\
                        .then_inc(tail_ready, 1)

                def gates(c):
                    tr, th, a2, ti = ysq[0], ysq[1], xsq[0], xsq[1]
                    name = f"{s}.r{c}"
                    wait_job(act, name)
                    if c:
                        act.wait_ge(tr_done, c)
                    drains(nc.scalar.activation(two(tr[:, :]), tile_of(J[name]), ACT.Tanh, scale=0.5,
                                                bias=lru[:, 2 * KC + c:2 * KC + c + 1]), name)
                    wait_drained(act, name)
                    name = f"{s}.i{c}"
                    wait_job(act, name)
                    if c:
                        act.wait_ge(xi_ready, c)
                    drains(nc.scalar.activation(two(ti[:, :]), tile_of(J[name]), ACT.Tanh, scale=0.5,
                                                bias=lru[:, 3 * KC + c:3 * KC + c + 1]), name)
                    nc.scalar.activation(lru_a[:, c, :], tr[:, :], ACT.Exp, scale=lru[:, c:c + 1],
                                         bias=lru[:, c:c + 1]).then_inc(a_done, 1)
                    if c:
                        act.wait_ge(v_ready, c)
                    nc.scalar.activation(th[:, :], tr[:, :], ACT.Tanh, scale=lru[:, KC + c:KC + c + 1],
                                         bias=lru[:, KC + c:KC + c + 1]).then_inc(tr_done, 1)
                    act.wait_ge(a_done, c + 1)
                    nc.scalar.activation(a2[:, :], lru_a[:, c, :], ACT.Square).then_inc(a2_ready, 1)

                act.wait_ge(nl_made, 1)
                for kind, c in c_steps("scalar"):
                    if kind == "conv":
                        conv_hi(c)
                    elif kind == "refill":
                        done(f"{s}.{c}")
                    elif kind == "gates":
                        gates(c)
                        done(f"{s}.i{c}")
                    elif kind == "gt":
                        done(f"{s}.gt{c}")
                for c in range(KC):
                    act.wait_ge(v_ready, c + 1)
                    nc.scalar.activation(lru_v[:, c, :], lru_v[:, c, :], ACT.Sqrt, scale=0.25).then_inc(root_ready, 1)

                def gelu(c):
                    wait_drained(act, f"{s}.gt{c}")
                    nc.scalar.activation(gt[:, c, :], gt[:, c, :], ACT.Gelu_apprx_tanh).then_inc(gelu_ready, 1)

                def mixed_hi(c):
                    act.wait_ge(hg_ready, c + 1)
                    nc.scalar.activation(mixed_of(c, xc_hi, act_hi), t[c % 2][:, :], ACT.Copy).then_inc(mixh_ready, 1)

                for c in range(4):
                    gelu(c)
                for c in range(4, KC):
                    done(f"{s}.gt{c}")
                    mixed_hi(c - 4)
                    gelu(c)
                wait_job(act, f"{s}.gt{KC - 1}")
                for c in range(4, KC):
                    mixed_hi(c)
                for m in range(KC):
                    squares(s, m, m % 2, f"{s}.out{m}")
                    done(f"{s}.out{m}")

            def ple(s):
                for m in range(KC):
                    if m == 0:
                        act.wait_ge(p_loaded, 16 * (s // 4 + 1))
                        nc.scalar.activation(p_hi[:, :, :], p_raw[:, :, :], ACT.Copy).then_inc(ph_ready, 1)
                    wait_drained(act, f"{s}.gate{m}")
                    nc.scalar.activation(sig[:, m, :], sig[:, m, :], ACT.Sigmoid).then_inc(sig_ready, 1)
                    done(f"{s}.gate{m}")
                    if m % 4 == 3:
                        done(f"{s}.pe{m}")

            for s in range(SUBS):
                begin(s)
                {S_AB: attention, S_C: recurrent}.get(s, ffn if IS_FFN(s) else ple)(s)

        @block.vector
        def _(dve):
            order = [0]

            def chained(ins):
                order[0] += 1
                ins.then_inc(dve_order, 1)
                dve.wait_ge(dve_order, order[0])

            def split_lo(slot, size, n):
                dve.wait_ge(hi_ready, n + 1)
                nc.vector.tensor_tensor(w_lo[slot][:, 0:size], raw[slot][:, 0:size],
                                        w_hi[slot][:, 0:size].bitcast(F32), ALU.subtract).then_inc(lo_ready, 1)

            def refill(n):
                split_lo(n % 2, PLAN.units[n][2], n)

            def done(name):
                if name in REFILL:
                    refill(REFILL[name])

            def log1p(e, parts, tmp):
                a, b = tmp
                chained(nc.vector.tensor_scalar(a, e, 2.0, None, ALU.add))
                chained(nc.vector.reciprocal(a, a))
                chained(nc.vector.tensor_tensor(e, e, a, ALU.mult))
                chained(nc.vector.tensor_tensor(a, e, e, ALU.mult))
                chained(nc.vector.tensor_scalar(b, a, 1.0 / 15, None, ALU.mult))
                for odd in (13, 11, 9, 7, 5, 3):
                    chained(nc.vector.scalar_tensor_tensor(out=b, in0=b, scalar=1.0 / odd, in1=a,
                                                           op0=ALU.add, op1=ALU.mult))
                chained(nc.vector.scalar_tensor_tensor(out=e, in0=b, scalar=1.0, in1=e, op0=ALU.add, op1=ALU.mult))

            refill(0)
            refill(1)
            nc.vector.memset(ysum[:, :], 0.0).then_inc(ysum_zeroed, 1)
            dve.wait_ge(in_params, 16)
            nc.vector.tensor_scalar(half_norm[:, :], par("norm", 0, DEPTH * NN * KC), 0.5, None, ALU.mult)\
                .then_inc(half_made, 1)
            dve.wait_ge(nl_act, 1)
            e = lru[:, KC:2 * KC]
            log1p(e, P, (lru[:, 2 * KC:3 * KC], lru[:, 3 * KC:4 * KC]))
            chained(nc.vector.tensor_scalar(lru[:, 0:KC], par("lam", 0, KC), -1.0, 0.0, ALU.mult, ALU.max))
            chained(nc.vector.scalar_tensor_tensor(out=lru[:, 0:KC], in0=e, scalar=2.0, in1=lru[:, 0:KC],
                                                   op0=ALU.mult, op1=ALU.add))
            chained(nc.vector.tensor_scalar(lru[:, KC:2 * KC], lru[:, 0:KC], LRU_C / 2, None, ALU.mult))
            chained(nc.vector.tensor_scalar(lru[:, 0:KC], lru[:, 0:KC], -LRU_C / 2, None, ALU.mult))
            chained(nc.vector.tensor_scalar(lru[:, 2 * KC:3 * KC], par("b_rg", 0, KC), 0.5, None, ALU.mult))
            nc.vector.tensor_scalar(lru[:, 3 * KC:4 * KC], par("b_ig", 0, KC), 0.5, None, ALU.mult)\
                .then_inc(nl_made, 1)

            def low(s, c):
                dve.wait_ge(acth_ready, KC * s + c + 1)
                nc.vector.scalar_tensor_tensor(out=act_lo[:, c, :], in0=x[:, c, :], scalar=pre_gain(s, c),
                                               in1=act_hi[:, c, :].bitcast(F32), op0=ALU.mult,
                                               op1=ALU.subtract).then_inc(actl_ready, 1)

            def begin(s):
                if s % 4:
                    name = f"{s}.post"
                    wait_drained(dve, name)
                    nc.vector.reciprocal(rs_post[:, :], rs_post[:, :]).then_inc(rs_ready, 1)
                    if s != POSTS[-1]:
                        nc.vector.memset(ysum[:, :], 0.0).then_inc(ysum_zeroed, 1)
                    dve.wait_ge(half_made, 1)

                for c in range(4 if s and s % 4 == 0 else 0, KC):
                    if s % 4:
                        dve.wait_ge(rs_ready, rs_count(f"{s}.post"))
                        nc.vector.scalar_tensor_tensor(out=t[c % 2][:, :], in0=y[:, c, :], scalar=post_gain(s, c),
                                                       in1=rs_post[:, :], op0=ALU.mult, op1=ALU.mult)\
                            .then_inc(t_ready, 1)
                        dve.wait_ge(t_ready, x_count(s, c))
                        nc.vector.tensor_tensor(x[:, c, :], x[:, c, :], t[c % 2][:, :], ALU.add).then_inc(x_ready, 1)
                        if c:
                            low(s, c - 1)
                    else:
                        low(s, c)
                if s % 4:
                    low(s, KC - 1)
                wait_drained(dve, f"{s}.pre")
                nc.vector.reciprocal(rs_pre[:, :], rs_pre[:, :]).then_inc(rs_ready, 1)
                dve.wait_ge(rs_ready, rs_count(f"{s}.pre"))

            def scaled(out, name):
                wait_job(dve, name)
                drains(nc.vector.tensor_tensor(two(out), tile_of(J[name]), two(rs_pre[:, :]), ALU.mult), name)

            def hidden(j, e, gate, up, tile, unit_lo):
                for out, (a, wait, _) in ((gs[e], gate), (us[e], up)):
                    dve.wait_ge(acc_ready, wait)
                    nc.vector.tensor_tensor(two(out[:, :]), acc[a][:, :, 0:HALF], two(rs_pre[:, :]), ALU.mult)\
                        .then_inc(drained[a], 1)
                unit_lo()
                dve.wait_ge(silu_ready, tile + 1)
                dve.wait_ge(drained[up[0]], up[2])
                nc.vector.tensor_tensor(us[e][:, :], us[e][:, :], gs[e][:, :], ALU.mult).then_inc(h_ready, 1)
                dve.wait_ge(h_ready, tile + 1)
                dve.wait_ge(hidh_ready, tile + 1)
                pick = (lambda z: z[:, j, :]) if isinstance(j, int) else \
                    (lambda z: z[:, j, :].rearrange("p a n -> p (a n)"))
                nc.vector.tensor_tensor(pick(hid_lo), us[e][:, :], pick(hid_hi).bitcast(F32), ALU.subtract)\
                    .then_inc(hidl_ready, 1)

            def add_square(s, m):
                if m == KC - 1:
                    return
                n = POSTS.index(s + 1)
                dve.wait_ge(ysq_ready, KC * n + m + 1)
                if m == 0:
                    dve.wait_ge(ysum_zeroed, n + 1)
                else:
                    dve.wait_ge(ysum_added, (KC - 1) * n + m)
                nc.vector.tensor_tensor(ysum[:, :], ysum[:, :], ysq[m % 2][:, :], ALU.add).then_inc(ysum_added, 1)

            def ffn(s):
                tile0 = FT * (s // 2)
                k0 = 0
                for half in range(2):
                    pairs = HID[half] // 2

                    def straight(i):
                        for e in range(2):
                            j = k0 + 2 * i + e
                            g, u = J[f"{s}.g{j}"], J[f"{s}.u{j}"]
                            hidden(j - k0, e, (g % ACCS, g + 1, g // ACCS + 1), (u % ACCS, u + 1, u // ACCS + 1),
                                   tile0 + j, lambda: done(f"{s}.u{j}"))
                    first = 0
                    if half == 0:
                        straight(0)
                        first = 1
                    j0 = k0 + 2 * first
                    base = J[f"{s}.g{j0}"]
                    unit = U[f"{s}.in{j0}"]
                    with dve.Fori(0, pairs - 1 - first) as i:
                        for e in range(2):
                            g, u = base + 2 * e, base + 2 * e + 1
                            hidden(bass.ds(2 * i + (2 * first + e), 1), e,
                                   (g % ACCS, ACCS * i + (g + 1), None),
                                   (u % ACCS, ACCS * i + (u + 1), i + (u // ACCS + 1)),
                                   2 * i + (tile0 + j0 + e),
                                   lambda: split_lo((unit + e) % 2, UNIT, 2 * i + (unit + e + 2)))
                    straight(pairs - 1)
                    for m in range(KC):
                        name = f"{s}.out{'ab'[half]}{m}"
                        wait_job(dve, name)
                        if half == 0:
                            ins = nc.vector.tensor_copy(two(y[:, m, :]), tile_of(J[name]))
                        else:
                            ins = nc.vector.tensor_tensor(two(y[:, m, :]), tile_of(J[name]), two(y[:, m, :]), ALU.add)
                        drains(ins, name)
                        if half == 1:
                            add_square(s, m)
                        done(name)
                    k0 += HID[half]

            def mixer_out(s):
                for m in range(KC):
                    name = f"{s}.out{m}"
                    wait_job(dve, name)
                    drains(nc.vector.tensor_copy(two(y[:, m, :]), tile_of(J[name])), name)
                    add_square(s, m)
                    done(name)

            def attention(s):
                for m in range(AC):
                    name = f"{s}.q{m}"
                    wait_job(dve, name)
                    drains(nc.vector.scalar_tensor_tensor(out=two(q[:, m, :]), in0=tile_of(J[name]), scalar=HD ** -0.5,
                                                          in1=two(rs_pre[:, :]), op0=ALU.mult, op1=ALU.mult), name)
                    done(name)
                def key_scores(i):
                    name = f"{s}.dec_s{i}"
                    wait_job(dve, name)
                    pick = lambda z: z.rearrange("p (g n) -> p g n", g=PAGES)[:, :, i * BH // STEPS:(i + 1) * BH // STEPS]
                    ins = nc.vector.tensor_copy(pick(sT[:, :]), pick(acc_of(name)[:, 0, 0:PAGES * BH]))
                    if i == STEPS - 1:
                        chained(ins)
                        ins = nc.vector.tensor_tensor(dtmp[:, :], acc_of(name)[0:BH, 1, 0:DEC], same_b, ALU.mult)
                    drains(ins, name)

                name = f"{s}.f"
                z, mag, e = t[0][0:HEADS, :], xsq[0][0:HEADS, :], xsq[1][0:HEADS, :]
                wait_job(dve, name)
                drains(nc.vector.tensor_tensor(two(z), acc_of(name)[0:HEADS, :, 0:HALF], two(rs_pre[0:HEADS, :]),
                                               ALU.mult), name)
                wait_drained(dve, name)
                nc.vector.tensor_scalar(z, z, par("bf", 0, 1, HEADS), None, ALU.add).then_inc(f_z, 1)
                done(name)
                dve.wait_ge(f_exp, 1)
                dve.wait_ge(f_z, 1)
                log1p(e, HEADS, (mag, t[1][0:HEADS, :]))
                chained(nc.vector.tensor_scalar(mag, z, 0.0, None, ALU.min))
                nc.vector.scalar_tensor_tensor(out=logf[:, :], in0=e, scalar=-2.0, in1=mag, op0=ALU.mult,
                                               op1=ALU.add).then_inc(f_log, 1)
                dve.wait_ge(f_log, 1)
                chained(nc.vector.memset(t[1][0:HEADS, :], 1.0))
                nc.vector.tensor_tensor_scan(ch[:, :], t[1][0:HEADS, 0:SEQ], logf[:, 0:SEQ], 0.0,
                                             ALU.mult, ALU.add).then_inc(f_ch, 1)
                for m in range(AC):
                    scaled(k[:, m, :], f"{s}.k{m}")
                    done(f"{s}.k{m}")
                dve.wait_ge(qbd_zero, 1)
                for m in range(AC):
                    wait_drained(dve, f"{s}.q{m}")
                    wait_drained(dve, f"{s}.k{m}")
                for r in range(2):
                    rows = slice(HD * r, HD * (r + 1))
                    nc.vector.tensor_copy(qbd[rows, :, :, r], q[rows, :, SEQ:TOK].rearrange("p c b -> p b c"))\
                        .then_inc(qbd_ready, 1)
                dve.wait_ge(qbd_ready, 2)
                knew = k[:, :, SEQ:TOK].rearrange("p c b -> p b c")
                for r in range(2):
                    nc.vector.tensor_tensor(kqbd[:, :, :, r], qbd[:, :, :, r], knew, ALU.mult).then_inc(kqbd_ready, 1)
                for m in range(AC):
                    scaled(v[:, m, :], f"{s}.v{m}")
                    done(f"{s}.v{m}")
                    if m % 2:
                        key_scores(m // 2)
                name = f"{s}.cq"
                wait_job(dve, name)
                drains(nc.vector.tensor_copy(cq[:, :, :], acc_of(name)[:, 0, 0:QB * HEADS]
                                             .rearrange("p (a h) -> p a h", a=QB)), name)
                wait_drained(dve, name)

                def softmax(h):
                    for qb in range(QB):
                        w = (qb + 1) * P
                        name = f"{s}.s{h}.{qb // 2 * 2}"
                        if qb % 2 == 0:
                            wait_job(dve, name)
                        if qb == 0:
                            wait_drained(dve, f"{s}.ck{h}")
                            if h:
                                wait_job(dve, f"{s}.pt{h - 1}.2")
                        ins = nc.vector.scalar_tensor_tensor(
                            out=sc[:, qb, 0:w], in0=acc_of(name)[:, qb % 2, 0:w], scalar=cq[:, qb, h:h + 1],
                            in1=ckb[:, 0:w], op0=ALU.add, op1=ALU.subtract)
                        if qb % 2:
                            drains(ins, name)
                            wait_drained(dve, name)
                        else:
                            chained(ins)
                        chained(nc.vector.tensor_tensor(sc[:, qb, w - P:w], sc[:, qb, w - P:w], mask, ALU.add))
                        nc.vector.tensor_reduce(nmx[:, qb:qb + 1], sc[:, qb, 0:w], AXX, ALU.max, negate=True)\
                            .then_inc(scores_ready, 1)
                    dve.wait_ge(exp_ready, QB * (h + 1))
                    chained(nc.vector.reciprocal(rden[:, :], den[:, :]))
                    for qb in range(QB):
                        w = (qb + 1) * P
                        nc.vector.tensor_scalar(sc[:, qb, 0:w], sc[:, qb, 0:w], rden[:, qb:qb + 1], None, ALU.mult)\
                            .then_inc(probs_ready, 1)

                def short_conv(m):
                    w = lambda j: par("convb_w", j * AC + m)
                    st = lambda j: par("state_b", (m * (CB - 1) + j) * DEC, DEC)
                    out, u = conv[:, m, :], t[0]
                    dve.wait_ge(cx_made, m + 1)
                    nc.vector.tensor_copy(cx_tail[:, m, :], u[:, SEQ - CB + 1:TOK]).then_inc(cx_ready, 1)
                    chained(nc.vector.tensor_scalar(out, u[:, :], w(CB - 1), None, ALU.mult))
                    for j in range(CB - 1):
                        back = CB - 1 - j
                        chained(nc.vector.scalar_tensor_tensor(out=out[:, SEQ:TOK], in0=st(j), scalar=w(j),
                                                               in1=out[:, SEQ:TOK], op0=ALU.mult, op1=ALU.add))
                        chained(nc.vector.scalar_tensor_tensor(out=out[:, back:SEQ], in0=u[:, 0:SEQ - back],
                                                               scalar=w(j), in1=out[:, back:SEQ],
                                                               op0=ALU.mult, op1=ALU.add))

                def decode(h):
                    if h == 0:
                        key_scores(2)
                    if h == 1:
                        key_scores(3)
                        wait_drained(dve, f"{s}.dec_s3")
                        chained(nc.vector.reduce_sum(dlf[:, PAST:PAST + 1], dtmp[:, :], AXX))
                        dve.wait_ge(lf_loaded, 16 * DEC * PAGES)
                        chained(nc.vector.memset(ds[:, :], 1.0))
                        chained(nc.vector.tensor_tensor_scan(dch[:, :], ds[:, :], dlf[:, :], 0.0, ALU.mult, ALU.add))
                    if h == 2:
                        name = f"{s}.dec_t"
                        wait_job(dve, name)
                        a = acc_of(name)
                        last = dch[:, PAST:PAST + 1]
                        chained(nc.vector.scalar_tensor_tensor(out=ds[:, 0:PAST], in0=a[0:BH, 0, 0:PAST], scalar=last,
                                                               in1=dch[:, 0:PAST], op0=ALU.add, op1=ALU.subtract))
                        drains(nc.vector.scalar_tensor_tensor(out=ds[:, PAST:PAST + 1], in0=a[0:BH, 1, 0:1],
                                                              scalar=last, in1=last, op0=ALU.add, op1=ALU.subtract),
                               name)
                        wait_drained(dve, name)
                        nc.vector.tensor_reduce(dnmx[:, :], ds[:, :], AXX, ALU.max, negate=True)\
                            .then_inc(dscores_ready, 1)
                        dve.wait_ge(dexp_ready, 1)
                        chained(nc.vector.reciprocal(dden[:, :], dden[:, :]))
                        chained(nc.vector.tensor_scalar(ds[:, :], ds[:, :], dden[:, 0:1], None, ALU.mult))
                        nc.vector.tensor_scalar(dsn[:, :], same_b, ds[:, PAST:PAST + 1], None, ALU.mult)\
                            .then_inc(dprobs_ready, 1)
                    if h == 3:
                        name = f"{s}.dec_p"
                        wait_job(dve, name)
                        a = acc_of(name)
                        chained(nc.vector.tensor_copy(pT[:, :], a[:, 0, 0:PAGES * BH]))
                        drains(nc.vector.tensor_tensor(onew[:, :, :], a[:, 1, 0:AC * DEC]
                                                       .rearrange("p (c b) -> p c b", c=AC),
                                                       v[:, :, SEQ:TOK], ALU.mult), name)
                        wait_drained(dve, name)
                    if h >= 4:
                        i = h - 4
                        name = f"{s}.dec_o{i}"
                        wait_job(dve, name)
                        n = DEC // STEPS
                        a = acc_of(name)[:, 0, 0:n * AC * 2].rearrange("p (b c r) -> p c b r", b=n, c=AC)
                        for r in range(2):
                            rows = slice(HD * r, HD * (r + 1))
                            ins = nc.vector.tensor_tensor(q[rows, :, SEQ + n * i:SEQ + n * (i + 1)], a[rows, :, :, r],
                                                          onew[rows, :, n * i:n * (i + 1)], ALU.add)
                            if r == 0:
                                chained(ins)
                        drains(ins, name)

                softmax(0)
                for h in range(HEADS):
                    if h < AC:
                        scaled(t[0][:, :], f"{s}.c{h}")
                        scaled(t[1][:, :], f"{s}.x{h}")
                    elif h < AC + AC // 2:
                        for m in (2 * (h - AC), 2 * (h - AC) + 1):
                            if m >= 2:
                                dve.wait_ge(bcx_ready, m - 1)
                            scaled(t[m % 2][:, :], f"{s}.b{m}")
                    for n in tiles_at(s, h):
                        done(n)
                    decode(h)
                    if h < AC:
                        short_conv(h)
                    if h == AC + AC // 2:
                        for c in range(AC):
                            dve.wait_ge(mixh_ready, c + 1)
                            nc.vector.tensor_tensor(act_lo[:, AC + c, :], conv[:, c, :],
                                                    act_hi[:, AC + c, :].bitcast(F32), ALU.subtract)\
                                .then_inc(mixl_ready, 1)
                    if h + 1 < HEADS:
                        softmax(h + 1)
                for c in range(AC):
                    dve.wait_ge(mixh_ready, AC + c + 1)
                    nc.vector.tensor_tensor(act_lo[:, c, :], q[:, c, :], act_hi[:, c, :].bitcast(F32), ALU.subtract)\
                        .then_inc(mixl_ready, 1)
                mixer_out(s)

            def recurrent(s):
                def conv_gates(c):
                    w = lambda j: par("convc_w", j * KC + c)
                    st = lambda j: par("state_c", (c * (CC - 1) + j) * DEC, DEC)
                    u, out = lru_v[:, c, :], xi[:, c, :]
                    wait_drained(dve, f"{s}.xr{c}")
                    chained(nc.vector.tensor_scalar(out, u, w(CC - 1), par("convc_b", c), ALU.mult, ALU.add))
                    for j in range(CC - 1):
                        back = CC - 1 - j
                        chained(nc.vector.scalar_tensor_tensor(out=out[:, SEQ:TOK], in0=st(j), scalar=w(j),
                                                               in1=out[:, SEQ:TOK], op0=ALU.mult, op1=ALU.add))
                        ins = nc.vector.scalar_tensor_tensor(out=out[:, back:SEQ], in0=u[:, 0:SEQ - back],
                                                             scalar=w(j), in1=out[:, back:SEQ],
                                                             op0=ALU.mult, op1=ALU.add)
                        if j < CC - 2:
                            chained(ins)
                    ins.then_inc(xc_ready, 1)

                def gates(c):
                    th, a2, ti = ysq[1], xsq[0], xsq[1]
                    dve.wait_ge(a2_ready, c + 1)
                    dve.wait_ge(tr_done, c + 1)
                    nc.vector.scalar_tensor_tensor(out=lru_v[:, c, :], in0=a2[:, :], scalar=1.0, in1=th[:, :],
                                                   op0=ALU.add, op1=ALU.mult).then_inc(v_ready, 1)
                    wait_drained(dve, f"{s}.i{c}")
                    nc.vector.scalar_tensor_tensor(out=xi[:, c, :], in0=ti[:, :], scalar=1.0, in1=xi[:, c, :],
                                                   op0=ALU.add, op1=ALU.mult).then_inc(xi_ready, 1)

                for kind, c in c_steps("vector"):
                    if kind == "drain":
                        scaled(lru_v[:, c, :], f"{s}.xr{c}")
                    elif kind == "conv":
                        conv_gates(c)
                    elif kind == "refill":
                        done(f"{s}.{c}")
                    elif kind == "gates":
                        gates(c)
                        done(f"{s}.i{c}")
                    else:
                        scaled(gt[:, c, :], f"{s}.gt{c}")
                        done(f"{s}.gt{c}")

                def mixed_lo(c):
                    dve.wait_ge(hg_ready, c + 1)
                    dve.wait_ge(mixh_ready, KC + c + 1)
                    nc.vector.tensor_tensor(mixed_of(c, xc_lo, act_lo), t[c % 2][:, :],
                                            mixed_of(c, xc_hi, act_hi).bitcast(F32), ALU.subtract)\
                        .then_inc(mixl_ready, 1)

                dve.wait_ge(xi_ready, KC)
                for c in range(KC):
                    dve.wait_ge(root_ready, c + 1)
                    chained(nc.vector.tensor_tensor(lru_v[:, c, :], lru_v[:, c, :], xi[:, c, :], ALU.mult))
                h0 = par("h0", 0, KC * DEC).rearrange("p (c b) -> p c b", c=KC)
                last = xi[:, :, SEQ:TOK]
                dve.wait_ge(a_done, KC)
                chained(nc.vector.tensor_tensor(last, lru_a[:, :, SEQ:TOK], h0, ALU.mult))
                nc.vector.tensor_tensor(last, last, lru_v[:, :, SEQ:TOK], ALU.add).then_inc(hs_ready, 1)
                for c in range(KC):
                    nc.vector.tensor_tensor_scan(xi[:, c, 0:SEQ], lru_a[:, c, 0:SEQ], lru_v[:, c, 0:SEQ], 0.0,
                                                 ALU.mult, ALU.add).then_inc(hs_ready, 1)
                    dve.wait_ge(hs_ready, c + 2)
                    dve.wait_ge(gelu_ready, c + 1)
                    if c >= 2:
                        dve.wait_ge(mixl_ready, KC + c - 1)
                        dve.wait_ge(mixh_ready, KC + c - 1)
                    nc.vector.tensor_tensor(t[c % 2][:, :], gt[:, c, :], xi[:, c, :], ALU.mult).then_inc(hg_ready, 1)
                    if c:
                        mixed_lo(c - 1)
                    if c < 4:
                        scaled(gt[:, c + 4, :], f"{s}.gt{c + 4}")
                        done(f"{s}.gt{c + 4}")
                mixed_lo(KC - 1)
                dve.wait_ge(stored, 16 * 8)
                mixer_out(s)

            def ple(s):
                n = KC * (s // 4)

                def embedding(m):
                    name = f"{s}.pe{m}"
                    wait_job(dve, name)
                    dve.wait_ge(sig_ready, n + m + 1)
                    ins = nc.vector.tensor_tensor(two(t[m % 2][:, :]), tile_of(J[name]), two(sig[:, m, :]), ALU.mult)
                    drains(ins, name)
                    wait_drained(dve, name)
                    nc.vector.tensor_tensor(x[:, m, :], x[:, m, :], t[m % 2][:, :], ALU.add).then_inc(ple_x, 1)
                for m in range(KC):
                    if m == 0:
                        dve.wait_ge(ph_ready, s // 4 + 1)
                        nc.vector.tensor_tensor(p_lo[:, :, :], p_raw[:, :, :], p_hi[:, :, :].bitcast(F32),
                                                ALU.subtract).then_inc(pl_ready, 1)
                    scaled(sig[:, m, :], f"{s}.gate{m}")
                    done(f"{s}.gate{m}")
                    if m % 4 == 3:
                        for c in range(m - 3, m + 1):
                            if m == KC - 1 and s + 1 < SUBS:
                                low(s + 1, c - 4)
                            embedding(c)
                        done(f"{s}.pe{m}")

            for s in range(SUBS):
                begin(s)
                {S_AB: attention, S_C: recurrent}.get(s, ffn if IS_FFN(s) else ple)(s)

        @block.tensor
        def _(pe):
            def claim(j, turn=None):
                if turn is not None:
                    pe.wait_ge(drained[j % ACCS], turn)
                elif j >= ACCS:
                    pe.wait_ge(drained[j % ACCS], j // ACCS)
                return acc[j % ACCS]

            def chunk(a, slot, at, hi, lo, first, last, width=P):
                for n, (w, m) in enumerate(((w_hi, hi), (w_hi, lo), (w_lo, hi))):
                    for half in range(2):
                        ins = nc.tensor.matmul(a[0:width, half, 0:HALF], w[slot][:, at:at + width],
                                               m[:, half * HALF:(half + 1) * HALF],
                                               start=first and n == 0, stop=last and n == 2)
                return ins

            def parts(hi, lo):
                return lambda c: (hi[:, c, :], lo[:, c, :])

            act_in = parts(act_hi, act_lo)

            def tile(j, slot, ks, at, inp, turn=None, wait=None, width=P):
                a = claim(j, turn)
                for c in range(ks):
                    if wait is not None:
                        wait(c)
                    ins = chunk(a, slot, at(c), *inp(c), c == 0, c == ks - 1, width)
                ins.then_inc(acc_ready, 1)

            def wait_unit(n):
                pe.wait_ge(lo_ready, n + 1)

            def pair(s, names, unit, ks=KC, tiles=2, inp=None):
                n = U[f"{s}.{unit}"]
                wait_unit(n)
                for i, name in enumerate(names):
                    tile(J[f"{s}.{name}"], n % 2, ks, lambda c: (c * tiles + i) * P, inp or act_in)

            def k_outer(jobs, units, inp, wait_hi, wait_lo, chunks=range(KC), before_last=lambda: None):
                accs = [claim(j) for j in jobs]

                def product(n, c, w, part, start, stop):
                    unit = units[n // 2]
                    at = (2 * c + n % 2) * P
                    for half in range(2):
                        ins = nc.tensor.matmul(accs[n][:, half, 0:HALF], w[unit % 2][:, at:at + P],
                                               part[:, half * HALF:(half + 1) * HALF], start=start, stop=stop)
                    return ins

                for c in chunks:
                    if c == chunks[-1]:
                        before_last()
                    hi, lo = inp(c)
                    wait_hi(c)
                    for n in range(len(jobs)):
                        if c == chunks[0] and n % 2 == 0:
                            wait_unit(units[n // 2])
                        product(n, c, w_hi, hi, c == chunks[0], False)
                        product(n, c, w_lo, hi, False, False)
                    wait_lo(c)
                    for n in range(len(jobs)):
                        ins = product(n, c, w_hi, lo, False, c == chunks[-1])
                        if c == chunks[-1]:
                            ins.then_inc(acc_ready, 1)

            def mean(name, squares_of, start=True, stop=True):
                a = claim(J[name]) if start else acc_of(name)
                for half in range(2):
                    ins = nc.tensor.matmul(a[:, half, 0:HALF], mean_of[:, :],
                                           squares_of[:, half * HALF:(half + 1) * HALF], start=start, stop=stop)
                if stop:
                    ins.then_inc(acc_ready, 1)

            def begin(s, tiles, units):
                if s % 4:
                    n = POSTS.index(s) + 1
                    pe.wait_ge(ysum_added, (KC - 1) * n)
                    mean(f"{s}.post", ysum, stop=False)
                    pe.wait_ge(ysq_ready, KC * n)
                    mean(f"{s}.post", ysq[1], start=False)
                un = [U[f"{s}.{u}"] for u in units]

                def pre():
                    pe.wait_ge(xsum_added, (KC - 1) * (s + 1))
                    mean(f"{s}.pre", xsum)
                k_outer([J[f"{s}.{n}"] for n in tiles[0:3]], un, act_in,
                        lambda c: pe.wait_ge(acth_ready, KC * s + c + 1),
                        lambda c: pe.wait_ge(actl_ready, KC * s + c + 1), before_last=pre)
                tile(J[f"{s}.{tiles[3]}"], un[1] % 2, KC, lambda c: (2 * c + 1) * P, act_in)

            def ffn(s):
                begin(s, ["g0", "u0", "g1", "u1"], ["in0", "in1"])
                tile0 = FT * (s // 2)
                k0 = 0
                for half in range(2):
                    first = 2 if half == 0 else 0
                    j0 = k0 + first
                    base, unit = J[f"{s}.g{j0}"], U[f"{s}.in{j0}"]
                    with pe.Fori(0, (HID[half] - first) // 2) as i:
                        for e in range(2):
                            pe.wait_ge(lo_ready, 2 * i + (unit + e + 1))
                            for n in range(2):
                                j = base + 2 * e + n
                                tile(j, (unit + e) % 2, KC, lambda c: (2 * c + n) * P, act_in,
                                     turn=i + j // ACCS)
                    tag = "ab"[half]
                    base, unit = J[f"{s}.out{tag}0"], U[f"{s}.out{tag}0"]
                    with pe.Fori(0, KC // 4) as i:
                        for e in range(4):
                            pe.wait_ge(lo_ready, 4 * i + (unit + e + 1))
                            wait = (lambda c: pe.wait_ge(hidl_ready, tile0 + k0 + c + 1)) if e == 0 else None
                            tile(base + e, (unit + e) % 2, HID[half], lambda c: c * P, parts(hid_hi, hid_lo),
                                 turn=i + (base + e) // ACCS, wait=wait)
                    k0 += HID[half]

            def mixer_out(s, n0, chunks=range(KC), inp=act_in):
                un = [U[f"{s}.out0"], U[f"{s}.out2"]]
                k_outer([J[f"{s}.out{m}"] for m in range(3)], un, inp,
                        lambda c: pe.wait_ge(mixh_ready, n0 + list(chunks).index(c) + 1),
                        lambda c: pe.wait_ge(mixl_ready, n0 + list(chunks).index(c) + 1), chunks)
                tile(J[f"{s}.out3"], un[1] % 2, KC, lambda c: (2 * c + 1) * P, inp)
                for m in (4, 6):
                    pair(s, [f"out{m}", f"out{m + 1}"], f"out{m}", inp=inp)

            def attention(s):
                begin(s, ["q0", "q1", "q2", "q3"], ["q0", "q2"])
                n = U[f"{s}.f"]
                wait_unit(n)
                tile(J[f"{s}.f"], n % 2, KC, lambda c: c * HEADS, act_in, width=HEADS)
                for m in (0, 2):
                    pair(s, [f"k{m}", f"k{m + 1}"], f"k{m}")

                def key_scores(i):
                    a = claim(J[f"{s}.dec_s{i}"])
                    pe.wait_ge(ring_loaded, 16 * RING * (i + 1))
                    for r in range(RING):
                        b, g = divmod(i * RING + r, PAGES)
                        for c in range(AC):
                            at = g * BH + b * HEADS + 2 * c
                            ins = nc.tensor.matmul(a[:, 0, at:at + 2], ring[:, r, c * P:(c + 1) * P],
                                                   qbd[:, b, c, :], start=True, stop=True)
                    if i == STEPS - 1:
                        ins = nc.tensor.matmul(a[0:BH, 1, 0:DEC], to_bh, logf[:, SEQ:TOK], start=True, stop=True)
                    ins.then_inc(acc_ready, 1)

                for m in (0, 2):
                    pair(s, [f"v{m}", f"v{m + 1}"], f"v{m}")
                    if m == 0:
                        pe.wait_ge(in_const, 16)
                        pe.wait_ge(qbd_ready, 2)
                    key_scores(m // 2)
                for m in range(AC):
                    wait_drained(pe, f"{s}.v{m}")
                    wait_drained(pe, f"{s}.q{m}")
                    wait_drained(pe, f"{s}.k{m}")
                for kb in (0, 2):
                    a = claim(J[f"{s}.vt{kb}"])
                    for n in range(2):
                        for m in range(AC):
                            ins = nc.tensor.transpose(a[:, n, m * P:(m + 1) * P],
                                                      v[:, m, (kb + n) * P:(kb + n + 1) * P], ident)
                    ins.then_inc(acc_ready, 1)
                pe.wait_ge(f_ch, 1)
                a = claim(J[f"{s}.cq"])
                for qb in range(QB):
                    ins = nc.tensor.transpose(a[:, 0, qb * HEADS:(qb + 1) * HEADS], ch[:, qb * P:(qb + 1) * P],
                                              const[0:HEADS, IDENT:IDENT + HEADS])
                ins.then_inc(acc_ready, 1)

                def scores(h):
                    a = claim(J[f"{s}.ck{h}"])
                    nc.tensor.matmul(a[:, 0, :], const[0:HEADS, IDENT + h:IDENT + h + 1].broadcast_to([HEADS, P]),
                                     ch[:, :], start=True, stop=True).then_inc(acc_ready, 1)
                    rows = slice(HD * (h % 2), HD * (h % 2) + HD)
                    for qb in range(QB):
                        if qb % 2 == 0:
                            a = claim(J[f"{s}.s{h}.{qb}"])
                        ins = nc.tensor.matmul(a[:, qb % 2, 0:(qb + 1) * P], q[rows, h // 2, qb * P:(qb + 1) * P],
                                               k[rows, h // 2, 0:(qb + 1) * P], start=True, stop=True)
                        if qb % 2:
                            ins.then_inc(acc_ready, 1)

                def decode(h):
                    if h < 2:
                        key_scores(2 + h)
                    if h == 2:
                        a = claim(J[f"{s}.dec_t"])
                        for i in range(STEPS):
                            wait_drained(pe, f"{s}.dec_s{i}")
                        for g in range(PAGES):
                            nc.tensor.transpose(a[0:BH, 0, g * PAGE:(g + 1) * PAGE], sT[:, g * BH:(g + 1) * BH], ident)
                        pe.wait_ge(kqbd_ready, 2)
                        nc.tensor.matmul(a[0:BH, 1, 0:1], kqbd[:, :, :, :].rearrange("p b c r -> p (b c r)"), one[:, :],
                                         start=True, stop=True).then_inc(acc_ready, 1)
                    if h == 3:
                        a = claim(J[f"{s}.dec_p"])
                        pe.wait_ge(dprobs_ready, 1)
                        for g in range(PAGES):
                            nc.tensor.transpose(a[:, 0, g * BH:(g + 1) * BH], ds[:, g * PAGE:(g + 1) * PAGE],
                                                const[0:BH, IDENT:IDENT + BH])
                        for c in range(AC):
                            ins = nc.tensor.matmul(a[:, 1, c * DEC:(c + 1) * DEC], to_rows[:, c * P:(c + 1) * P],
                                                   dsn[:, :], start=True, stop=True)
                        ins.then_inc(acc_ready, 1)
                    if h >= 4:
                        i = h - 4
                        a = claim(J[f"{s}.dec_o{i}"])
                        wait_drained(pe, f"{s}.dec_p")
                        pe.wait_ge(ring_loaded, 16 * RING * (STEPS + i + 1))
                        for r in range(0, RING, PAGES):
                            b = (i * RING + r) // PAGES
                            for c in range(AC):
                                at = (r // PAGES * AC + c) * 2
                                for g in range(PAGES):
                                    src = g * BH + b * HEADS + 2 * c
                                    ins = nc.tensor.matmul(a[:, 0, at:at + 2], ring[:, r + g, c * P:(c + 1) * P],
                                                           pT[:, src:src + 2], start=g == 0, stop=g == PAGES - 1)
                        ins.then_inc(acc_ready, 1)

                scores(0)
                for h in range(HEADS):
                    if h < AC:
                        pair(s, [f"c{h}", f"x{h}"], f"cx{h}")
                    elif h < AC + AC // 2:
                        m = 2 * (h - AC)
                        pair(s, [f"b{m}", f"b{m + 1}"], f"b{m}")
                    decode(h)
                    pe.wait_ge(probs_ready, QB * (h + 1))
                    for kb in range(QB):
                        if kb % 2 == 0:
                            a = claim(J[f"{s}.pt{h}.{kb}"])
                        for qb in range(kb, QB):
                            ins = nc.tensor.transpose(a[:, kb % 2, qb * P:(qb + 1) * P],
                                                      sc[:, qb, kb * P:(kb + 1) * P], ident)
                        if kb % 2:
                            ins.then_inc(acc_ready, 1)
                    if h + 1 < HEADS:
                        scores(h + 1)
                    a = claim(J[f"{s}.pv{h}"])
                    wait_drained(pe, f"{s}.pt{h}.0")
                    wait_drained(pe, f"{s}.pt{h}.2")
                    if h == 0:
                        wait_drained(pe, f"{s}.vt0")
                        wait_drained(pe, f"{s}.vt2")
                    r = HD * (h % 2)
                    for kb in range(QB):
                        ins = nc.tensor.matmul(a[r:r + HD, 0, kb * P:SEQ], v_tok[:, kb, h * HD:(h + 1) * HD],
                                               pt[:, kb, kb * P:SEQ], start=kb == 0, stop=kb == QB - 1)
                    ins.then_inc(acc_ready, 1)
                mixer_out(s, 0, [*range(AC, KC), *range(AC)])

            def recurrent(s):
                begin(s, ["xr0", "xr1", "xr2", "xr3"], ["xr0", "xr2"])

                def gates(m):
                    n = U[f"{s}.ri{m}"]
                    wait_unit(n)
                    for c in (m, m + 1):
                        pe.wait_ge(xcl_ready, c + 1)
                        for i, kind in enumerate("ri"):
                            j = J[f"{s}.{kind}{c}"]
                            a = claim(j)
                            chunk(a, n % 2, (2 * (c - m) + i) * P, xc_hi[:, c % 4, :], xc_lo[:, c % 4, :], True, True)\
                                .then_inc(acc_ready, 1)

                pair(s, ["gt0", "gt1"], "gt0")
                gates(0)
                for m in (4, 6):
                    pair(s, [f"xr{m}", f"xr{m + 1}"], f"xr{m}")
                    gates(m - 2)
                pair(s, ["gt2", "gt3"], "gt2")
                gates(6)
                for m in (4, 6):
                    pair(s, [f"gt{m}", f"gt{m + 1}"], f"gt{m}")
                mixer_out(s, KC, inp=lambda c: (mixed_of(c, xc_hi, act_hi), mixed_of(c, xc_lo, act_lo)))

            def ple(s):
                begin(s, ["gate0", "gate1", "gate2", "gate3"], ["gate0", "gate2"])
                for m in (0, 4):
                    if m:
                        pair(s, ["gate4", "gate5"], "gate4")
                        pair(s, ["gate6", "gate7"], "gate6")
                    pe.wait_ge(pl_ready, s // 4 + 1)
                    pair(s, [f"pe{n}" for n in range(m, m + 4)], f"pe{m}", ks=PLE_K, tiles=4, inp=parts(p_hi, p_lo))

            pe.wait_ge(consts_made, 3)
            for s in range(SUBS):
                {S_AB: attention, S_C: recurrent}.get(s, ffn if IS_FFN(s) else ple)(s)


def tiles_at(s, h):
    if h < AC:
        return [f"{s}.c{h}", f"{s}.x{h}"]
    if h < AC + AC // 2:
        return [f"{s}.b{2 * (h - AC)}", f"{s}.b{2 * (h - AC) + 1}"]
    return []


def c_steps(engine):
    vector = engine == "vector"
    steps = [("drain", 0), ("drain", 1), ("drain", 2), ("refill", "xr1"), ("conv", 0), ("drain", 3),
             ("refill", "xr3"), ("conv", 1), ("gt", 0)]
    steps += [("conv", 2), ("gt", 1), ("conv", 3), ("gates", 0), ("gates", 1)] if vector else \
        [("gt", 1), ("gates", 0), ("conv", 2), ("gates", 1), ("conv", 3)]
    for m in (4, 6):
        steps += [("drain", m), ("conv", m), ("drain", m + 1), ("refill", f"xr{m + 1}")] if vector else \
            [("refill", f"xr{m + 1}"), ("conv", m)]
        gates = [("gates", m - 2), ("gates", m - 1)]
        steps += [("conv", m + 1), *gates] if vector else [*gates, ("conv", m + 1)]
    return steps + [("gt", 2), ("gt", 3), ("gates", 6), ("gates", 7)]


def kernel(**inputs):
    import concourse.bacc as bacc
    from concourse.bass_utils import run_bass_kernel_spmd

    a = {name: np.asarray(value) for name, value in inputs.items()}
    f32 = np.float32

    def feature_major(m):
        return m.T.reshape(m.shape[1] // P, P, m.shape[0]).transpose(1, 0, 2)

    def by_chunk(m):
        lead = m.shape[:-1]
        return np.moveaxis(m.reshape(*lead, m.shape[-1] // P, P), -1, 0)

    ri = np.stack([a["c_w_rg"][0], a["c_w_ig"][0]], axis=1)
    a["c_w_ri"] = ri.transpose(2, 0, 1, 3).reshape(1, P, 2 * D)
    stream = np.empty(PLAN.size, f32)
    for _, at, size, (array, layer, k0, ks, ranges) in PLAN.units:
        w = a[array][layer][k0 * P:(k0 + ks) * P]
        w = np.concatenate([w[:, lo:hi] for lo, hi in ranges], axis=1)
        stream[at:at + P * size] = w.reshape(ks, P, -1).transpose(1, 0, 2).reshape(-1)

    blocks = {
        "norm": by_chunk(a["norms"]),
        "bf": np.concatenate([a["ab_b_f"][0], np.zeros(P - HEADS, f32)]),
        "convb_w": by_chunk(a["ab_conv_w"][0]), "convc_w": by_chunk(a["c_conv_w"][0]),
        "convc_b": by_chunk(a["c_conv_b"][0]), "b_rg": by_chunk(a["c_b_rg"][0]),
        "b_ig": by_chunk(a["c_b_ig"][0]), "lam": by_chunk(a["c_lam"][0]),
        "state_b": by_chunk(a["state_conv_b"][:, 0]).transpose(0, 3, 2, 1),
        "state_c": by_chunk(a["state_conv_c"][:, 0]).transpose(0, 3, 2, 1),
        "h0": by_chunk(a["state_h_c"][:, 0]).transpose(0, 2, 1),
    }
    params = np.concatenate([blocks[n].reshape(P, -1) for n in PARAMS], axis=1)

    const = np.zeros((P, N_CONST), f32)
    const[:, IDENT:IDENT + P] = np.eye(P)
    const[:, MASK:MASK + P] = np.triu(np.full((P, P), NEG), 1)
    const[0:BH, SAME_B:SAME_B + DEC] = np.repeat(np.eye(DEC), HEADS, axis=0)
    const[0:HEADS, TO_BH:TO_BH + BH] = np.tile(np.eye(HEADS), (1, DEC))
    const[0:BH, TO_ROWS:TO_ROWS + AC * P] = np.tile(np.repeat(np.eye(HEADS), HD, axis=1), (DEC, 1))

    tokens = np.concatenate([a["x_prompt"][0], a["x_sample"][:, 0]])
    p = np.stack([feature_major(np.concatenate([a["p_prompt"][i, 0], a["p_sample"][i, :, 0]])) for i in range(DEPTH)])
    pages = a["cache_k"].shape[0]
    k_pages = a["cache_k"][:, 0].reshape(pages, PAGE, AC, P).transpose(0, 3, 2, 1).reshape(pages, P, D_A)
    v_pages = a["cache_v"][:, 0].reshape(pages, PAGE, D_A)
    lf_pages = a["cache_logf"][:, 0].transpose(0, 2, 1)
    host = {"weights": stream, "params": params, "const": const, "x": feature_major(tokens), "p": p,
            "k_pages": k_pages, "v_pages": v_pages, "lf_pages": lf_pages,
            "table": a["page_table"].reshape(1, DEC * PAGES)}
    outs = {"y": (P, KC, TOK), "k": (P, AC, TOK), "v": (P, AC, TOK), "logf": (HEADS, TOK),
            "cx": (P, AC, CB - 1 + DEC), "cb_state": (P, AC, DEC),
            "xr": (P, KC, CC - 1 + DEC), "cc_state": (P, KC, (CC - 2) * DEC), "h": (P, KC, 1 + DEC)}

    nc = bacc.Bacc("TRN2", target_bir_lowering=False, num_devices=1)
    arrays, args = {}, []
    for name, value in host.items():
        value = np.ascontiguousarray(value)
        arrays[f"in_{name}"] = value
        args.append(nc.dram_tensor(f"in_{name}", value.shape, mybir.dt.from_np(value.dtype), kind="ExternalInput").ap())
    for name, shape in outs.items():
        args.append(nc.dram_tensor(f"out_{name}", shape, F32, kind="ExternalOutput").ap())
    trunk(nc, *args)
    r = run_bass_kernel_spmd(nc, [arrays], core_ids=[0]).results[0]
    o = {name: np.asarray(r[f"out_{name}"]) for name in outs}

    def tokens_of(m):
        return m.transpose(2, 1, 0).reshape(m.shape[2], -1)

    y, k, v = (tokens_of(o[n]) for n in "ykv")
    logf, cx, xr, h = o["logf"].T, tokens_of(o["cx"]), tokens_of(o["xr"]), tokens_of(o["h"])
    heads = lambda m: m.reshape(m.shape[0], HEADS, HD)
    cb0 = tokens_of(o["cb_state"])
    cc0 = o["cc_state"].reshape(P, KC, CC - 2, DEC).transpose(3, 2, 1, 0).reshape(DEC, CC - 2, D)
    return (
        y[None, :SEQ], y[SEQ:, None],
        heads(k[:SEQ])[None, None], heads(v[:SEQ])[None, None], logf[None, None, :SEQ],
        heads(k[SEQ:])[:, None, None], heads(v[SEQ:])[:, None, None], logf[SEQ:][:, None, None],
        cx[None, None, :CB - 1], np.stack([cb0, cx[CB - 1:]], axis=1)[:, None],
        xr[None, None, :CC - 1], np.concatenate([cc0, xr[CC - 1:][:, None]], axis=1)[:, None],
        h[None, None, 0], h[1:][:, None],
    )
```

```python
import math
from contextlib import ExitStack

import numpy as np
import concourse.bass as bass
from concourse import mybir

F32 = mybir.dt.float32
F32R = mybir.dt.float32r
I32 = mybir.dt.int32
ALU = mybir.AluOpType
ACT = mybir.ActivationFunctionType
AXX = mybir.AxisListType.X

P = 128
D = 1024
KC = D // P
SEQ, DEC = 512, 8
TOK = SEQ + DEC
HALF = TOK // 2
DEPTH = 2
D_FF = 2816
FT = D_FF // P
HID = (12, FT - 12)
HEADS, HD = 8, 64
AC = HEADS * HD // P
D_A = HEADS * HD
CB, CC = 3, 4
LRU_C = 8.0
PLE_K = 256 // P
PAGES, PAGE = 2, 128
PAST = PAGES * PAGE
BH = DEC * HEADS
NN = 7
EPS = 1e-6
NEG = -1e30
QB = SEQ // P
ACCS = 4
UNIT = 2048
RING = 4
STEPS = DEC * PAGES // RING

PARAMS = {}
_at = 0
for _name, _n in (("norm", DEPTH * NN * KC), ("bf", 1), ("convb_w", CB * AC), ("convc_w", CC * KC),
                  ("convc_b", KC), ("b_rg", KC), ("b_ig", KC), ("lam", KC),
                  ("state_b", AC * (CB - 1) * DEC), ("state_c", KC * (CC - 1) * DEC), ("h0", KC * DEC)):
    PARAMS[_name] = (_at, _n)
    _at += _n
N_PARAMS = _at
IDENT, MASK, SAME_B, TO_BH, TO_ROWS = 0, P, 2 * P, 2 * P + DEC, 2 * P + DEC + BH
N_CONST = TO_ROWS + AC * P


def decode_step(h):
    return ["dec_s2", "dec_s3", "dec_t", "dec_p", "dec_o0", "dec_o1", "dec_o2", "dec_o3"][h]


B_TILES = {4: [0, 1], 5: [2], 6: [3]}
MIX_HEAD = 7


class Plan:

    def __init__(self):
        self.job, self.units, self.unit, self.last_of, self.size = {}, [], {}, {}, 0

    def add_job(self, name, unit=None):
        self.job[name] = len(self.job)
        if unit is not None:
            self.last_of[unit] = name

    def add_unit(self, name, what):
        size = what[3] * sum(b - a for a, b in what[4])
        self.unit[name] = len(self.units)
        self.units.append((name, self.size, size, what))
        self.size += P * size

    def refills(self):
        return {job: self.unit[u] + 2 for u, job in self.last_of.items() if self.unit[u] + 2 < len(self.units)}


def col(i, n=1):
    return (i * P, (i + n) * P)


def make_plan():
    pl = Plan()

    def first_group(s, tiles, units):
        pl.add_job(f"{s}.pre")
        for n in range(3):
            pl.add_job(f"{s}.{tiles[n]}", units[n // 2])
        pl.add_job(f"{s}.{tiles[3]}", units[1])

    def out_tiles(s, what, k, ks, tag=""):
        for m in range(KC):
            pl.add_unit(f"{s}.out{tag}{m}", (*what, k, ks, [col(m)]))
            pl.add_job(f"{s}.out{tag}{m}", f"{s}.out{tag}{m}")

    def out_pairs(s, what):
        for m in range(0, KC, 2):
            pl.add_unit(f"{s}.out{m}", (*what, 0, KC, [col(m, 2)]))
            pl.add_job(f"{s}.out{m}", f"{s}.out{m}")
            pl.add_job(f"{s}.out{m + 1}", f"{s}.out{m}")

    def ffn(s, name, layer):
        if s % 4:
            pl.add_job(f"{s}.post")
        for half, k0 in enumerate((0, HID[0])):
            for j in range(k0, k0 + HID[half]):
                pl.add_unit(f"{s}.in{j}", (name + "_wi", layer, 0, KC, [col(j), col(FT + j)]))
            if half == 0:
                first_group(s, ["g0", "u0", "g1", "u1"], [f"{s}.in0", f"{s}.in1"])
            for j in range(k0 + 2 * (half == 0), k0 + HID[half]):
                pl.add_job(f"{s}.g{j}", f"{s}.in{j}")
                pl.add_job(f"{s}.u{j}", f"{s}.in{j}")
            out_tiles(s, (name + "_wo", layer), k0, HID[half], "ab"[half])

    def ple(s, layer):
        pl.add_job(f"{s}.post")
        gate = lambda m: (f"{s}.gate{m}", ("ple_w_pg", layer, 0, KC, [col(m, 2)]))
        embed = lambda m: (f"{s}.pe{m}", ("ple_w_pe", layer, 0, PLE_K, [col(m, 4)]))
        for m in (0, 4):
            pl.add_unit(*gate(m))
            pl.add_unit(*gate(m + 2))
            pl.add_unit(*embed(m))
            if m == 0:
                first_group(s, ["gate0", "gate1", "gate2", "gate3"], [f"{s}.gate0", f"{s}.gate2"])
            else:
                for n in range(m, m + 4):
                    pl.add_job(f"{s}.gate{n}", f"{s}.gate{n // 2 * 2}")
            for n in range(m, m + 4):
                pl.add_job(f"{s}.pe{n}", f"{s}.pe{m}")

    def ab(s):
        w = ("ab_w_in", 0, 0, KC)
        f0 = 3 * D_A
        gate0, c0, x0 = (f0 + HEADS + n * D_A for n in range(3))
        tile = lambda at, m, n=1: (at + m * P, at + (m + n) * P)
        pl.add_job(f"{s}.post")
        for m in (0, 2):
            pl.add_unit(f"{s}.q{m}", (*w, [tile(0, m, 2)]))
        first_group(s, ["q0", "q1", "q2", "q3"], [f"{s}.q0", f"{s}.q2"])
        pl.add_unit(f"{s}.f", (*w, [(f0, f0 + HEADS)]))
        pl.add_job(f"{s}.f", f"{s}.f")
        for m in (0, 2):
            pl.add_unit(f"{s}.k{m}", (*w, [tile(D_A, m, 2)]))
            pl.add_job(f"{s}.k{m}", f"{s}.k{m}")
            pl.add_job(f"{s}.k{m + 1}", f"{s}.k{m}")
        for m in (0, 2):
            pl.add_unit(f"{s}.v{m}", (*w, [tile(2 * D_A, m, 2)]))
            pl.add_job(f"{s}.v{m}", f"{s}.v{m}")
            pl.add_job(f"{s}.v{m + 1}", f"{s}.v{m}")
            pl.add_job(f"{s}.dec_s{m // 2}")
        for j in ("vt0", "vt2", "cq", "ck0", "s0.0", "s0.2"):
            pl.add_job(f"{s}.{j}")
        for h in range(HEADS):
            if h < AC:
                pl.add_unit(f"{s}.cx{h}", (*w, [tile(c0, h), tile(x0, h)]))
                pl.add_job(f"{s}.c{h}", f"{s}.cx{h}")
                pl.add_job(f"{s}.x{h}", f"{s}.cx{h}")
            for m in B_TILES.get(h, []):
                if m % 2 == 0:
                    pl.add_unit(f"{s}.b{m}", (*w, [tile(gate0, m, 2)]))
                pl.add_job(f"{s}.b{m}", f"{s}.b{m // 2 * 2}")
            pl.add_job(f"{s}.{decode_step(h)}")
            pl.add_job(f"{s}.pt{h}.0")
            pl.add_job(f"{s}.pt{h}.2")
            if h + 1 < HEADS:
                for j in (f"ck{h + 1}", f"s{h + 1}.0", f"s{h + 1}.2"):
                    pl.add_job(f"{s}.{j}")
            pl.add_job(f"{s}.pv{h}")
        out_pairs(s, ("ab_w_out", 0))

    def cm(s):
        pl.add_job(f"{s}.post")
        xr = lambda m: pl.add_unit(f"{s}.xr{m}", ("c_w_in", 0, 0, KC, [(D + m * P, D + (m + 2) * P)]))

        def pair(kind, m):
            pl.add_job(f"{s}.{kind}{m}", f"{s}.{kind}{m}")
            pl.add_job(f"{s}.{kind}{m + 1}", f"{s}.{kind}{m}")

        def gates(m):
            pl.add_unit(f"{s}.ri{m}", ("c_w_ri", 0, 0, 1, [col(2 * m, 4)]))
            for n in (m, m + 1):
                pl.add_job(f"{s}.r{n}", f"{s}.ri{m}")
                pl.add_job(f"{s}.i{n}", f"{s}.ri{m}")

        def gate(m):
            pl.add_unit(f"{s}.gt{m}", ("c_w_in", 0, 0, KC, [col(m, 2)]))
            pair("gt", m)

        xr(0)
        xr(2)
        first_group(s, ["xr0", "xr1", "xr2", "xr3"], [f"{s}.xr0", f"{s}.xr2"])
        gate(0)
        gates(0)
        for m in (4, 6):
            xr(m)
            pair("xr", m)
            gates(m - 2)
        gate(2)
        gates(6)
        for m in (4, 6):
            gate(m)
        out_pairs(s, ("c_w_out", 0))

    for layer in range(DEPTH):
        ffn(4 * layer, "ffn1", layer)
        (ab if layer % 2 == 0 else cm)(4 * layer + 1)
        ffn(4 * layer + 2, "ffn2", layer)
        ple(4 * layer + 3, layer)
    return pl


PLAN = make_plan()
SUBS = 4 * DEPTH
POSTS = [s for s in range(SUBS) if s % 4]
IS_FFN = lambda s: s % 2 == 0
S_AB, S_C = 1, 5


def trunk(nc, weights, params_d, const_d, x_d, p_d, kpages_d, vpages_d, lfpages_d, table_d,
          y_o, k_o, v_o, logf_o, cx_o, cbstate_o, xr_o, ccstate_o, h_o):
    J, U = PLAN.job, PLAN.unit
    REFILL = PLAN.refills()
    n_units = len(PLAN.units)
    last_job = [J[PLAN.last_of[name]] for name, *_ in PLAN.units]

    ctx = ExitStack()
    with ctx:
        def sb(name, shape, dt=F32):
            return ctx.enter_context(nc.sbuf_tensor(name, shape, dt))

        def sem(name):
            return ctx.enter_context(nc.semaphore(name))

        def overlay(*groups):
            made, most = [], 0
            for group in groups:
                with ExitStack() as own:
                    made += [own.enter_context(nc.sbuf_tensor(n, s, dt)) for n, s, dt in group]
                    most = max(most, sum(4 * math.prod(s[1:]) for _, s, _ in group))
            sb("under_" + groups[0][0][0], [P, (most + 63) // 4])
            return made

        x = sb("x", [P, KC, TOK])
        act_hi = sb("act_hi", [P, KC, TOK], F32R)
        act_lo = sb("act_lo", [P, KC, TOK], F32R)
        raw = [sb(f"raw{i}", [P, UNIT]) for i in range(2)]
        w_hi = [sb(f"w_hi{i}", [P, UNIT], F32R) for i in range(2)]
        w_lo = [sb(f"w_lo{i}", [P, UNIT], F32R) for i in range(2)]
        params = sb("params", [P, N_PARAMS])
        half_norm = sb("half_norm", [P, DEPTH * NN * KC])
        const = sb("const", [P, N_CONST])
        mean_of = sb("mean_of", [P, P])
        one = sb("one", [P, 1])
        eps = sb("eps", [P, 1])
        table_use = sb("table_use", [P, 1])
        rs_pre = sb("rs_pre", [P, TOK])
        rs_post = sb("rs_post", [P, TOK])
        xsum = sb("xsum", [P, TOK])
        ysum = sb("ysum", [P, TOK])
        xsq = [sb(f"xsq{i}", [P, TOK]) for i in range(2)]
        ysq = [sb(f"ysq{i}", [P, TOK]) for i in range(2)]
        t = [sb(f"t{i}", [P, TOK]) for i in range(2)]
        lru = sb("lru", [P, 4 * KC])
        xr_tail = sb("xr_tail", [P, KC, CC - 1 + DEC])
        y, ring, v_tok, xi = overlay(
            [("y", [P, KC, TOK], F32)],
            [("ring", [P, RING, D_A], F32), ("v_tok", [P, QB, D_A], F32)],
            [("xi", [P, KC, TOK], F32)])
        (hid_hi, hid_lo, gs0, gs1, us0, us1,
         p_raw, p_hi, p_lo, sig,
         q, k, v, conv, sc, pt, ckb, logf, ch, cq, nmx, den, rden, cx_tail,
         ch_hi, ch_lo, qbd, kqbd, sT, dlf, dch, ds, dsn, pT, onew, dnmx, dden, dtmp,
         lru_a, lru_v, gt, xc_hi, xc_lo) = overlay(
            [("hid_hi", [P, HID[0], TOK], F32R), ("hid_lo", [P, HID[0], TOK], F32R),
             ("gs0", [P, TOK], F32), ("gs1", [P, TOK], F32), ("us0", [P, TOK], F32), ("us1", [P, TOK], F32)],
            [("p_raw", [P, PLE_K, TOK], F32), ("p_hi", [P, PLE_K, TOK], F32R), ("p_lo", [P, PLE_K, TOK], F32R),
             ("sig", [P, KC, TOK], F32)],
            [("q", [P, AC, TOK], F32), ("k", [P, AC, TOK], F32), ("v", [P, AC, TOK], F32),
             ("conv", [P, AC, TOK], F32), ("sc", [P, QB, SEQ], F32), ("pt", [P, QB, SEQ], F32),
             ("ckb", [P, SEQ], F32), ("logf", [HEADS, TOK], F32), ("ch", [HEADS, SEQ], F32),
             ("cq", [P, QB, HEADS], F32), ("nmx", [P, QB], F32), ("den", [P, QB], F32), ("rden", [P, QB], F32),
             ("cx_tail", [P, AC, CB - 1 + DEC], F32),
             ("ch_hi", [HEADS, SEQ], F32R), ("ch_lo", [HEADS, SEQ], F32R),
             ("qbd", [P, DEC, AC, 2], F32), ("kqbd", [P, DEC, AC, 2], F32), ("sT", [P, PAGES * BH], F32),
             ("dlf", [BH, PAST + 1], F32), ("dch", [BH, PAST + 1], F32), ("ds", [BH, PAST + 1], F32),
             ("dsn", [BH, DEC], F32), ("pT", [P, PAGES * BH], F32), ("onew", [P, AC, DEC], F32),
             ("dnmx", [BH, 1], F32), ("dden", [BH, 1], F32), ("dtmp", [BH, DEC], F32)],
            [("lru_a", [P, KC, TOK], F32), ("lru_v", [P, KC, TOK], F32), ("gt", [P, KC, TOK], F32),
             ("xc_hi", [P, 4, TOK], F32R), ("xc_lo", [P, 4, TOK], F32R)])
        gs, us = [gs0, gs1], [us0, us1]
        ident_r = sb("ident_r", [HEADS, HEADS], F32R)
        table = sb("table", [1, DEC * PAGES], I32)
        ident = const[:, IDENT:IDENT + P]
        mask = const[:, MASK:MASK + P]
        same_b = const[0:BH, SAME_B:SAME_B + DEC]
        to_bh = const[0:HEADS, TO_BH:TO_BH + BH]
        to_rows = const[0:BH, TO_ROWS:TO_ROWS + AC * P]
        acc = [ctx.enter_context(nc.psum_tensor(f"acc{i}", [P, 2, 512], F32)) for i in range(ACCS)]

        def par(name, i=0, n=1, parts=P):
            at = PARAMS[name][0] + i
            return params[0:parts, at:at + n]

        def gain(s, which, c, scaled=False):
            src = half_norm if scaled else params
            at = ((s // 4) * NN + which) * KC + c
            return src[:, at:at + 1]

        def pre_gain(s, c):
            return gain(s, (0, 2, 4, 6)[s % 4], c)

        def post_gain(s, c):
            return gain(s, (None, 1, 3, 5)[s % 4], c, scaled=IS_FFN(s - 1))

        def mixed_of(c, early, late):
            return early[:, c, :] if c < 4 else late[:, c, :]

        def gate_buffers(c):
            return (ysq[1], xsq[0], xsq[1]) if c % 2 == 0 else (t[0], t[1], rs_post)

        def cols(ap, half):
            return ap[:, half * HALF:(half + 1) * HALF]

        def two(ap):
            return ap.rearrange("p (a n) -> p a n", a=2)

        def acc_of(name):
            return acc[J[name] % ACCS]

        def tile_of(j):
            return acc[j % ACCS][:, :, 0:HALF]

        in_x = [sem(f"in_x{c}") for c in range(KC)]
        in_params, in_const, in_table = sem("in_params"), sem("in_const"), sem("in_table")
        raw_loaded = [sem(f"raw_loaded{i}") for i in range(2)]
        quarter_loaded = [[sem(f"quarter_loaded{n}_{i}") for i in range(3)] + [raw_loaded[n]] for n in range(2)]
        quarter_hi, quarter_lo = sem("quarter_hi"), sem("quarter_lo")
        p_loaded = sem("p_loaded")
        ring_loaded = sem("ring_loaded")
        lf_loaded = sem("lf_loaded")
        hi_ready, lo_ready = sem("hi_ready"), sem("lo_ready")
        acc_ready = sem("acc_ready")
        drained = [sem(f"drained{i}") for i in range(ACCS)]
        consts_made = sem("consts_made")
        half_made, nl_act, nl_made = sem("half_made"), sem("nl_act"), sem("nl_made")
        table_set = sem("table_set")
        y7_half, post_half, root_half, rs_half = sem("y7_half"), sem("post_half"), sem("root_half"), sem("rs_half")
        ysq7_ready, across_lo = sem("ysq7_ready"), sem("across_lo")
        rs_ready = sem("rs_ready")
        ysq_ready, ysum_added = sem("ysq_ready"), sem("ysum_added")
        xsq_ready, xsum_added = sem("xsq_ready"), sem("xsum_added")
        t_ready, x_ready, ple_x = sem("t_ready"), sem("x_ready"), sem("ple_x")
        acth_ready, actl_ready = sem("acth_ready"), sem("actl_ready")
        silu_ready, h_ready = sem("silu_ready"), sem("h_ready")
        hidh_ready, hidl_ready = sem("hidh_ready"), sem("hidl_ready")
        ph_ready, pl_ready, sig_ready, pe_t = sem("ph_ready"), sem("pl_ready"), sem("sig_ready"), sem("pe_t")
        y_stored = sem("y_stored")
        stored = sem("stored")
        f_z, f_exp, f_log, f_ch = sem("f_z"), sem("f_exp"), sem("f_log"), sem("f_ch")
        ch_hi_ready, ch_lo_ready, ident_ready = sem("ch_hi_ready"), sem("ch_lo_ready"), sem("ident_ready")
        scores_ready, exp_ready, probs_ready = sem("scores_ready"), sem("exp_ready"), sem("probs_ready")
        cx_made, cx_ready, bcx_ready = sem("cx_made"), sem("cx_ready"), sem("bcx_ready")
        mixh_ready, mixl_ready = sem("mixh_ready"), sem("mixl_ready")
        qbd_zero, qbd_ready, kqbd_ready = sem("qbd_zero"), sem("qbd_ready"), sem("kqbd_ready")
        dscores_ready, dexp_ready, dprobs_ready = sem("dscores_ready"), sem("dexp_ready"), sem("dprobs_ready")
        xc_ready, xch_ready, xcl_ready = sem("xc_ready"), sem("xch_ready"), sem("xcl_ready")
        tail_ready = sem("tail_ready")
        tr_done, a_done, a2_ready, ti_ready = sem("tr_done"), sem("a_done"), sem("a2_ready"), sem("ti_ready")
        v_ready, xi_ready, root_ready, gelu_ready = sem("v_ready"), sem("xi_ready"), sem("root_ready"), sem("gelu_ready")
        u_ready = sem("u_ready")
        hs_ready, hg_ready = sem("hs_ready"), sem("hg_ready")
        dve_order, act_order = sem("dve_order"), sem("act_order")

        block = ctx.enter_context(nc.Block())

        def across(s):
            return REFILL[f"{s - 1}.out" + ("b" if IS_FFN(s - 1) else "") + str(KC - 1)]

        ACROSS = [across(s) for s in POSTS]

        def wait_job(eng, name_or_j):
            j = J[name_or_j] if isinstance(name_or_j, str) else name_or_j
            eng.wait_ge(acc_ready, j + 1)

        def wait_drained(eng, name):
            eng.wait_ge(drained[J[name] % ACCS], J[name] // ACCS + 1)

        def drains(ins, name):
            ins.then_inc(drained[J[name] % ACCS], 1)

        stat_order = [f"{s}.{w}" for s in range(SUBS) for w in ("post", "pre") if f"{s}.{w}" in J]

        def rs_count(name):
            return stat_order.index(name) + 1

        def x_count(s, c):
            return KC * POSTS.index(s) + c + 1

        def wait_x(eng, s, c):
            if s == 0:
                eng.wait_ge(in_x[c], 16)
            elif s % 4 == 0:
                eng.wait_ge(ple_x, KC * (s // 4 - 1) + c + 1)
            else:
                eng.wait_ge(x_ready, x_count(s, c))

        @block.sync
        def _(sp):
            sp.dma_start(params[:, :], params_d).then_inc(in_params, 16)
            for i in range(4):
                for n in range(2):
                    at, size = PLAN.units[n][1:3]
                    part = slice(i * size // 4, (i + 1) * size // 4)
                    sp.dma_start(raw[n][:, part], weights[at:at + P * size].rearrange("(p n) -> p n", p=P)[:, part])\
                        .then_inc(quarter_loaded[n][i], 16)
                    c = 2 * i + n
                    sp.dma_start(x[:, c, :], x_d[:, c, :]).then_inc(in_x[c], 16)

            def load(n, slot, size, src):
                sp.wait_ge(lo_ready, n - 1)
                sp.dma_start(raw[slot][:, 0:size], src.rearrange("(p n) -> p n", p=P)).then_inc(raw_loaded[slot], 16)

            n = 2
            while n < n_units:
                _, at, size, _ = PLAN.units[n]
                alike = 1
                while n + alike < n_units and PLAN.units[n + alike][2] == size:
                    alike += 1
                pairs = alike // 2
                if pairs >= 2:
                    with sp.Fori(0, pairs) as i:
                        for e in range(2):
                            load(n + e + 2 * i, (n + e) % 2, size,
                                 weights[bass.ds(at + e * P * size + i * (2 * P * size), P * size)])
                    n += 2 * pairs
                else:
                    load(n, n % 2, size, weights[at:at + P * size])
                    n += 1
            for m in range(KC):
                sp.wait_ge(ple_x, KC * (DEPTH - 1) + m + 1)
                sp.dma_start(y_o[:, m, :], x[:, m, :]).then_inc(y_stored, 16)
            sp.wait_ge(y_stored, 16 * KC)

        @block.gpsimd
        def _(pool):
            pool.memset(mean_of[:, :], 1.0 / D).then_inc(consts_made, 1)
            pool.memset(one[:, :], 1.0).then_inc(consts_made, 1)
            pool.memset(eps[:, :], EPS).then_inc(consts_made, 1)
            pool.dma_start(const[:, :], const_d).then_inc(in_const, 16)
            pool.dma_start(table[:, :], table_d).then_inc(in_table, 16)

            def add_squares(s):
                for c in range(1, KC):
                    pool.wait_ge(xsq_ready, KC * s + c + 1)
                    if c > 1:
                        pool.wait_ge(xsum_added, (KC - 1) * s + c - 1)
                    nc.gpsimd.tensor_tensor(xsum[:, :], xsum[:, :], xsq[c % 2][:, :], ALU.add)\
                        .then_inc(xsum_added, 1)

            def store(out, src):
                pool.dma_start(out, src).then_inc(stored, 16)
                count[0] += 16

            count = [0]
            for s in range(SUBS):
                if s in POSTS:
                    n = across(s)
                    size = PLAN.units[n][2]
                    pool.wait_ge(hi_ready, n + 1)
                    for part in range(2):
                        at = slice(part * size // 2, (part + 1) * size // 2)
                        nc.gpsimd.tensor_tensor(w_lo[n % 2][:, at], raw[n % 2][:, at], w_hi[n % 2][:, at].bitcast(F32),
                                                ALU.subtract).then_inc(lo_ready if part else across_lo, 1)
                if s % 4 == 3:
                    pool.wait_ge(x_ready, x_count(s, 0))
                    pool.dma_start(p_raw[:, :, :], p_d[s // 4]).then_inc(p_loaded, 16)
                add_squares(s)
                if s % 4 == 3:
                    pool.wait_ge(ph_ready, s // 4 + 1)
                    nc.gpsimd.tensor_tensor(p_lo[:, :, :], p_raw[:, :, :], p_hi[:, :, :].bitcast(F32),
                                            ALU.subtract).then_inc(pl_ready, 1)
                    if s + 1 < SUBS:
                        for m in range(KC):
                            wait_drained(pool, f"{s}.pe{m}")
                            nc.gpsimd.tensor_tensor(x[:, m, :], x[:, m, :], sig[:, m, :], ALU.add).then_inc(ple_x, 1)
                if s == S_AB:
                    pool.wait_ge(x_ready, x_count(s, KC - 1))
                    nc.gpsimd.memset(qbd[:, :, :, :], 0.0).then_inc(qbd_zero, 1)
                    pool.wait_ge(in_table, 16)

                    def gather(step):
                        src = kpages_d if step < STEPS else vpages_d
                        if step:
                            wait_job(pool, f"{s}.dec_{'so'[(step - 1) // STEPS]}{(step - 1) % STEPS}")
                        for i in range(RING):
                            n = step % STEPS * RING + i
                            page = pool.value_load(table[0:1, n:n + 1], min_val=0, max_val=kpages_d.shape[0] - 1)
                            pool.dma_start(ring[:, i, :], src[bass.ds(page, 1), :, :]
                                           .rearrange("a p n -> (a p) n")).then_inc(ring_loaded, 16)

                    gather(0)
                    for n in range(DEC * PAGES):
                        page = pool.value_load(table[0:1, n:n + 1], min_val=0, max_val=kpages_d.shape[0] - 1)
                        b, g = divmod(n, PAGES)
                        pool.dma_start(dlf[b * HEADS:(b + 1) * HEADS, g * PAGE:(g + 1) * PAGE],
                                       lfpages_d[bass.ds(page, 1), :, :].rearrange("a h n -> (a h) n"))\
                            .then_inc(lf_loaded, 16)
                    gather(1)
                    gather(2)
                    for h in range(HEADS):
                        if h < AC:
                            wait_drained(pool, f"{s}.c{h}")
                            wait_drained(pool, f"{s}.x{h}")
                            nc.gpsimd.tensor_tensor(t[0][:, :], t[0][:, :], t[1][:, :], ALU.mult).then_inc(cx_made, 1)
                        for m in B_TILES.get(h, []):
                            wait_drained(pool, f"{s}.b{m}")
                            nc.gpsimd.tensor_tensor(conv[:, m, :], conv[:, m, :], t[m % 2][:, :], ALU.mult)\
                                .then_inc(bcx_ready, 1)
                        if h in (0, 1, 4, 5, 6):
                            gather(3 + h if h < 2 else 1 + h)
                    wait_drained(pool, f"{s}.k3")
                    store(k_o, k[:, :, :])
                    wait_drained(pool, f"{s}.v3")
                    store(v_o, v[:, :, :])
                    pool.wait_ge(f_log, 1)
                    store(logf_o, logf[:, :])
                    pool.wait_ge(cx_ready, AC)
                    store(cx_o, cx_tail[:, :, :])
                    state = par("state_b", 0, AC * (CB - 1) * DEC).rearrange("p (c j b) -> p c j b", c=AC, j=CB - 1)
                    store(cbstate_o, state[:, :, CB - 2, :])
                    pool.wait_ge(stored, count[0])
                if s == S_C:
                    for c in range(KC):
                        pool.wait_ge(xch_ready, c + 1)
                        nc.gpsimd.tensor_tensor(xc_lo[:, c % 4, :], xi[:, c, :], xc_hi[:, c % 4, :].bitcast(F32),
                                                ALU.subtract).then_inc(xcl_ready, 1)
                    pool.wait_ge(tail_ready, KC)
                    store(xr_o, xr_tail[:, :, :])
                    state = par("state_c", 0, KC * (CC - 1) * DEC)\
                        .rearrange("p (c j) -> p c j", c=KC)
                    store(ccstate_o, state[:, :, DEC:(CC - 1) * DEC])
                    for c in range(KC):
                        pool.wait_ge(root_ready, c + 1)
                        pool.wait_ge(xi_ready, c + 1)
                        nc.gpsimd.tensor_tensor(lru_v[:, c, :], lru_v[:, c, :], xi[:, c, :], ALU.mult)\
                            .then_inc(u_ready, 1)
                    pool.wait_ge(hs_ready, 2 * KC)
                    store(h_o, xi[:, :, SEQ - 1:TOK])
                    pool.wait_ge(stored, count[0])

        @block.scalar
        def _(act):
            order = [0]

            def chained(ins):
                order[0] += 1
                ins.then_inc(act_order, 1)
                act.wait_ge(act_order, order[0])

            def split_hi(n, slot, size, before=None):
                act.wait_ge(raw_loaded[slot], 16 * (n // 2) + 16 if isinstance(n, int) else n)
                if before is not None:
                    act.wait_ge(acc_ready, before + 1)
                nc.scalar.activation(w_hi[slot][:, 0:size], raw[slot][:, 0:size], ACT.Copy).then_inc(hi_ready, 1)

            def refill(n):
                split_hi(n, n % 2, PLAN.units[n][2], last_job[n - 2] if n >= 2 else None)

            def done(name):
                if name in REFILL and REFILL[name] not in ACROSS:
                    refill(REFILL[name])

            def split_quarter(n, i):
                part = slice(i * UNIT // 4, (i + 1) * UNIT // 4)
                act.wait_ge(quarter_loaded[n][i], 16)
                nc.scalar.activation(w_hi[n][:, part], raw[n][:, part], ACT.Copy)\
                    .then_inc(quarter_hi if i < 3 else hi_ready, 1)

            act.wait_ge(consts_made, 3)
            act.wait_ge(in_params, 16)
            chained(nc.scalar.activation(lru[:, 0:KC], par("lam", 0, KC), ACT.Abs))
            nc.scalar.activation(lru[:, KC:2 * KC], lru[:, 0:KC], ACT.Exp, scale=-1.0).then_inc(nl_act, 1)

            def statistics(name, rs):
                wait_job(act, name)
                drains(nc.scalar.activation(two(rs[:, :]), tile_of(J[name]), ACT.Sqrt, bias=eps[:, 0:1]), name)

            def high(s, c):
                wait_x(act, s, c)
                if c == 0:
                    act.wait_ge(in_params, 16)
                nc.scalar.activation(act_hi[:, c, :], x[:, c, :], ACT.Copy, scale=pre_gain(s, c))\
                    .then_inc(acth_ready, 1)
                if c >= 3:
                    act.wait_ge(xsum_added, (KC - 1) * s + c - 2)
                nc.scalar.activation(xsum[:, :] if c == 0 else xsq[c % 2][:, :], x[:, c, :], ACT.Square)\
                    .then_inc(xsq_ready, 1)

            def begin(s):
                if s % 4:
                    a = acc_of(f"{s}.post")
                    act.wait_ge(post_half, POSTS.index(s) + 1)
                    nc.scalar.activation(cols(rs_post, 0), a[:, 0, 0:HALF], ACT.Sqrt, bias=eps[:, 0:1])\
                        .then_inc(root_half, 1)
                    wait_job(act, f"{s}.post")
                    drains(nc.scalar.activation(cols(rs_post, 1), a[:, 1, 0:HALF], ACT.Sqrt, bias=eps[:, 0:1]),
                           f"{s}.post")
                    refill(across(s))
                for c in range(1 if s and s % 4 == 0 else 0, KC):
                    if s == 0 and c % 2 == 0:
                        split_quarter(0, c // 2)
                    high(s, c)
                    if s == 0 and c % 2 == 0:
                        split_quarter(1, c // 2)
                    if s % 4 == 3 and c == KC // 2:
                        act.wait_ge(p_loaded, 16 * (s // 4 + 1))
                        nc.scalar.activation(p_hi[:, :, :], p_raw[:, :, :], ACT.Copy).then_inc(ph_ready, 1)
                statistics(f"{s}.pre", rs_pre)

            def hidden(s, j, jobs, e, unit_hi):
                g, u, tile = jobs
                act.wait_ge(drained[g % ACCS if isinstance(g, int) else g[0]],
                            g // ACCS + 1 if isinstance(g, int) else g[1])
                nc.scalar.activation(gs[e][:, :], gs[e][:, :], ACT.Silu).then_inc(silu_ready, 1)
                unit_hi()
                act.wait_ge(h_ready, tile + 1)
                nc.scalar.activation(hid_hi[:, j, :] if isinstance(j, int) else
                                     hid_hi[:, j, :].rearrange("p a n -> p (a n)"),
                                     us[e][:, :], ACT.Copy).then_inc(hidh_ready, 1)

            def squares(s, m, e, name):
                if m == KC - 1:
                    if POSTS.index(s + 1):
                        act.wait_ge(table_set, POSTS.index(s + 1))
                    nc.scalar.activation(table_use[:, :], eps[:, :], ACT.Sqrt).then_inc(table_set, 1)
                if m < KC - 1:
                    wait_drained(act, name)
                n = POSTS.index(s + 1)
                if m >= 3:
                    act.wait_ge(ysum_added, (KC - 2) * n + m - 2)
                elif n:
                    wait_job(act, f"{POSTS[n - 1]}.post")
                if m < KC - 1:
                    nc.scalar.activation(ysq[e][:, :] if m else ysum[:, :], y[:, m, :], ACT.Square)\
                        .then_inc(ysq_ready, 1)
                    return
                for half in range(2):
                    if half:
                        wait_drained(act, name)
                    else:
                        act.wait_ge(y7_half, n + 1)
                    nc.scalar.activation(cols(ysq[e], half), cols(y[:, m, :], half), ACT.Square)\
                        .then_inc(ysq7_ready, 1)

            def ffn(s):
                tile0 = FT * (s // 2)
                k0 = 0
                for half in range(2):
                    n_t = HID[half]
                    pairs = n_t // 2

                    def straight(i):
                        for e in range(2):
                            j = k0 + 2 * i + e
                            if j == 0:
                                done(f"{s}.u0")
                            hidden(s, j - k0, (J[f"{s}.g{j}"], J[f"{s}.u{j}"], tile0 + j), e,
                                   lambda: done(f"{s}.u{j}") if j else None)
                    first = 0
                    if half == 0:
                        straight(0)
                        first = 1
                    j0 = k0 + 2 * first
                    base = J[f"{s}.g{j0}"]
                    unit = U[f"{s}.in{j0}"]
                    with act.Fori(0, pairs - 1 - first) as i:
                        for e in range(2):
                            g = base + 2 * e
                            hidden(s, bass.ds(2 * i + (2 * first + e), 1),
                                   ((g % ACCS, i + (g // ACCS + 1)), None, 2 * i + (tile0 + j0 + e)), e,
                                   lambda: hidden_refill(unit + e, base + 2 * e + 1, i))
                    straight(pairs - 1)
                    for m in range(KC):
                        name = f"{s}.out{'ab'[half]}{m}"
                        if half == 1:
                            squares(s, m, m % 2, name)
                        done(name)
                    k0 += n_t

            def hidden_refill(n, last, i):
                slot = n % 2
                act.wait_ge(raw_loaded[slot], 16 * i + 16 * ((n + 2) // 2 + 1))
                act.wait_ge(acc_ready, ACCS * i + (last + 1))
                nc.scalar.activation(w_hi[slot][:, :], raw[slot][:, :], ACT.Copy).then_inc(hi_ready, 1)

            def attention(s):
                for m in range(4):
                    done(f"{s}.q{m}")
                act.wait_ge(f_z, 1)
                chained(nc.scalar.activation(xsq[0][0:HEADS, :], t[0][0:HEADS, :], ACT.Abs))
                nc.scalar.activation(xsq[1][0:HEADS, :], xsq[0][0:HEADS, :], ACT.Exp, scale=-1.0).then_inc(f_exp, 1)
                done(f"{s}.f")
                act.wait_ge(in_const, 16)
                nc.scalar.activation(ident_r[:, :], const[0:HEADS, IDENT:IDENT + HEADS], ACT.Copy)\
                    .then_inc(ident_ready, 1)
                for m in range(AC):
                    done(f"{s}.k{m}")
                for m in range(AC):
                    done(f"{s}.v{m}")
                act.wait_ge(f_ch, 1)
                nc.scalar.activation(ch_hi[:, :], ch[:, :], ACT.Copy).then_inc(ch_hi_ready, 1)
                for kb in (0, 2):
                    name = f"{s}.vt{kb}"
                    wait_job(act, name)
                    drains(nc.scalar.activation(v_tok[:, kb:kb + 2, :], acc_of(name)[:, :, :], ACT.Copy), name)

                def decay_row(h):
                    name = f"{s}.ck{h}"
                    wait_job(act, name)
                    if h:
                        wait_drained(act, f"{s}.s{h - 1}.2")
                    drains(nc.scalar.activation(ckb[:, :], acc_of(name)[:, 0, :], ACT.Copy), name)

                def exponentials(h):
                    for qb in range(QB):
                        w = (qb + 1) * P
                        act.wait_ge(scores_ready, QB * h + qb + 1)
                        nc.scalar.activation(sc[:, qb, 0:w], sc[:, qb, 0:w], ACT.Exp, bias=nmx[:, qb:qb + 1],
                                             accum_out=den[:, qb:qb + 1]).then_inc(exp_ready, 1)

                decay_row(0)
                exponentials(0)
                for h in range(HEADS):
                    if h == 2:
                        act.wait_ge(dscores_ready, 1)
                        nc.scalar.activation(ds[:, :], ds[:, :], ACT.Exp, bias=dnmx[:, 0:1],
                                             accum_out=dden[:, 0:1]).then_inc(dexp_ready, 1)
                    if h == MIX_HEAD:
                        wait_job(act, f"{s}.b{AC - 1}")
                        for c in range(AC):
                            act.wait_ge(bcx_ready, c + 1)
                            nc.scalar.activation(act_hi[:, AC + c, :], conv[:, c, :], ACT.Copy).then_inc(mixh_ready, 1)
                    for kb in (0, 2):
                        name = f"{s}.pt{h}.{kb}"
                        wait_job(act, name)
                        if h:
                            wait_job(act, f"{s}.pv{h - 1}")
                        a = acc_of(name)
                        chained(nc.scalar.activation(pt[:, kb, kb * P:SEQ], a[:, 0, kb * P:SEQ], ACT.Copy))
                        drains(nc.scalar.activation(pt[:, kb + 1, (kb + 1) * P:SEQ], a[:, 1, (kb + 1) * P:SEQ], ACT.Copy),
                               name)
                    if h + 1 < HEADS:
                        decay_row(h + 1)
                        exponentials(h + 1)
                    name = f"{s}.pv{h}"
                    wait_job(act, name)
                    r = HD * (h % 2)
                    drains(nc.scalar.activation(q[r:r + HD, h // 2, 0:SEQ], acc_of(name)[r:r + HD, 0, :], ACT.Copy), name)
                    for n in tiles_at(s, h):
                        done(n)
                for i in range(STEPS):
                    wait_drained(act, f"{s}.dec_o{i}")
                for c in range(AC):
                    wait_drained(act, f"{s}.pv{2 * c}")
                    wait_drained(act, f"{s}.pv{2 * c + 1}")
                    nc.scalar.activation(act_hi[:, c, :], q[:, c, :], ACT.Copy).then_inc(mixh_ready, 1)
                for m in range(KC):
                    squares(s, m, m % 2, f"{s}.out{m}")
                    done(f"{s}.out{m}")

            def recurrent(s):
                def conv_hi(c):
                    if c >= 4:
                        wait_job(act, f"{s}.i{c - 4}")
                    act.wait_ge(xc_ready, c + 1)
                    nc.scalar.activation(xc_hi[:, c % 4, :], xi[:, c, :], ACT.Copy).then_inc(xch_ready, 1)
                    nc.scalar.activation(xr_tail[:, c, :], lru_v[:, c, SEQ - CC + 1:TOK], ACT.Copy)\
                        .then_inc(tail_ready, 1)

                def gates(c):
                    tr = ysq[0]
                    th, a2, ti = gate_buffers(c)
                    name = f"{s}.r{c}"
                    wait_job(act, name)
                    if c:
                        act.wait_ge(tr_done, c)
                    drains(nc.scalar.activation(two(tr[:, :]), tile_of(J[name]), ACT.Tanh, scale=0.5,
                                                bias=lru[:, 2 * KC + c:2 * KC + c + 1]), name)
                    wait_drained(act, name)
                    name = f"{s}.i{c}"
                    wait_job(act, name)
                    if c >= 2:
                        act.wait_ge(xi_ready, c - 1)
                    drains(nc.scalar.activation(two(ti[:, :]), tile_of(J[name]), ACT.Tanh, scale=0.5,
                                                bias=lru[:, 3 * KC + c:3 * KC + c + 1]), name)
                    nc.scalar.activation(lru_a[:, c, :], tr[:, :], ACT.Exp, scale=lru[:, c:c + 1],
                                         bias=lru[:, c:c + 1]).then_inc(a_done, 1)
                    if c >= 2:
                        act.wait_ge(v_ready, c - 1)
                    nc.scalar.activation(th[:, :], tr[:, :], ACT.Tanh, scale=lru[:, KC + c:KC + c + 1],
                                         bias=lru[:, KC + c:KC + c + 1]).then_inc(tr_done, 1)
                    act.wait_ge(a_done, c + 1)
                    nc.scalar.activation(a2[:, :], lru_a[:, c, :], ACT.Square).then_inc(a2_ready, 1)

                act.wait_ge(nl_made, 1)
                for kind, c in c_steps("scalar"):
                    if kind == "conv":
                        conv_hi(c)
                    elif kind == "refill":
                        done(f"{s}.{c}")
                    elif kind == "gates":
                        gates(c)
                        done(f"{s}.i{c}")
                    elif kind == "gt":
                        done(f"{s}.gt{c}")
                for c in range(KC):
                    act.wait_ge(v_ready, c + 1)
                    nc.scalar.activation(lru_v[:, c, :], lru_v[:, c, :], ACT.Sqrt, scale=0.25).then_inc(root_ready, 1)

                def gelu(c):
                    wait_drained(act, f"{s}.gt{c}")
                    nc.scalar.activation(gt[:, c, :], gt[:, c, :], ACT.Gelu_apprx_tanh).then_inc(gelu_ready, 1)

                def mixed_hi(c):
                    act.wait_ge(hg_ready, c + 1)
                    nc.scalar.activation(mixed_of(c, xc_hi, act_hi), t[c % 2][:, :], ACT.Copy).then_inc(mixh_ready, 1)

                for c in range(4):
                    gelu(c)
                for c in range(4, KC):
                    done(f"{s}.gt{c}")
                    mixed_hi(c - 4)
                    gelu(c)
                wait_job(act, f"{s}.gt{KC - 1}")
                for c in range(4, KC):
                    mixed_hi(c)
                for m in range(KC):
                    squares(s, m, m % 2, f"{s}.out{m}")
                    done(f"{s}.out{m}")

            def ple(s):
                for m in range(KC):
                    wait_drained(act, f"{s}.gate{m}")
                    nc.scalar.activation(sig[:, m, :], sig[:, m, :], ACT.Sigmoid).then_inc(sig_ready, 1)
                    done(f"{s}.gate{m}")
                    if m == KC - 1 and s + 1 < SUBS:
                        wait_job(act, f"{s}.gate{m}")
                        high(s + 1, 0)
                    if m % 4 == 3:
                        done(f"{s}.pe{m}")

            for s in range(SUBS):
                begin(s)
                {S_AB: attention, S_C: recurrent}.get(s, ffn if IS_FFN(s) else ple)(s)

        @block.vector
        def _(dve):
            order = [0]

            def chained(ins):
                order[0] += 1
                ins.then_inc(dve_order, 1)
                dve.wait_ge(dve_order, order[0])

            def split_lo(slot, size, n):
                dve.wait_ge(hi_ready, n + 1)
                nc.vector.tensor_tensor(w_lo[slot][:, 0:size], raw[slot][:, 0:size],
                                        w_hi[slot][:, 0:size].bitcast(F32), ALU.subtract).then_inc(lo_ready, 1)

            def refill(n):
                split_lo(n % 2, PLAN.units[n][2], n)

            def done(name):
                if name in REFILL and REFILL[name] not in ACROSS:
                    refill(REFILL[name])

            def log1p(e, parts, tmp, between=lambda: None):
                a, b = tmp
                chained(nc.vector.tensor_scalar(a, e, 2.0, None, ALU.add))
                chained(nc.vector.reciprocal(a, a))
                chained(nc.vector.tensor_tensor(e, e, a, ALU.mult))
                chained(nc.vector.tensor_tensor(a, e, e, ALU.mult))
                chained(nc.vector.tensor_scalar(b, a, 1.0 / 15, None, ALU.mult))
                for odd in (13, 11, 9, 7, 5, 3):
                    if odd == 7:
                        between()
                    chained(nc.vector.scalar_tensor_tensor(out=b, in0=b, scalar=1.0 / odd, in1=a,
                                                           op0=ALU.add, op1=ALU.mult))
                chained(nc.vector.scalar_tensor_tensor(out=e, in0=b, scalar=1.0, in1=e, op0=ALU.add, op1=ALU.mult))

            def split_quarter(n, i):
                part = slice(i * UNIT // 4, (i + 1) * UNIT // 4)
                if i < 3:
                    dve.wait_ge(quarter_hi, 2 * i + n + 1)
                else:
                    dve.wait_ge(hi_ready, n + 1)
                nc.vector.tensor_tensor(w_lo[n][:, part], raw[n][:, part], w_hi[n][:, part].bitcast(F32),
                                        ALU.subtract).then_inc(quarter_lo if i < 3 else lo_ready, 1)

            dve.wait_ge(in_params, 16)
            nc.vector.tensor_scalar(half_norm[:, :], par("norm", 0, DEPTH * NN * KC), 0.5, None, ALU.mult)\
                .then_inc(half_made, 1)
            dve.wait_ge(nl_act, 1)
            e = lru[:, KC:2 * KC]
            log1p(e, P, (lru[:, 2 * KC:3 * KC], lru[:, 3 * KC:4 * KC]))
            chained(nc.vector.tensor_scalar(lru[:, 0:KC], par("lam", 0, KC), -1.0, 0.0, ALU.mult, ALU.max))
            chained(nc.vector.scalar_tensor_tensor(out=lru[:, 0:KC], in0=e, scalar=2.0, in1=lru[:, 0:KC],
                                                   op0=ALU.mult, op1=ALU.add))
            chained(nc.vector.tensor_scalar(lru[:, KC:2 * KC], lru[:, 0:KC], LRU_C / 2, None, ALU.mult))
            chained(nc.vector.tensor_scalar(lru[:, 0:KC], lru[:, 0:KC], -LRU_C / 2, None, ALU.mult))
            chained(nc.vector.tensor_scalar(lru[:, 2 * KC:3 * KC], par("b_rg", 0, KC), 0.5, None, ALU.mult))
            nc.vector.tensor_scalar(lru[:, 3 * KC:4 * KC], par("b_ig", 0, KC), 0.5, None, ALU.mult)\
                .then_inc(nl_made, 1)

            def low(s, c):
                dve.wait_ge(acth_ready, KC * s + c + 1)
                nc.vector.scalar_tensor_tensor(out=act_lo[:, c, :], in0=x[:, c, :], scalar=pre_gain(s, c),
                                               in1=act_hi[:, c, :].bitcast(F32), op0=ALU.mult,
                                               op1=ALU.subtract).then_inc(actl_ready, 1)

            def begin(s):
                if s % 4:
                    name = f"{s}.post"
                    dve.wait_ge(root_half, POSTS.index(s) + 1)
                    nc.vector.reciprocal(cols(rs_post, 0), cols(rs_post, 0)).then_inc(rs_half, 1)
                    wait_drained(dve, name)
                    nc.vector.reciprocal(cols(rs_post, 1), cols(rs_post, 1)).then_inc(rs_ready, 1)
                    dve.wait_ge(rs_half, POSTS.index(s) + 1)
                    dve.wait_ge(half_made, 1)

                for c in range(1 if s and s % 4 == 0 else 0, KC):
                    if s == 0 and c % 2 == 0:
                        split_quarter(0, c // 2)
                    if s % 4:
                        dve.wait_ge(rs_ready, rs_count(f"{s}.post"))
                        nc.vector.scalar_tensor_tensor(out=t[c % 2][:, :], in0=y[:, c, :], scalar=post_gain(s, c),
                                                       in1=rs_post[:, :], op0=ALU.mult, op1=ALU.mult)\
                            .then_inc(t_ready, 1)
                        dve.wait_ge(t_ready, x_count(s, c))
                        nc.vector.tensor_tensor(x[:, c, :], x[:, c, :], t[c % 2][:, :], ALU.add).then_inc(x_ready, 1)
                        if c:
                            low(s, c - 1)
                    else:
                        low(s, c)
                    if s == 0 and c % 2 == 0:
                        split_quarter(1, c // 2)
                if s % 4:
                    low(s, KC - 1)
                wait_drained(dve, f"{s}.pre")
                nc.vector.reciprocal(rs_pre[:, :], rs_pre[:, :]).then_inc(rs_ready, 1)
                dve.wait_ge(rs_ready, rs_count(f"{s}.pre"))

            def scaled(out, name):
                wait_job(dve, name)
                drains(nc.vector.tensor_tensor(two(out), tile_of(J[name]), two(rs_pre[:, :]), ALU.mult), name)

            def hidden(j, e, gate, up, tile, unit_lo):
                for out, (a, wait, _) in ((gs[e], gate), (us[e], up)):
                    dve.wait_ge(acc_ready, wait)
                    nc.vector.tensor_tensor(two(out[:, :]), acc[a][:, :, 0:HALF], two(rs_pre[:, :]), ALU.mult)\
                        .then_inc(drained[a], 1)
                unit_lo()
                dve.wait_ge(silu_ready, tile + 1)
                dve.wait_ge(drained[up[0]], up[2])
                nc.vector.tensor_tensor(us[e][:, :], us[e][:, :], gs[e][:, :], ALU.mult).then_inc(h_ready, 1)
                dve.wait_ge(h_ready, tile + 1)
                dve.wait_ge(hidh_ready, tile + 1)
                pick = (lambda z: z[:, j, :]) if isinstance(j, int) else \
                    (lambda z: z[:, j, :].rearrange("p a n -> p (a n)"))
                nc.vector.tensor_tensor(pick(hid_lo), us[e][:, :], pick(hid_hi).bitcast(F32), ALU.subtract)\
                    .then_inc(hidl_ready, 1)

            def last_output(s, name, add):
                m = KC - 1
                for half in range(2):
                    src, out = acc_of(name)[:, half, 0:HALF], cols(y[:, m, :], half)
                    ins = nc.vector.tensor_tensor(out, src, out, ALU.add) if add else nc.vector.tensor_copy(out, src)
                    if half:
                        drains(ins, name)
                    else:
                        ins.then_inc(y7_half, 1)

            def add_square(s, m):
                if m in (0, KC - 1):
                    return
                n = POSTS.index(s + 1)
                dve.wait_ge(ysq_ready, (KC - 1) * n + m + 1)
                if m > 1:
                    dve.wait_ge(ysum_added, (KC - 2) * n + m - 1)
                nc.vector.tensor_tensor(ysum[:, :], ysum[:, :], ysq[m % 2][:, :], ALU.add).then_inc(ysum_added, 1)

            def ffn(s):
                tile0 = FT * (s // 2)
                k0 = 0
                for half in range(2):
                    pairs = HID[half] // 2

                    def straight(i):
                        for e in range(2):
                            j = k0 + 2 * i + e
                            g, u = J[f"{s}.g{j}"], J[f"{s}.u{j}"]
                            if j == 0:
                                done(f"{s}.u0")
                            hidden(j - k0, e, (g % ACCS, g + 1, g // ACCS + 1), (u % ACCS, u + 1, u // ACCS + 1),
                                   tile0 + j, lambda: done(f"{s}.u{j}") if j else None)
                    first = 0
                    if half == 0:
                        straight(0)
                        first = 1
                    j0 = k0 + 2 * first
                    base = J[f"{s}.g{j0}"]
                    unit = U[f"{s}.in{j0}"]
                    with dve.Fori(0, pairs - 1 - first) as i:
                        for e in range(2):
                            g, u = base + 2 * e, base + 2 * e + 1
                            hidden(bass.ds(2 * i + (2 * first + e), 1), e,
                                   (g % ACCS, ACCS * i + (g + 1), None),
                                   (u % ACCS, ACCS * i + (u + 1), i + (u // ACCS + 1)),
                                   2 * i + (tile0 + j0 + e),
                                   lambda: split_lo((unit + e) % 2, UNIT, 2 * i + (unit + e + 2)))
                    straight(pairs - 1)
                    for m in range(KC):
                        name = f"{s}.out{'ab'[half]}{m}"
                        wait_job(dve, name)
                        if half == 0:
                            drains(nc.vector.tensor_copy(two(y[:, m, :]), tile_of(J[name])), name)
                        elif m < KC - 1:
                            drains(nc.vector.tensor_tensor(two(y[:, m, :]), tile_of(J[name]), two(y[:, m, :]),
                                                           ALU.add), name)
                        else:
                            last_output(s, name, True)
                        if half == 1:
                            add_square(s, m)
                        done(name)
                    k0 += HID[half]

            def mixer_out(s):
                for m in range(KC):
                    name = f"{s}.out{m}"
                    wait_job(dve, name)
                    if m < KC - 1:
                        drains(nc.vector.tensor_copy(two(y[:, m, :]), tile_of(J[name])), name)
                    else:
                        last_output(s, name, False)
                    add_square(s, m)
                    done(name)

            def attention(s):
                for m in range(AC):
                    name = f"{s}.q{m}"
                    wait_job(dve, name)
                    drains(nc.vector.scalar_tensor_tensor(out=two(q[:, m, :]), in0=tile_of(J[name]), scalar=HD ** -0.5,
                                                          in1=two(rs_pre[:, :]), op0=ALU.mult, op1=ALU.mult), name)
                    done(name)
                def key_scores(i):
                    name = f"{s}.dec_s{i}"
                    wait_job(dve, name)
                    pick = lambda z: z.rearrange("p (g n) -> p g n", g=PAGES)[:, :, i * BH // STEPS:(i + 1) * BH // STEPS]
                    ins = nc.vector.tensor_copy(pick(sT[:, :]), pick(acc_of(name)[:, 0, 0:PAGES * BH]))
                    if i == STEPS - 1:
                        chained(ins)
                        ins = nc.vector.tensor_tensor(dtmp[:, :], acc_of(name)[0:BH, 1, 0:DEC], same_b, ALU.mult)
                    drains(ins, name)

                name = f"{s}.f"
                z, mag, e = t[0][0:HEADS, :], xsq[0][0:HEADS, :], xsq[1][0:HEADS, :]
                wait_job(dve, name)
                drains(nc.vector.tensor_tensor(two(z), acc_of(name)[0:HEADS, :, 0:HALF], two(rs_pre[0:HEADS, :]),
                                               ALU.mult), name)
                wait_drained(dve, name)
                nc.vector.tensor_scalar(z, z, par("bf", 0, 1, HEADS), None, ALU.add).then_inc(f_z, 1)
                done(name)
                dve.wait_ge(f_exp, 1)
                dve.wait_ge(f_z, 1)

                def first_keys():
                    for m in (0, 1):
                        scaled(k[:, m, :], f"{s}.k{m}")
                        done(f"{s}.k{m}")
                log1p(e, HEADS, (mag, t[1][0:HEADS, :]), first_keys)
                chained(nc.vector.tensor_scalar(mag, z, 0.0, None, ALU.min))
                nc.vector.scalar_tensor_tensor(out=logf[:, :], in0=e, scalar=-2.0, in1=mag, op0=ALU.mult,
                                               op1=ALU.add).then_inc(f_log, 1)
                dve.wait_ge(f_log, 1)
                chained(nc.vector.memset(t[1][0:HEADS, :], 1.0))
                nc.vector.tensor_tensor_scan(ch[:, :], t[1][0:HEADS, 0:SEQ], logf[:, 0:SEQ], 0.0,
                                             ALU.mult, ALU.add).then_inc(f_ch, 1)
                for m in range(2, AC):
                    scaled(k[:, m, :], f"{s}.k{m}")
                    done(f"{s}.k{m}")
                dve.wait_ge(qbd_zero, 1)
                for m in range(AC):
                    wait_drained(dve, f"{s}.q{m}")
                    wait_drained(dve, f"{s}.k{m}")
                for r in range(2):
                    rows = slice(HD * r, HD * (r + 1))
                    nc.vector.tensor_copy(qbd[rows, :, :, r], q[rows, :, SEQ:TOK].rearrange("p c b -> p b c"))\
                        .then_inc(qbd_ready, 1)
                dve.wait_ge(qbd_ready, 2)
                knew = k[:, :, SEQ:TOK].rearrange("p c b -> p b c")
                for r in range(2):
                    nc.vector.tensor_tensor(kqbd[:, :, :, r], qbd[:, :, :, r], knew, ALU.mult).then_inc(kqbd_ready, 1)
                for m in range(AC):
                    scaled(v[:, m, :], f"{s}.v{m}")
                    done(f"{s}.v{m}")
                    if m % 2:
                        key_scores(m // 2)
                dve.wait_ge(ch_hi_ready, 1)
                nc.vector.tensor_tensor(ch_lo[:, :], ch[:, :], ch_hi[:, :].bitcast(F32), ALU.subtract)\
                    .then_inc(ch_lo_ready, 1)
                name = f"{s}.cq"
                wait_job(dve, name)
                drains(nc.vector.tensor_copy(cq[:, :, :], acc_of(name)[:, 0, 0:QB * HEADS]
                                             .rearrange("p (a h) -> p a h", a=QB)), name)
                wait_drained(dve, name)

                def softmax(h):
                    for qb in range(QB):
                        w = (qb + 1) * P
                        name = f"{s}.s{h}.{qb // 2 * 2}"
                        if qb % 2 == 0:
                            wait_job(dve, name)
                        if qb == 0:
                            wait_drained(dve, f"{s}.ck{h}")
                            if h:
                                wait_job(dve, f"{s}.pt{h - 1}.2")
                        ins = nc.vector.scalar_tensor_tensor(
                            out=sc[:, qb, 0:w], in0=acc_of(name)[:, qb % 2, 0:w], scalar=cq[:, qb, h:h + 1],
                            in1=ckb[:, 0:w], op0=ALU.add, op1=ALU.subtract)
                        if qb % 2:
                            drains(ins, name)
                            wait_drained(dve, name)
                        else:
                            chained(ins)
                        chained(nc.vector.tensor_tensor(sc[:, qb, w - P:w], sc[:, qb, w - P:w], mask, ALU.add))
                        nc.vector.tensor_reduce(nmx[:, qb:qb + 1], sc[:, qb, 0:w], AXX, ALU.max, negate=True)\
                            .then_inc(scores_ready, 1)
                    dve.wait_ge(exp_ready, QB * (h + 1))
                    chained(nc.vector.reciprocal(rden[:, :], den[:, :]))
                    for qb in range(QB):
                        w = (qb + 1) * P
                        nc.vector.tensor_scalar(sc[:, qb, 0:w], sc[:, qb, 0:w], rden[:, qb:qb + 1], None, ALU.mult)\
                            .then_inc(probs_ready, 1)

                def short_conv(m):
                    w = lambda j: par("convb_w", j * AC + m)
                    st = lambda j: par("state_b", (m * (CB - 1) + j) * DEC, DEC)
                    out, u = conv[:, m, :], t[0]
                    dve.wait_ge(cx_made, m + 1)
                    nc.vector.tensor_copy(cx_tail[:, m, :], u[:, SEQ - CB + 1:TOK]).then_inc(cx_ready, 1)
                    chained(nc.vector.tensor_scalar(out, u[:, :], w(CB - 1), None, ALU.mult))
                    for j in range(CB - 1):
                        back = CB - 1 - j
                        chained(nc.vector.scalar_tensor_tensor(out=out[:, SEQ:TOK], in0=st(j), scalar=w(j),
                                                               in1=out[:, SEQ:TOK], op0=ALU.mult, op1=ALU.add))
                        chained(nc.vector.scalar_tensor_tensor(out=out[:, back:SEQ], in0=u[:, 0:SEQ - back],
                                                               scalar=w(j), in1=out[:, back:SEQ],
                                                               op0=ALU.mult, op1=ALU.add))

                def decode(h):
                    if h == 0:
                        key_scores(2)
                    if h == 1:
                        key_scores(3)
                        wait_drained(dve, f"{s}.dec_s3")
                        chained(nc.vector.reduce_sum(dlf[:, PAST:PAST + 1], dtmp[:, :], AXX))
                        dve.wait_ge(lf_loaded, 16 * DEC * PAGES)
                        chained(nc.vector.memset(ds[:, :], 1.0))
                        chained(nc.vector.tensor_tensor_scan(dch[:, :], ds[:, :], dlf[:, :], 0.0, ALU.mult, ALU.add))
                    if h == 2:
                        name = f"{s}.dec_t"
                        wait_job(dve, name)
                        a = acc_of(name)
                        last = dch[:, PAST:PAST + 1]
                        chained(nc.vector.scalar_tensor_tensor(out=ds[:, 0:PAST], in0=a[0:BH, 0, 0:PAST], scalar=last,
                                                               in1=dch[:, 0:PAST], op0=ALU.add, op1=ALU.subtract))
                        drains(nc.vector.scalar_tensor_tensor(out=ds[:, PAST:PAST + 1], in0=a[0:BH, 1, 0:1],
                                                              scalar=last, in1=last, op0=ALU.add, op1=ALU.subtract),
                               name)
                        wait_drained(dve, name)
                        nc.vector.tensor_reduce(dnmx[:, :], ds[:, :], AXX, ALU.max, negate=True)\
                            .then_inc(dscores_ready, 1)
                        dve.wait_ge(dexp_ready, 1)
                        chained(nc.vector.reciprocal(dden[:, :], dden[:, :]))
                        chained(nc.vector.tensor_scalar(ds[:, :], ds[:, :], dden[:, 0:1], None, ALU.mult))
                        nc.vector.tensor_scalar(dsn[:, :], same_b, ds[:, PAST:PAST + 1], None, ALU.mult)\
                            .then_inc(dprobs_ready, 1)
                    if h == 3:
                        name = f"{s}.dec_p"
                        wait_job(dve, name)
                        a = acc_of(name)
                        chained(nc.vector.tensor_copy(pT[:, :], a[:, 0, 0:PAGES * BH]))
                        drains(nc.vector.tensor_tensor(onew[:, :, :], a[:, 1, 0:AC * DEC]
                                                       .rearrange("p (c b) -> p c b", c=AC),
                                                       v[:, :, SEQ:TOK], ALU.mult), name)
                        wait_drained(dve, name)
                    if h >= 4:
                        i = h - 4
                        name = f"{s}.dec_o{i}"
                        wait_job(dve, name)
                        n = DEC // STEPS
                        a = acc_of(name)[:, 0, 0:n * AC * 2].rearrange("p (b c r) -> p c b r", b=n, c=AC)
                        for r in range(2):
                            rows = slice(HD * r, HD * (r + 1))
                            ins = nc.vector.tensor_tensor(q[rows, :, SEQ + n * i:SEQ + n * (i + 1)], a[rows, :, :, r],
                                                          onew[rows, :, n * i:n * (i + 1)], ALU.add)
                            if r == 0:
                                chained(ins)
                        drains(ins, name)

                softmax(0)
                for h in range(HEADS):
                    if h < AC:
                        scaled(t[0][:, :], f"{s}.c{h}")
                        scaled(t[1][:, :], f"{s}.x{h}")
                    for m in B_TILES.get(h, []):
                        if m >= 2:
                            dve.wait_ge(bcx_ready, m - 1)
                        scaled(t[m % 2][:, :], f"{s}.b{m}")
                    decode(h)
                    if h < AC:
                        short_conv(h)
                    if h == MIX_HEAD:
                        for c in range(AC):
                            dve.wait_ge(mixh_ready, c + 1)
                            nc.vector.tensor_tensor(act_lo[:, AC + c, :], conv[:, c, :],
                                                    act_hi[:, AC + c, :].bitcast(F32), ALU.subtract)\
                                .then_inc(mixl_ready, 1)
                    if h + 1 < HEADS:
                        softmax(h + 1)
                    for n in tiles_at(s, h):
                        done(n)
                for c in range(AC):
                    dve.wait_ge(mixh_ready, AC + c + 1)
                    nc.vector.tensor_tensor(act_lo[:, c, :], q[:, c, :], act_hi[:, c, :].bitcast(F32), ALU.subtract)\
                        .then_inc(mixl_ready, 1)
                mixer_out(s)

            def recurrent(s):
                def conv_gates(c):
                    w = lambda j: par("convc_w", j * KC + c)
                    st = lambda j: par("state_c", (c * (CC - 1) + j) * DEC, DEC)
                    u, out = lru_v[:, c, :], xi[:, c, :]
                    wait_drained(dve, f"{s}.xr{c}")
                    chained(nc.vector.tensor_scalar(out, u, w(CC - 1), par("convc_b", c), ALU.mult, ALU.add))
                    for j in range(CC - 1):
                        back = CC - 1 - j
                        chained(nc.vector.scalar_tensor_tensor(out=out[:, SEQ:TOK], in0=st(j), scalar=w(j),
                                                               in1=out[:, SEQ:TOK], op0=ALU.mult, op1=ALU.add))
                        ins = nc.vector.scalar_tensor_tensor(out=out[:, back:SEQ], in0=u[:, 0:SEQ - back],
                                                             scalar=w(j), in1=out[:, back:SEQ],
                                                             op0=ALU.mult, op1=ALU.add)
                        if j < CC - 2:
                            chained(ins)
                    ins.then_inc(xc_ready, 1)

                def gates(c):
                    th, a2, ti = gate_buffers(c)
                    dve.wait_ge(a2_ready, c + 1)
                    dve.wait_ge(tr_done, c + 1)
                    nc.vector.scalar_tensor_tensor(out=lru_v[:, c, :], in0=a2[:, :], scalar=1.0, in1=th[:, :],
                                                   op0=ALU.add, op1=ALU.mult).then_inc(v_ready, 1)
                    wait_drained(dve, f"{s}.i{c}")
                    nc.vector.scalar_tensor_tensor(out=xi[:, c, :], in0=ti[:, :], scalar=1.0, in1=xi[:, c, :],
                                                   op0=ALU.add, op1=ALU.mult).then_inc(xi_ready, 1)

                for kind, c in c_steps("vector"):
                    if kind == "drain":
                        scaled(lru_v[:, c, :], f"{s}.xr{c}")
                    elif kind == "conv":
                        conv_gates(c)
                    elif kind == "refill":
                        done(f"{s}.{c}")
                    elif kind == "gates":
                        gates(c)
                        done(f"{s}.i{c}")
                    else:
                        scaled(gt[:, c, :], f"{s}.gt{c}")
                        done(f"{s}.gt{c}")

                def mixed_lo(c):
                    dve.wait_ge(hg_ready, c + 1)
                    dve.wait_ge(mixh_ready, KC + c + 1)
                    nc.vector.tensor_tensor(mixed_of(c, xc_lo, act_lo), t[c % 2][:, :],
                                            mixed_of(c, xc_hi, act_hi).bitcast(F32), ALU.subtract)\
                        .then_inc(mixl_ready, 1)

                h0 = par("h0", 0, KC * DEC).rearrange("p (c b) -> p c b", c=KC)
                dve.wait_ge(a_done, KC)
                chained(nc.vector.tensor_tensor(lru_a[:, :, SEQ:TOK], lru_a[:, :, SEQ:TOK], h0, ALU.mult))
                for c in range(KC):
                    dve.wait_ge(u_ready, c + 1)
                    nc.vector.tensor_tensor(xi[:, c, SEQ:TOK], lru_a[:, c, SEQ:TOK], lru_v[:, c, SEQ:TOK], ALU.add)\
                        .then_inc(hs_ready, 1)
                    nc.vector.tensor_tensor_scan(xi[:, c, 0:SEQ], lru_a[:, c, 0:SEQ], lru_v[:, c, 0:SEQ], 0.0,
                                                 ALU.mult, ALU.add).then_inc(hs_ready, 1)
                    dve.wait_ge(hs_ready, 2 * c + 2)
                    dve.wait_ge(gelu_ready, c + 1)
                    if c >= 2:
                        dve.wait_ge(mixl_ready, KC + c - 1)
                        dve.wait_ge(mixh_ready, KC + c - 1)
                    nc.vector.tensor_tensor(t[c % 2][:, :], gt[:, c, :], xi[:, c, :], ALU.mult).then_inc(hg_ready, 1)
                    if c:
                        mixed_lo(c - 1)
                    if c < 4:
                        scaled(gt[:, c + 4, :], f"{s}.gt{c + 4}")
                        done(f"{s}.gt{c + 4}")
                mixed_lo(KC - 1)
                dve.wait_ge(stored, 16 * 8)
                mixer_out(s)

            def ple(s):
                def embedding(m):
                    name = f"{s}.pe{m}"
                    wait_job(dve, name)
                    dve.wait_ge(sig_ready, KC * (s // 4) + m + 1)
                    drains(nc.vector.tensor_tensor(two(sig[:, m, :]), tile_of(J[name]), two(sig[:, m, :]), ALU.mult),
                           name)
                    if s + 1 == SUBS:
                        wait_drained(dve, name)
                        nc.vector.tensor_tensor(x[:, m, :], x[:, m, :], sig[:, m, :], ALU.add).then_inc(ple_x, 1)
                for m in range(KC):
                    scaled(sig[:, m, :], f"{s}.gate{m}")
                    if m < KC - 1:
                        done(f"{s}.gate{m}")
                    if m % 4 == 3:
                        for c in range(m - 3, m + 1):
                            embedding(c)
                            if c == KC - 3:
                                done(f"{s}.gate{m}")
                        if m == KC - 1 and s + 1 < SUBS:
                            low(s + 1, 0)
                        done(f"{s}.pe{m}")

            for s in range(SUBS):
                begin(s)
                {S_AB: attention, S_C: recurrent}.get(s, ffn if IS_FFN(s) else ple)(s)

        @block.tensor
        def _(pe):
            def claim(j, turn=None):
                if turn is not None:
                    pe.wait_ge(drained[j % ACCS], turn)
                elif j >= ACCS:
                    pe.wait_ge(drained[j % ACCS], j // ACCS)
                return acc[j % ACCS]

            def chunk(a, slot, at, hi, lo, first, last, width=P):
                for n, (w, m) in enumerate(((w_hi, hi), (w_hi, lo), (w_lo, hi))):
                    for half in range(2):
                        ins = nc.tensor.matmul(a[0:width, half, 0:HALF], w[slot][:, at:at + width],
                                               m[:, half * HALF:(half + 1) * HALF],
                                               start=first and n == 0, stop=last and n == 2)
                return ins

            def parts(hi, lo):
                return lambda c: (hi[:, c, :], lo[:, c, :])

            act_in = parts(act_hi, act_lo)

            def tile(j, slot, ks, at, inp, turn=None, wait=None, width=P):
                a = claim(j, turn)
                for c in range(ks):
                    if wait is not None:
                        wait(c)
                    ins = chunk(a, slot, at(c), *inp(c), c == 0, c == ks - 1, width)
                ins.then_inc(acc_ready, 1)

            def wait_unit(n):
                pe.wait_ge(lo_ready, n + 1)

            def pair(s, names, unit, ks=KC, tiles=2, inp=None):
                n = U[f"{s}.{unit}"]
                wait_unit(n)
                for i, name in enumerate(names):
                    tile(J[f"{s}.{name}"], n % 2, ks, lambda c: (c * tiles + i) * P, inp or act_in)

            def k_outer(jobs, units, inp, wait_hi, wait_lo, chunks=range(KC), before_last=lambda: None):
                accs = [claim(j) for j in jobs]

                def product(n, c, w, part, start, stop):
                    unit = units[n // 2]
                    at = (2 * c + n % 2) * P
                    for half in range(2):
                        ins = nc.tensor.matmul(accs[n][:, half, 0:HALF], w[unit % 2][:, at:at + P],
                                               part[:, half * HALF:(half + 1) * HALF], start=start, stop=stop)
                    return ins

                def wait_split(c, n, quarter, ready):
                    unit = units[n // 2]
                    if n % 2 == 0:
                        if unit < 2 and c % 2 == 0 and c < 6:
                            pe.wait_ge(quarter, c + n // 2 + 1)
                        elif unit in ACROSS and ready is lo_ready:
                            if c == 0:
                                pe.wait_ge(across_lo, ACROSS.index(unit) + 1)
                            elif c == 4:
                                pe.wait_ge(lo_ready, unit + 1)
                        elif c == (6 if unit < 2 else chunks[0]):
                            pe.wait_ge(ready, unit + 1)

                tiles = range(len(jobs))
                for c in chunks:
                    if c == chunks[-1]:
                        before_last()
                    hi, lo = inp(c)
                    wait_hi(c)
                    for n in tiles:
                        wait_split(c, n, quarter_hi, hi_ready)
                        product(n, c, w_hi, hi, c == chunks[0], False)
                    for n in tiles:
                        wait_split(c, n, quarter_lo, lo_ready)
                        product(n, c, w_lo, hi, False, False)
                    wait_lo(c)
                    for n in tiles:
                        ins = product(n, c, w_hi, lo, False, c == chunks[-1])
                        if c == chunks[-1]:
                            ins.then_inc(acc_ready, 1)

            def begin(s, tiles, units):
                if s % 4:
                    n = POSTS.index(s)
                    a = claim(J[f"{s}.post"])
                    pe.wait_ge(ysum_added, (KC - 2) * (n + 1))
                    for half in range(2):
                        nc.tensor.matmul(a[:, half, 0:HALF], mean_of[:, :], cols(ysum, half), start=True, stop=False)
                    for half in range(2):
                        pe.wait_ge(ysq7_ready, 2 * n + half + 1)
                        nc.tensor.matmul(a[:, half, 0:HALF], mean_of[:, :], cols(ysq[1], half), start=False, stop=True)\
                            .then_inc(acc_ready if half else post_half, 1)
                un = [U[f"{s}.{u}"] for u in units]

                def pre():
                    pe.wait_ge(xsum_added, (KC - 1) * (s + 1))
                    a = claim(J[f"{s}.pre"])
                    for half in range(2):
                        ins = nc.tensor.matmul(a[:, half, 0:HALF], mean_of[:, :], cols(xsum, half),
                                               start=True, stop=True)
                    ins.then_inc(acc_ready, 1)
                k_outer([J[f"{s}.{n}"] for n in tiles[0:3]], un, act_in,
                        lambda c: pe.wait_ge(acth_ready, KC * s + c + 1),
                        lambda c: pe.wait_ge(actl_ready, KC * s + c + 1), before_last=pre)
                tile(J[f"{s}.{tiles[3]}"], un[1] % 2, KC, lambda c: (2 * c + 1) * P, act_in)

            def ffn(s):
                begin(s, ["g0", "u0", "g1", "u1"], ["in0", "in1"])
                tile0 = FT * (s // 2)
                k0 = 0
                for half in range(2):
                    first = 2 if half == 0 else 0
                    j0 = k0 + first
                    base, unit = J[f"{s}.g{j0}"], U[f"{s}.in{j0}"]
                    with pe.Fori(0, (HID[half] - first) // 2) as i:
                        for e in range(2):
                            pe.wait_ge(lo_ready, 2 * i + (unit + e + 1))
                            for n in range(2):
                                j = base + 2 * e + n
                                tile(j, (unit + e) % 2, KC, lambda c: (2 * c + n) * P, act_in,
                                     turn=i + j // ACCS)
                    tag = "ab"[half]
                    base, unit = J[f"{s}.out{tag}0"], U[f"{s}.out{tag}0"]
                    with pe.Fori(0, KC // 4) as i:
                        for e in range(4):
                            pe.wait_ge(lo_ready, 4 * i + (unit + e + 1))
                            wait = (lambda c: pe.wait_ge(hidl_ready, tile0 + k0 + c + 1)) if e == 0 else None
                            tile(base + e, (unit + e) % 2, HID[half], lambda c: c * P, parts(hid_hi, hid_lo),
                                 turn=i + (base + e) // ACCS, wait=wait)
                    k0 += HID[half]

            def mixer_out(s, n0, chunks=range(KC), inp=act_in):
                un = [U[f"{s}.out0"], U[f"{s}.out2"]]
                k_outer([J[f"{s}.out{m}"] for m in range(3)], un, inp,
                        lambda c: pe.wait_ge(mixh_ready, n0 + list(chunks).index(c) + 1),
                        lambda c: pe.wait_ge(mixl_ready, n0 + list(chunks).index(c) + 1), chunks)
                tile(J[f"{s}.out3"], un[1] % 2, KC, lambda c: (2 * c + 1) * P, inp)
                for m in (4, 6):
                    pair(s, [f"out{m}", f"out{m + 1}"], f"out{m}", inp=inp)

            def attention(s):
                begin(s, ["q0", "q1", "q2", "q3"], ["q0", "q2"])
                n = U[f"{s}.f"]
                wait_unit(n)
                tile(J[f"{s}.f"], n % 2, KC, lambda c: c * HEADS, act_in, width=HEADS)
                for m in (0, 2):
                    pair(s, [f"k{m}", f"k{m + 1}"], f"k{m}")

                def key_scores(i):
                    a = claim(J[f"{s}.dec_s{i}"])
                    pe.wait_ge(ring_loaded, 16 * RING * (i + 1))
                    for r in range(RING):
                        b, g = divmod(i * RING + r, PAGES)
                        for c in range(AC):
                            at = g * BH + b * HEADS + 2 * c
                            ins = nc.tensor.matmul(a[:, 0, at:at + 2], ring[:, r, c * P:(c + 1) * P],
                                                   qbd[:, b, c, :], start=True, stop=True)
                    if i == STEPS - 1:
                        ins = nc.tensor.matmul(a[0:BH, 1, 0:DEC], to_bh, logf[:, SEQ:TOK], start=True, stop=True)
                    ins.then_inc(acc_ready, 1)

                for m in (0, 2):
                    pair(s, [f"v{m}", f"v{m + 1}"], f"v{m}")
                    if m == 0:
                        pe.wait_ge(in_const, 16)
                        pe.wait_ge(qbd_ready, 2)
                    key_scores(m // 2)
                for m in range(AC):
                    wait_drained(pe, f"{s}.v{m}")
                    wait_drained(pe, f"{s}.q{m}")
                    wait_drained(pe, f"{s}.k{m}")
                for kb in (0, 2):
                    a = claim(J[f"{s}.vt{kb}"])
                    for n in range(2):
                        for m in range(AC):
                            ins = nc.tensor.transpose(a[:, n, m * P:(m + 1) * P],
                                                      v[:, m, (kb + n) * P:(kb + n + 1) * P], ident)
                    ins.then_inc(acc_ready, 1)
                pe.wait_ge(f_ch, 1)
                a = claim(J[f"{s}.cq"])
                for qb in range(QB):
                    ins = nc.tensor.transpose(a[:, 0, qb * HEADS:(qb + 1) * HEADS], ch[:, qb * P:(qb + 1) * P],
                                              const[0:HEADS, IDENT:IDENT + HEADS])
                ins.then_inc(acc_ready, 1)

                def scores(h):
                    a = claim(J[f"{s}.ck{h}"])
                    row = ident_r[:, h:h + 1].broadcast_to([HEADS, P])
                    nc.tensor.matmul(a[:, 0, :], row, ch_hi[:, :], start=True, stop=False)
                    nc.tensor.matmul(a[:, 0, :], row, ch_lo[:, :], start=False, stop=True).then_inc(acc_ready, 1)
                    rows = slice(HD * (h % 2), HD * (h % 2) + HD)
                    for qb in range(QB):
                        if qb % 2 == 0:
                            a = claim(J[f"{s}.s{h}.{qb}"])
                        ins = nc.tensor.matmul(a[:, qb % 2, 0:(qb + 1) * P], q[rows, h // 2, qb * P:(qb + 1) * P],
                                               k[rows, h // 2, 0:(qb + 1) * P], start=True, stop=True)
                        if qb % 2:
                            ins.then_inc(acc_ready, 1)

                def decode(h):
                    if h < 2:
                        key_scores(2 + h)
                    if h == 2:
                        a = claim(J[f"{s}.dec_t"])
                        for i in range(STEPS):
                            wait_drained(pe, f"{s}.dec_s{i}")
                        for g in range(PAGES):
                            nc.tensor.transpose(a[0:BH, 0, g * PAGE:(g + 1) * PAGE], sT[:, g * BH:(g + 1) * BH], ident)
                        pe.wait_ge(kqbd_ready, 2)
                        nc.tensor.matmul(a[0:BH, 1, 0:1], kqbd[:, :, :, :].rearrange("p b c r -> p (b c r)"), one[:, :],
                                         start=True, stop=True).then_inc(acc_ready, 1)
                    if h == 3:
                        a = claim(J[f"{s}.dec_p"])
                        pe.wait_ge(dprobs_ready, 1)
                        for g in range(PAGES):
                            nc.tensor.transpose(a[:, 0, g * BH:(g + 1) * BH], ds[:, g * PAGE:(g + 1) * PAGE],
                                                const[0:BH, IDENT:IDENT + BH])
                        for c in range(AC):
                            ins = nc.tensor.matmul(a[:, 1, c * DEC:(c + 1) * DEC], to_rows[:, c * P:(c + 1) * P],
                                                   dsn[:, :], start=True, stop=True)
                        ins.then_inc(acc_ready, 1)
                    if h >= 4:
                        i = h - 4
                        a = claim(J[f"{s}.dec_o{i}"])
                        wait_drained(pe, f"{s}.dec_p")
                        pe.wait_ge(ring_loaded, 16 * RING * (STEPS + i + 1))
                        for r in range(0, RING, PAGES):
                            b = (i * RING + r) // PAGES
                            for c in range(AC):
                                at = (r // PAGES * AC + c) * 2
                                for g in range(PAGES):
                                    src = g * BH + b * HEADS + 2 * c
                                    ins = nc.tensor.matmul(a[:, 0, at:at + 2], ring[:, r + g, c * P:(c + 1) * P],
                                                           pT[:, src:src + 2], start=g == 0, stop=g == PAGES - 1)
                        ins.then_inc(acc_ready, 1)

                pe.wait_ge(ident_ready, 1)
                pe.wait_ge(ch_lo_ready, 1)
                scores(0)
                for h in range(HEADS):
                    if h < AC:
                        pair(s, [f"c{h}", f"x{h}"], f"cx{h}")
                    for m in B_TILES.get(h, []):
                        n = U[f"{s}.b{m // 2 * 2}"]
                        wait_unit(n)
                        tile(J[f"{s}.b{m}"], n % 2, KC, lambda c: (2 * c + m % 2) * P, act_in)
                    decode(h)
                    pe.wait_ge(probs_ready, QB * (h + 1))
                    for kb in range(QB):
                        if kb % 2 == 0:
                            a = claim(J[f"{s}.pt{h}.{kb}"])
                        for qb in range(kb, QB):
                            ins = nc.tensor.transpose(a[:, kb % 2, qb * P:(qb + 1) * P],
                                                      sc[:, qb, kb * P:(kb + 1) * P], ident)
                        if kb % 2:
                            ins.then_inc(acc_ready, 1)
                    if h + 1 < HEADS:
                        scores(h + 1)
                    a = claim(J[f"{s}.pv{h}"])
                    wait_drained(pe, f"{s}.pt{h}.0")
                    wait_drained(pe, f"{s}.pt{h}.2")
                    if h == 0:
                        wait_drained(pe, f"{s}.vt0")
                        wait_drained(pe, f"{s}.vt2")
                    r = HD * (h % 2)
                    for kb in range(QB):
                        ins = nc.tensor.matmul(a[r:r + HD, 0, kb * P:SEQ], v_tok[:, kb, h * HD:(h + 1) * HD],
                                               pt[:, kb, kb * P:SEQ], start=kb == 0, stop=kb == QB - 1)
                    ins.then_inc(acc_ready, 1)
                mixer_out(s, 0, [*range(AC, KC), *range(AC)])

            def recurrent(s):
                begin(s, ["xr0", "xr1", "xr2", "xr3"], ["xr0", "xr2"])

                def gates(m):
                    n = U[f"{s}.ri{m}"]
                    wait_unit(n)
                    for c in (m, m + 1):
                        pe.wait_ge(xcl_ready, c + 1)
                        for i, kind in enumerate("ri"):
                            j = J[f"{s}.{kind}{c}"]
                            a = claim(j)
                            chunk(a, n % 2, (2 * (c - m) + i) * P, xc_hi[:, c % 4, :], xc_lo[:, c % 4, :], True, True)\
                                .then_inc(acc_ready, 1)

                pair(s, ["gt0", "gt1"], "gt0")
                gates(0)
                for m in (4, 6):
                    pair(s, [f"xr{m}", f"xr{m + 1}"], f"xr{m}")
                    gates(m - 2)
                pair(s, ["gt2", "gt3"], "gt2")
                gates(6)
                for m in (4, 6):
                    pair(s, [f"gt{m}", f"gt{m + 1}"], f"gt{m}")
                mixer_out(s, KC, inp=lambda c: (mixed_of(c, xc_hi, act_hi), mixed_of(c, xc_lo, act_lo)))

            def ple(s):
                begin(s, ["gate0", "gate1", "gate2", "gate3"], ["gate0", "gate2"])
                for m in (0, 4):
                    if m:
                        pair(s, ["gate4", "gate5"], "gate4")
                        pair(s, ["gate6", "gate7"], "gate6")
                    pe.wait_ge(pl_ready, s // 4 + 1)
                    pair(s, [f"pe{n}" for n in range(m, m + 4)], f"pe{m}", ks=PLE_K, tiles=4, inp=parts(p_hi, p_lo))

            pe.wait_ge(consts_made, 3)
            for s in range(SUBS):
                {S_AB: attention, S_C: recurrent}.get(s, ffn if IS_FFN(s) else ple)(s)


def tiles_at(s, h):
    if h < AC:
        return [f"{s}.c{h}", f"{s}.x{h}"]
    return [f"{s}.b{m}" for m in B_TILES.get(h, [])]


def c_steps(engine):
    vector = engine == "vector"
    steps = [("drain", 0), ("drain", 1), ("drain", 2), ("refill", "xr1"), ("conv", 0), ("drain", 3),
             ("refill", "xr3"), ("conv", 1), ("gt", 0)]
    steps += [("conv", 2), ("gt", 1), ("conv", 3), ("gates", 0), ("gates", 1)] if vector else \
        [("gt", 1), ("gates", 0), ("conv", 2), ("gates", 1), ("conv", 3)]
    for m in (4, 6):
        steps += [("drain", m), ("conv", m), ("drain", m + 1), ("refill", f"xr{m + 1}")] if vector else \
            [("refill", f"xr{m + 1}"), ("conv", m)]
        gates = [("gates", m - 2), ("gates", m - 1)]
        steps += [("conv", m + 1), *gates] if vector else [*gates, ("conv", m + 1)]
    return steps + [("gt", 2), ("gt", 3), ("gates", 6), ("gates", 7)]


def kernel(**inputs):
    import concourse.bacc as bacc
    from concourse.bass_utils import run_bass_kernel_spmd

    a = {name: np.asarray(value) for name, value in inputs.items()}
    f32 = np.float32

    def feature_major(m):
        return m.T.reshape(m.shape[1] // P, P, m.shape[0]).transpose(1, 0, 2)

    def by_chunk(m):
        lead = m.shape[:-1]
        return np.moveaxis(m.reshape(*lead, m.shape[-1] // P, P), -1, 0)

    ri = np.stack([a["c_w_rg"][0], a["c_w_ig"][0]], axis=1)
    a["c_w_ri"] = ri.transpose(2, 0, 1, 3).reshape(1, P, 2 * D)
    stream = np.empty(PLAN.size, f32)
    for _, at, size, (array, layer, k0, ks, ranges) in PLAN.units:
        w = a[array][layer][k0 * P:(k0 + ks) * P]
        w = np.concatenate([w[:, lo:hi] for lo, hi in ranges], axis=1)
        stream[at:at + P * size] = w.reshape(ks, P, -1).transpose(1, 0, 2).reshape(-1)

    blocks = {
        "norm": by_chunk(a["norms"]),
        "bf": np.concatenate([a["ab_b_f"][0], np.zeros(P - HEADS, f32)]),
        "convb_w": by_chunk(a["ab_conv_w"][0]), "convc_w": by_chunk(a["c_conv_w"][0]),
        "convc_b": by_chunk(a["c_conv_b"][0]), "b_rg": by_chunk(a["c_b_rg"][0]),
        "b_ig": by_chunk(a["c_b_ig"][0]), "lam": by_chunk(a["c_lam"][0]),
        "state_b": by_chunk(a["state_conv_b"][:, 0]).transpose(0, 3, 2, 1),
        "state_c": by_chunk(a["state_conv_c"][:, 0]).transpose(0, 3, 2, 1),
        "h0": by_chunk(a["state_h_c"][:, 0]).transpose(0, 2, 1),
    }
    params = np.concatenate([blocks[n].reshape(P, -1) for n in PARAMS], axis=1)

    const = np.zeros((P, N_CONST), f32)
    const[:, IDENT:IDENT + P] = np.eye(P)
    const[:, MASK:MASK + P] = np.triu(np.full((P, P), NEG), 1)
    const[0:BH, SAME_B:SAME_B + DEC] = np.repeat(np.eye(DEC), HEADS, axis=0)
    const[0:HEADS, TO_BH:TO_BH + BH] = np.tile(np.eye(HEADS), (1, DEC))
    const[0:BH, TO_ROWS:TO_ROWS + AC * P] = np.tile(np.repeat(np.eye(HEADS), HD, axis=1), (DEC, 1))

    tokens = np.concatenate([a["x_prompt"][0], a["x_sample"][:, 0]])
    p = np.stack([feature_major(np.concatenate([a["p_prompt"][i, 0], a["p_sample"][i, :, 0]])) for i in range(DEPTH)])
    pages = a["cache_k"].shape[0]
    k_pages = a["cache_k"][:, 0].reshape(pages, PAGE, AC, P).transpose(0, 3, 2, 1).reshape(pages, P, D_A)
    v_pages = a["cache_v"][:, 0].reshape(pages, PAGE, D_A)
    lf_pages = a["cache_logf"][:, 0].transpose(0, 2, 1)
    host = {"weights": stream, "params": params, "const": const, "x": feature_major(tokens), "p": p,
            "k_pages": k_pages, "v_pages": v_pages, "lf_pages": lf_pages,
            "table": a["page_table"].reshape(1, DEC * PAGES)}
    outs = {"y": (P, KC, TOK), "k": (P, AC, TOK), "v": (P, AC, TOK), "logf": (HEADS, TOK),
            "cx": (P, AC, CB - 1 + DEC), "cb_state": (P, AC, DEC),
            "xr": (P, KC, CC - 1 + DEC), "cc_state": (P, KC, (CC - 2) * DEC), "h": (P, KC, 1 + DEC)}

    nc = bacc.Bacc("TRN2", target_bir_lowering=False, num_devices=1)
    arrays, args = {}, []
    for name, value in host.items():
        value = np.ascontiguousarray(value)
        arrays[f"in_{name}"] = value
        args.append(nc.dram_tensor(f"in_{name}", value.shape, mybir.dt.from_np(value.dtype), kind="ExternalInput").ap())
    for name, shape in outs.items():
        args.append(nc.dram_tensor(f"out_{name}", shape, F32, kind="ExternalOutput").ap())
    trunk(nc, *args)
    r = run_bass_kernel_spmd(nc, [arrays], core_ids=[0]).results[0]
    o = {name: np.asarray(r[f"out_{name}"]) for name in outs}

    def tokens_of(m):
        return m.transpose(2, 1, 0).reshape(m.shape[2], -1)

    y, k, v = (tokens_of(o[n]) for n in "ykv")
    logf, cx, xr, h = o["logf"].T, tokens_of(o["cx"]), tokens_of(o["xr"]), tokens_of(o["h"])
    heads = lambda m: m.reshape(m.shape[0], HEADS, HD)
    cb0 = tokens_of(o["cb_state"])
    cc0 = o["cc_state"].reshape(P, KC, CC - 2, DEC).transpose(3, 2, 1, 0).reshape(DEC, CC - 2, D)
    return (
        y[None, :SEQ], y[SEQ:, None],
        heads(k[:SEQ])[None, None], heads(v[:SEQ])[None, None], logf[None, None, :SEQ],
        heads(k[SEQ:])[:, None, None], heads(v[SEQ:])[:, None, None], logf[SEQ:][:, None, None],
        cx[None, None, :CB - 1], np.stack([cb0, cx[CB - 1:]], axis=1)[:, None],
        xr[None, None, :CC - 1], np.concatenate([cc0, xr[CC - 1:][:, None]], axis=1)[:, None],
        h[None, None, 0], h[1:][:, None],
    )
```
